# Optimizing a Trainium2 kernel written in Bass

```python
import jax, jax.numpy as jnp
from jax import lax
import numpy as np

D_MODEL = 1024
BATCH = 1
SEQ = 256
DEPTH = 2

GRID_W = 64
CTX_LEN = 256
D_MIX = D_MODEL
D_LRU = D_MIX // 2
D_CONV = D_MIX - D_LRU
LRU_HEADS = 8
LRU_HEAD_DIM = D_LRU // LRU_HEADS
LRU_CONV_W = 4
LRU_CONV_PAD = (2, 1)
LRU_C = 8.0
CONF_CONV_W = 31
CONF_CONV_PAD = ((CONF_CONV_W - 1) // 2, (CONF_CONV_W - 1) // 2)
D_IN = 2 * D_LRU + 2 * D_CONV
D_FF = 2816
N_EXPERTS = 8
TOP_K = 2
N_DENSE = (DEPTH + 1) // 2
N_MOE = DEPTH // 2
N_MOD = 6
EPS = 1e-6

kernel_name = "hybrid_rglru_conformer_moe_dit"

def rmsnorm(x, g):
    xf = x.astype(jnp.float32)
    y = xf * lax.rsqrt(jnp.mean(xf * xf, axis=-1, keepdims=True) + EPS)
    return (y * g.astype(jnp.float32)).astype(x.dtype)

def layernorm(x, g, b):
    xf = x.astype(jnp.float32)
    mu = jnp.mean(xf, axis=-1, keepdims=True)
    var = jnp.mean(jnp.square(xf - mu), axis=-1, keepdims=True)
    y = (xf - mu) * lax.rsqrt(var + EPS)
    return (y * g.astype(jnp.float32) + b.astype(jnp.float32)).astype(x.dtype)

def modulate(h, shift, scale):
    return h * (1 + scale) + shift

def sincos_2d(rows, cols, dim):
    quarter = dim // 4
    omega = 1.0 / (10000.0 ** (jnp.arange(quarter, dtype=jnp.float32) / quarter))

    def emb1d(n):
        ang = jnp.arange(n, dtype=jnp.float32)[:, None] * omega[None, :]
        return jnp.concatenate([jnp.sin(ang), jnp.cos(ang)], axis=-1)

    er = jnp.broadcast_to(emb1d(rows)[:, None, :], (rows, cols, dim // 2))
    ec = jnp.broadcast_to(emb1d(cols)[None, :, :], (rows, cols, dim // 2))
    return jnp.concatenate([er, ec], axis=-1).reshape(rows * cols, dim)

def dwconv(x, w, b, pad):
    y = lax.conv_general_dilated(
        x, w[:, None, :].astype(x.dtype), window_strides=(1,), padding=[pad],
        dimension_numbers=("NWC", "WIO", "NWC"), feature_group_count=x.shape[-1])
    return y + b.astype(x.dtype)

def block_diag(x, w, b):
    xh = x.reshape(x.shape[:-1] + (LRU_HEADS, LRU_HEAD_DIM))
    return jnp.einsum("blhi,hij->blhj", xh, w).reshape(x.shape) + b

def rglru_coeffs(x, wa, ba, wx, bx, lam):
    r = jax.nn.sigmoid(block_diag(x, wa, ba)).astype(jnp.float32)
    i = jax.nn.sigmoid(block_diag(x, wx, bx)).astype(jnp.float32)
    log_a = -LRU_C * r * jax.nn.softplus(-lam.astype(jnp.float32))
    a = jnp.exp(log_a)
    b = jnp.sqrt(-jnp.expm1(2.0 * log_a)) * (i * x.astype(jnp.float32))
    return a, b

def linear_scan(a, b, h0, reverse):
    if h0 is not None:
        idx = -1 if reverse else 0
        b = b.at[:, idx].add(a[:, idx] * h0)

    def combine(left, right):
        a_l, b_l = left
        a_r, b_r = right
        return a_l * a_r, a_r * b_l + b_r

    _, h = lax.associative_scan(combine, (a, b), axis=1, reverse=reverse)
    return h

def conformer_branch(v, dw_w, dw_b, ln_g, ln_b):
    g = v[..., :D_CONV] * jax.nn.sigmoid(v[..., D_CONV:])
    g = dwconv(g, dw_w, dw_b, CONF_CONV_PAD)
    return jax.nn.silu(layernorm(g, ln_g, ln_b))

def mixer(h_c, h_x, need_ctx, w_in, w_out, conv_w, conv_b, wa, ba, wx, bx, lam,
          dw_w, dw_b, ln_g, ln_b):
    u_x = h_x @ w_in
    u_c = h_c @ w_in if need_ctx else h_c @ w_in[:, :D_LRU]
    r_x, gate_x, v_x = u_x[..., :D_LRU], u_x[..., D_LRU:2 * D_LRU], u_x[..., 2 * D_LRU:]
    r_c = dwconv(u_c[..., :D_LRU], conv_w, conv_b, LRU_CONV_PAD)
    r_x = dwconv(r_x, conv_w, conv_b, LRU_CONV_PAD)
    y_x = None
    y_c = None
    for d, rev in enumerate((False, True)):
        a, b = rglru_coeffs(r_c, wa[d], ba[d], wx[d], bx[d], lam[d])
        hc = linear_scan(a, b, None, rev)
        h_end = hc[:, 0] if rev else hc[:, -1]
        a, b = rglru_coeffs(r_x, wa[d], ba[d], wx[d], bx[d], lam[d])
        hx = linear_scan(a, b, h_end, rev)
        y_x = hx if y_x is None else y_x + hx
        if need_ctx:
            y_c = hc if y_c is None else y_c + hc

    def merge(y, gate, v):
        lru = y.astype(gate.dtype) * jax.nn.gelu(gate)
        conf = conformer_branch(v, dw_w, dw_b, ln_g, ln_b)
        return jnp.concatenate([lru, conf], axis=-1) @ w_out

    out_x = merge(y_x, gate_x, v_x)
    out_c = merge(y_c, u_c[..., D_LRU:2 * D_LRU], u_c[..., 2 * D_LRU:]) if need_ctx else None
    return out_c, out_x

def swiglu(h, w1, w3, w2):
    return (jax.nn.silu(h @ w1) * (h @ w3)) @ w2

def moe_swiglu(h, w_router, w1, w3, w2):
    logits = (h @ w_router).astype(jnp.float32)
    probs = jax.nn.softmax(logits, axis=-1)
    top_p, top_i = lax.top_k(probs, TOP_K)
    top_p = top_p / jnp.sum(top_p, axis=-1, keepdims=True)
    comb = jnp.sum(jax.nn.one_hot(top_i, N_EXPERTS, dtype=jnp.float32) * top_p[..., None], axis=-2)
    comb = comb.astype(h.dtype)
    y = jnp.zeros_like(h)
    for e in range(N_EXPERTS):
        y = y + comb[..., e:e + 1] * swiglu(h, w1[e], w3[e], w2[e])
    return y

def setup_inputs(seed: int = 0) -> dict:
    key = jax.random.key(seed)
    ks = jax.random.split(key, 32)

    def nrm(k, shape, scale):
        return jax.random.normal(k, shape, jnp.float32) * scale

    x = nrm(ks[0], (BATCH, SEQ, D_MODEL), 1.0)
    c = nrm(ks[1], (BATCH, D_MODEL), 1.0)
    ctx = nrm(ks[2], (BATCH, CTX_LEN, D_MODEL), 1.0)
    c_ctx = nrm(ks[3], (D_MODEL,), 1.0)
    w_mod = nrm(ks[4], (DEPTH, D_MODEL, N_MOD * D_MODEL), 0.5 * D_MODEL ** -0.5)
    b_mod = nrm(ks[5], (DEPTH, N_MOD * D_MODEL), 0.02)
    norm1_g = 1.0 + nrm(ks[6], (DEPTH, D_MODEL), 0.02)
    norm2_g = 1.0 + nrm(ks[7], (DEPTH, D_MODEL), 0.02)
    w_in = nrm(ks[8], (DEPTH, D_MODEL, D_IN), D_MODEL ** -0.5)
    w_out = nrm(ks[9], (DEPTH, D_MIX, D_MODEL), D_MIX ** -0.5)
    lru_conv_w = nrm(ks[10], (DEPTH, LRU_CONV_W, D_LRU), LRU_CONV_W ** -0.5)
    lru_conv_b = nrm(ks[11], (DEPTH, D_LRU), 0.02)
    lru_wa = nrm(ks[12], (DEPTH, 2, LRU_HEADS, LRU_HEAD_DIM, LRU_HEAD_DIM), LRU_HEAD_DIM ** -0.5)
    lru_ba = nrm(ks[13], (DEPTH, 2, D_LRU), 0.02)
    lru_wx = nrm(ks[14], (DEPTH, 2, LRU_HEADS, LRU_HEAD_DIM, LRU_HEAD_DIM), LRU_HEAD_DIM ** -0.5)
    lru_bx = nrm(ks[15], (DEPTH, 2, D_LRU), 0.02)
    a_c = jax.random.uniform(ks[16], (DEPTH, 2, D_LRU), jnp.float32, 0.9, 0.999)
    s = a_c ** (1.0 / LRU_C)
    lru_lambda = jnp.log(s) - jnp.log1p(-s)
    conf_dw_w = nrm(ks[17], (DEPTH, CONF_CONV_W, D_CONV), CONF_CONV_W ** -0.5)
    conf_dw_b = nrm(ks[18], (DEPTH, D_CONV), 0.02)
    conf_ln_g = 1.0 + nrm(ks[19], (DEPTH, D_CONV), 0.02)
    conf_ln_b = nrm(ks[20], (DEPTH, D_CONV), 0.02)
    ffn_w1 = nrm(ks[21], (N_DENSE, D_MODEL, D_FF), D_MODEL ** -0.5)
    ffn_w3 = nrm(ks[22], (N_DENSE, D_MODEL, D_FF), D_MODEL ** -0.5)
    ffn_w2 = nrm(ks[23], (N_DENSE, D_FF, D_MODEL), D_FF ** -0.5)
    moe_router = nrm(ks[24], (N_MOE, D_MODEL, N_EXPERTS), D_MODEL ** -0.5)
    moe_w1 = nrm(ks[25], (N_MOE, N_EXPERTS, D_MODEL, D_FF), D_MODEL ** -0.5)
    moe_w3 = nrm(ks[26], (N_MOE, N_EXPERTS, D_MODEL, D_FF), D_MODEL ** -0.5)
    moe_w2 = nrm(ks[27], (N_MOE, N_EXPERTS, D_FF, D_MODEL), D_FF ** -0.5)
    final_g = 1.0 + nrm(ks[28], (D_MODEL,), 0.02)
    return {"x": x, "c": c, "ctx": ctx, "c_ctx": c_ctx, "w_mod": w_mod, "b_mod": b_mod,
            "norm1_g": norm1_g, "norm2_g": norm2_g, "w_in": w_in, "w_out": w_out,
            "lru_conv_w": lru_conv_w, "lru_conv_b": lru_conv_b, "lru_wa": lru_wa, "lru_ba": lru_ba,
            "lru_wx": lru_wx, "lru_bx": lru_bx, "lru_lambda": lru_lambda,
            "conf_dw_w": conf_dw_w, "conf_dw_b": conf_dw_b, "conf_ln_g": conf_ln_g, "conf_ln_b": conf_ln_b,
            "ffn_w1": ffn_w1, "ffn_w3": ffn_w3, "ffn_w2": ffn_w2, "moe_router": moe_router,
            "moe_w1": moe_w1, "moe_w3": moe_w3, "moe_w2": moe_w2, "final_g": final_g}

def reference(x, c, ctx, c_ctx, w_mod, b_mod, norm1_g, norm2_g, w_in, w_out,
              lru_conv_w, lru_conv_b, lru_wa, lru_ba, lru_wx, lru_bx, lru_lambda,
              conf_dw_w, conf_dw_b, conf_ln_g, conf_ln_b,
              ffn_w1, ffn_w3, ffn_w2, moe_router, moe_w1, moe_w3, moe_w2, final_g):
    rows = x.shape[1] // GRID_W
    x = x + sincos_2d(rows, GRID_W, D_MODEL).astype(x.dtype)
    xc = ctx
    n_ctx = ctx.shape[1]
    for l in range(DEPTH):
        last = l == DEPTH - 1
        m_x = jax.nn.silu(c) @ w_mod[l] + b_mod[l]
        m_c = jax.nn.silu(c_ctx) @ w_mod[l] + b_mod[l]
        sh1x, sc1x, g1x, sh2x, sc2x, g2x = [t[:, None, :] for t in jnp.split(m_x, N_MOD, axis=-1)]
        sh1c, sc1c, g1c, sh2c, sc2c, g2c = jnp.split(m_c, N_MOD, axis=-1)

        h_x = modulate(rmsnorm(x, norm1_g[l]), sh1x, sc1x)
        h_c = modulate(rmsnorm(xc, norm1_g[l]), sh1c, sc1c)
        o_c, o_x = mixer(h_c, h_x, not last, w_in[l], w_out[l], lru_conv_w[l], lru_conv_b[l],
                         lru_wa[l], lru_ba[l], lru_wx[l], lru_bx[l], lru_lambda[l],
                         conf_dw_w[l], conf_dw_b[l], conf_ln_g[l], conf_ln_b[l])
        x = x + g1x * o_x

        f_x = modulate(rmsnorm(x, norm2_g[l]), sh2x, sc2x)
        if last:
            h = f_x
        else:
            xc = xc + g1c * o_c
            f_c = modulate(rmsnorm(xc, norm2_g[l]), sh2c, sc2c)
            h = jnp.concatenate([f_c, f_x], axis=1)
        if l % 2 == 0:
            j = l // 2
            y = swiglu(h, ffn_w1[j], ffn_w3[j], ffn_w2[j])
        else:
            j = l // 2
            y = moe_swiglu(h, moe_router[j], moe_w1[j], moe_w3[j], moe_w2[j])
        if last:
            x = x + g2x * y
        else:
            xc = xc + g2c * y[:, :n_ctx]
            x = x + g2x * y[:, n_ctx:]
    return rmsnorm(x, final_g)


_drawn_inputs = setup_inputs


def setup_inputs(seed=0):
    import zlib

    import numpy as np

    out = dict(_drawn_inputs(seed))
    spreads = {}
    factors = {'norm2_g': 5.011,
     'lru_ba': 8.0,
     'lru_bx': 8.0,
     'conf_dw_b': 7.019,
     'conf_ln_g': 7.996,
     'conf_ln_b': 8.0,
     'final_g': 2.677}
    for name, (base, spread) in spreads.items():
        noise = np.random.default_rng([zlib.crc32(name.encode()), seed]).standard_normal(out[name].shape)
        drawn = base * np.exp(spread * noise) if base else spread * noise
        out[name] = __import__('jax').numpy.asarray(drawn.astype(out[name].dtype))
    for name, factor in factors.items():
        out[name] = (out[name] * factor).astype(out[name].dtype)
    return out
```

```python
import numpy as np
import concourse.bass as bass
from concourse import mybir
from concourse.alu_op_type import AluOpType as ALU

F32 = mybir.dt.float32
F32R = mybir.dt.float32r
I32 = mybir.dt.int32
U32 = mybir.dt.uint32
ACT = mybir.ActivationFunctionType
AX = mybir.AxisListType

P = 128
D = 1024
KD = D // P
S = 256
C = 256
T = S + C
DL = 512
KL = DL // P
NH, DH = 8, 64
TAPS, PAD = 31, 15
RTAPS, RPL, RPR = 4, 2, 1
LRU_C = 8.0
DIN = 4 * DL
DFF = 2816
NE = 8
NMOD = 6
DEPTH = 2
EPS = 1e-6
UC = 256
UW = KD * UC
CAP = 128
FAR = 1000.0
GW = 2 * PAD + C
RW = RPL + RPR + C

K_ID, K_UP, K_ONE, K_IOTA, K_IOTA8, K_COMB, K_W = 0, 128, 256, 384, 512, 520, 522
R_BMOD, R_N1, R_N2, R_CW, R_CB, R_BA, R_BX, R_LAM, R_DWB, R_LNG, R_LNB, R_END = (
    0, 48, 56, 64, 80, 84, 92, 100, 108, 112, 116, 120)
R_C, R_CC, R_FG, R_MEND = 0, 8, 16, 24

WIN_COLS = [1536, 1792, 1024, 1280, 0, 256, 512, 768]
FFN_GROUPS = [4, 4, 3]
NPAIR = DFF // (2 * UC)
BODIES = 2 * NPAIR + 1


def weight_units():
    units = [("ad", 0, q) for q in range(8)]
    for i in range(8):
        units += [("win", 0, i), ("ad", 0, 8 + 2 * i), ("ad", 0, 9 + 2 * i)]
    units += [("wout", 0, i) for i in range(4)]
    ffn, j = [], 0
    for g, n in enumerate(FFN_GROUPS):
        for _ in range(n):
            ffn += [("f1", g, j), ("f3", g, j)]
            j += 1
        ffn += [("f2", g, i) for i in range(4)]
    for n, unit in enumerate(ffn):
        units.append(unit)
        if n < 24:
            units.append(("ad", 1, n))
    units += [("win", 1, i) for i in range(8)]
    units += [("wout", 1, i) for i in range(4)]
    return units


UNITS = weight_units()
RING = 3
RING2 = 6
MM_BANKS = 4


def dit_kernel(nc, x, c, ctx, c_ctx, w_mod, b_mod, norm1_g, norm2_g, w_in, w_out,
               lru_conv_w, lru_conv_b, lru_wa, lru_ba, lru_wx, lru_bx, lru_lambda,
               conf_dw_w, conf_dw_b, conf_ln_g, conf_ln_b,
               ffn_w1, ffn_w3, ffn_w2, moe_router, moe_w1, moe_w3, moe_w2, final_g,
               pos_t, consts, out):
    place = {"at": 16512}

    def sb(name, shape, dt=F32, at=None):
        size = int(np.prod(shape[1:])) * 4
        size = (size + 31) // 32 * 32
        off = place["at"] if at is None else at
        if at is None:
            place["at"] += size
        assert off + size <= 229368, (name, off + size)
        t = nc.alloc_sbuf_tensor_at(name, [P] + list(shape[1:]), dt, offset=off)
        return t, off, off + size

    K, _, _ = sb("shape_consts", [P, K_W])
    eps, _, _ = sb("eps", [P, 1])
    fg, _, _ = sb("final_g_t", [P, KD])
    mt = [sb(f"mod_t{l}", [P, NMOD * KD, 2])[0] for l in range(DEPTH)]
    amp, _, _ = sb("norm_scale", [P, KD, 2])
    rounds, _, _ = sb("rounds", [P, 1], I32)
    rt, _, _ = sb("router", [P, KD, NE])
    spn, _, _ = sb("decay_rate", [P, DEPTH, 2, 8])
    sp_t, _, _ = sb("softplus_tmp", [P, 4, 8])
    zeros, _, _ = sb("zeros", [P, UC], F32R)
    xT, xT_at, _ = sb("x_t", [P, 2, KD, C])
    raw = [sb(f"raw{s}", [P, UW])[0] for s in range(RING)]
    wh = [sb(f"w_hi{s}", [P, UW], F32R)[0] for s in range(RING)]
    wl = [sb(f"w_lo{s}", [P, UW], F32R)[0] for s in range(RING)]
    scratch = place["at"]
    gate_r, nb_at, _ = sb("decay_a", [P, 2, T])
    root, _, _ = sb("root", [P, 2, T])
    h32, _, _ = sb("h32", [P, 2, T])
    sq, _, _ = sb("squares", [P, 2, T], at=nb_at)
    rstd, _, _ = sb("rstd", [P, T], at=nb_at + 4096)
    norm_t, _, _ = sb("norm_tmp", [P, T], at=nb_at + 6144)
    par, _, par_end = sb("params_t", [P, 2 * DEPTH + 1, P])
    mrow, _, _ = sb("mod_rows", [P, 2, UC])
    smat, _, _ = sb("silu_c_cols", [P, KD, P], F32R)
    sv, _, _ = sb("silu_c", [P, 2 * KD])
    experts_at = place["at"]
    hH, hH_at, _ = sb("h_hi", [P, KD, T], F32R)
    hL, _, _ = sb("h_lo", [P, KD, T], F32R)
    bdw, _, _ = sb("block_diag", [P, KL, 2, 2, P])
    mix_at = place["at"]
    glu, _, _ = sb("glu_pad", [P, KL, 2, GW])
    cv, _, _ = sb("conv_out", [P, KL, 2, C])
    rpad, rpad_at, _ = sb("rec_pad", [P, KL, 2, RW])
    rc, _, _ = sb("rec_conv", [P, KL, T])
    gg, _, _ = sb("gelu_gate", [P, KL, T])
    yy, _, _ = sb("scan_sum", [P, KL, T])
    rg, _, _ = sb("rec_gate", [P, 2, T], at=rpad_at)
    ig, _, _ = sb("in_gate", [P, 2, T], at=rpad_at + 4096)
    assert 2 * RW * KL * 4 >= 8192
    gH, _, e_ = sb("g_hi", [P, KD, T], F32R, at=mix_at)
    gL, _, e_ = sb("g_lo", [P, KD, T], F32R, at=e_)
    sg, _, e_ = sb("silu_out", [P, 4, T], at=e_)
    gt, _, e_ = sb("g_prod", [P, 2, T], at=nb_at)
    prow, _, e_ = sb("param_rows", [P, 2 * DEPTH + 1, P], at=mix_at)
    xrow, _, e_ = sb("x_rows", [P, 4, D], at=e_)
    pos, _, e_ = sb("pos_t", [P, KD, S], at=e_)
    esg, _, e_ = sb("e_silu", [P, 2, UC], at=scratch)
    egH, _, e_ = sb("e_g_hi", [P, 2, UC], F32R, at=e_)
    egL, _, e_ = sb("e_g_lo", [P, 2, UC], F32R, at=e_)
    yH, _, e_ = sb("y_hi", [P, 2, 512], F32R, at=e_)
    yL, _, e_ = sb("y_lo", [P, 2, 512], F32R, at=e_)
    pick, _, e_ = sb("pick", [P, 2, 2 * CAP], F32R, at=e_)
    pickT, _, e_ = sb("pick_t", [P, 2, S], F32R, at=e_)
    tab, _, e_ = sb("slot_table", [P, 2, 2, 2 * NE + 2], at=e_)
    cur, _, e_ = sb("slot_now", [P, 2, 2, 2], at=e_)
    cs, _, e_ = sb("slot_weight", [P, 2], at=e_)
    assert e_ >= par_end
    for s in range(RING, RING2):
        t, _, e_ = sb(f"raw{s}", [P, UW], at=e_)
        raw.append(t)
        t, _, e_ = sb(f"w_hi{s}", [P, UW], F32R, at=e_)
        wh.append(t)
        t, _, e_ = sb(f"w_lo{s}", [P, UW], F32R, at=e_)
        wl.append(t)
    ftH, _, _ = sb("f_tok_hi", [P, 2, D], F32R, at=xT_at)
    ftL, _, e_ = sb("f_tok_lo", [P, 2, D], F32R, at=e_)
    xe_at = e_
    xeH, _, e_ = sb("xe_hi", [P, KD, 2 * CAP], F32R, at=e_)
    xeL, _, e_ = sb("xe_lo", [P, KD, 2 * CAP], F32R, at=e_)
    fT, _, e3 = sb("f_t", [P, KD, S], at=xe_at)
    lg, _, e3 = sb("logits", [P, 2, NE], at=e3)
    pr, _, e3 = sb("probs", [P, 2, NE], at=e3)
    top, _, e3 = sb("top8", [P, 2, 8], at=e3)
    tix, _, e3 = sb("top8_index", [P, 2, 8], U32, at=e3)
    tif, _, e3 = sb("top8_index_f", [P, 2, 8], at=e3)
    oh, _, e3 = sb("one_hots", [P, 2, 2, NE], at=e3)
    mask, _, e3 = sb("mask", [P, 2, NE], at=e3)
    col, _, e3 = sb("route_cols", [P, 2, 8], at=e3)
    flag, _, e3 = sb("rounds_f", [P, 2], at=e3)
    assert e3 <= 229368
    orow, _, _ = sb("out_rows", [P, 2, D], at=experts_at)

    bank = [nc.alloc_psum_tensor(f"bank{b}", [P, 512], F32) for b in range(8)]
    B_ROW, B_MT, B_ST = 4, 6, 7

    names = """consts_in params_in x_in bd_in x_out params_t x_tr x_ready params_ready silu_ready cols_ready
        memset_done hi_done lo_done row_out mt_mm mod_ready decay_done decay_exp
        sq_done sum_mm root_done norm_step h32_done hH_done hL_done
        mm_done gates_done glu_done rec_done gelu_done rconv_done conv_step
        bd_mm sig_done act_step dve_step ig_done root_in scan_done lru_done ln_mm ln_step ln_act
        res_done silu_out g_prod gH_done gL_done fT_done
        router_in logits_mm route_step route_exp pos_mm rounds_done tok_tr tokH tokL
        e_hi e_lo e_used e_silu e_prod g_tr e_gH e_gL y_mm y_hi y_lo comb_mm acc_done
        pick_done gather_mm xe_hi xe_lo zero_done fin_tr fin_out pad_zero bd_zero""".split()
    sem = {n: nc.alloc_semaphore(n) for n in names}
    unit_full = [nc.alloc_semaphore(f"unit_full{s}") for s in range(RING)]
    e_full = [nc.alloc_semaphore(f"e_full{s}") for s in range(RING2)]

    def inc(ins, name, n=1):
        return ins.then_inc(sem[name], n)

    def split3(hi_l, lo_l, hi_r, lo_r):
        return ((hi_l, hi_r), (hi_l, lo_r), (lo_l, hi_r))

    def layer_par(l, row, n=1):
        return par[:, 2 * l, row:row + n]

    def tap(l, t, c_):
        return par[:, 2 * l + 1, t * KL + c_:t * KL + c_ + 1]

    def side(l, kind):
        return 0 if l == 0 or kind == "rec" else 1

    def cols(full):
        return slice(0, T) if full == 0 else slice(C, T)

    NU = len(UNITS)

    def win_kind(i):
        return ("gates", "values", "rec", "gelu")[i // 2]

    MM, USED, n = {}, [], 0
    for kind, a, i in UNITS:
        for h in range(1 if kind == "ad" else 2):
            n += 1
            MM[(kind, a, i if kind == "ad" else 2 * i + h)] = n
        USED.append(n)
    AT = {unit: u for u, unit in enumerate(UNITS)}
    RES = {("wout", 0): 0, ("f2", 0): KD, ("f2", 1): 2 * KD, ("f2", 2): 3 * KD, ("wout", 1): 4 * KD,
           (0, 2): KD, (1, 1): 4 * KD, (1, 2): 5 * KD}
    HL = {("norm", 0, 1): KD, ("mix", 0): 2 * KD, ("norm", 0, 2): 3 * KD, ("norm", 1, 1): 4 * KD, ("mix", 1): 5 * KD}
    ROOT = {(0, 1): 1, ("mix", 0): 1, ("ln", 0): 2 + 2 * KL, (0, 2): 3 + 2 * KL, (1, 1): 4 + 2 * KL, ("mix", 1): 4 + 2 * KL,
            ("ln", 1): 5 + 4 * KL, (1, 2): 6 + 4 * KL, "final": 7 + 4 * KL}
    LN_STEPS = 2 * KL + 1
    DECAY_ALL = 3 * DEPTH
    ROUTE_MASKS, ROUTE_ALL = 7 + 13 * 2, 7 + 13 * 2 + 3 * 2 + 2

    def unit_src(kind, a, i):
        if kind == "ad":
            return w_mod[a, :, i * UC:(i + 1) * UC].rearrange("(k p) n -> p k n", p=P)
        if kind == "win":
            return w_in[a, :, WIN_COLS[i]:WIN_COLS[i] + UC].rearrange("(k p) n -> p k n", p=P)
        if kind == "wout":
            return w_out[a, :, i * UC:(i + 1) * UC].rearrange("(k p) n -> p k n", p=P)
        if kind in ("f1", "f3"):
            w = ffn_w1 if kind == "f1" else ffn_w3
            return w[0, :, i * UC:(i + 1) * UC].rearrange("(k p) n -> p k n", p=P)
        r0 = sum(FFN_GROUPS[:a]) * UC
        r1 = r0 + FFN_GROUPS[a] * UC
        return ffn_w2[0, r0:r1, i * UC:(i + 1) * UC].rearrange("(k p) n -> p k n", p=P)

    def unit_k(kind, a):
        return 2 * FFN_GROUPS[a] if kind == "f2" else KD

    PARAM_DMAS = 11 * DEPTH + DEPTH + 3
    ROW_PARTS = [(2 * l, R_END) for l in range(DEPTH)] + [(2 * l + 1, TAPS * KL) for l in range(DEPTH)] + [(4, R_MEND)]

    block = nc.Block()
    with block:
        @block.sync
        def _(sp):
            inc(sp.dma_start(K[:, :], consts), "consts_in", 16)
            inc(sp.dma_start(rt[:, :, :], moe_router[0].rearrange("(k p) e -> p k e", p=P)), "router_in", 16)
            for u, (kind, a, i) in enumerate(UNITS):
                if u >= RING:
                    sp.wait_ge(sem["lo_done"], u - RING + 1)
                nk = unit_k(kind, a)
                sp.dma_start(raw[u % RING][:, 0:nk * UC].rearrange("p (k n) -> p k n", n=UC),
                             unit_src(kind, a, i)).then_inc(unit_full[u % RING], 16)
            sp.wait_ge(sem["rounds_done"], 1)
            n_rounds = sp.value_load(rounds[0:1, 0:1], min_val=1, max_val=2)

            def load(n, s, w, e, f):
                sp.wait_ge(sem["e_lo"], n * 6 + s + 1)
                if w is moe_w2:
                    src = w[0, bass.ds(e, 1), bass.ds(f * UC, UC), :].rearrange("a (k p) n -> p (a k) n", p=P)
                    dst = raw[s][:, :].rearrange("p (k n) -> p k n", k=2)
                else:
                    src = w[0, bass.ds(e, 1), :, bass.ds(f * UC, UC)].rearrange("a (k p) n -> p (a k) n", p=P)
                    dst = raw[s][:, :].rearrange("p (k n) -> p k n", k=KD)
                sp.dma_start(dst, src).then_inc(e_full[s], 16)

            def load_body(n, ea, fa, eb, fb):
                load(n, 0, moe_w1, ea, fa)
                load(n, 1, moe_w3, ea, fa)
                load(n, 2, moe_w1, eb, fb)
                load(n, 3, moe_w3, eb, fb)
                load(n, 4, moe_w2, ea, fa)
                load(n, 5, moe_w2, eb, fb)

            with sp.Fori(0, n_rounds) as r:
                with sp.Fori(0, NE // 2) as i:
                    n0 = (r * (NE // 2) + i) * BODIES
                    with sp.Fori(0, NPAIR) as j:
                        load_body(n0 + j, i * 2, j * 2, i * 2, j * 2 + 1)
                    load_body(n0 + NPAIR, i * 2, 2 * NPAIR, i * 2 + 1, 0)
                    with sp.Fori(0, NPAIR) as j:
                        load_body(n0 + NPAIR + 1 + j, i * 2 + 1, j * 2 + 1, i * 2 + 1, j * 2 + 2)
            for t in range(2):
                sp.wait_ge(sem["fin_out"], 2 * (t + 1))
                inc(sp.dma_start(out[0, t * P:(t + 1) * P, :], orow[:, t, :]), "x_out", 16)
            sp.wait_ge(sem["x_out"], 32)

        @block.gpsimd
        def _(pool):
            inc(nc.gpsimd.memset(zeros[:, :].bitcast(F32), 0.0), "memset_done")
            inc(nc.gpsimd.memset(smat[:, :, :].bitcast(F32), 0.0), "memset_done")
            inc(nc.gpsimd.memset(eps[:, :], EPS), "memset_done")
            inc(nc.gpsimd.memset(bdw[:, :, :, :, :], 0.0), "bd_zero")

            def load_block_diag(l):
                for kind, w in enumerate((lru_wa, lru_wx)):
                    for d in range(2):
                        for odd in range(2):
                            src = w[l, d, odd:NH:2, :, :].rearrange("c i j -> i c j")
                            dst = bdw[DH * odd:DH * (odd + 1), :, d, kind, DH * odd:DH * (odd + 1)]
                            inc(pool.dma_start(dst, src), "bd_in", 16)

            pool.wait_ge(sem["bd_zero"], 1)
            load_block_diag(0)

            counts = {"low": 0}

            def low(dst, hi, k):
                pool.wait_ge(sem["hH_done"], counts["low"] + 1)
                inc(nc.gpsimd.tensor_tensor(dst, h32[:, counts["low"] % 2, k], hi.bitcast(F32), ALU.subtract), "hL_done")
                counts["low"] += 1

            def norm_low(full):
                for k in range(KD):
                    low(hL[:, k, cols(full)], hH[:, k, cols(full)], cols(full))

            norm_low(0)
            for l in range(DEPTH):
                full = side(l, "x")
                for c_ in range(KL):
                    for d in range(2):
                        n = (l * KL + c_) * 2 + d
                        pool.wait_ge(sem["sig_done"], 4 * (l * KL + c_) + 4)
                        inc(nc.gpsimd.tensor_tensor(ig[:, d, :], ig[:, d, :], rc[:, c_, :], ALU.mult), "ig_done")
                    low(hL[:, c_, cols(full)], hH[:, c_, cols(full)], cols(full))
                if l == 0:
                    pool.wait_ge(sem["bd_mm"], 4 * KL)
                    load_block_diag(1)
                for c_ in range(KL):
                    low(hL[:, KL + c_, cols(full)], hH[:, KL + c_, cols(full)], cols(full))
                if l == 0:
                    norm_low(0)
                    for j in range(2 * sum(FFN_GROUPS)):
                        pool.wait_ge(sem["gH_done"], j + 1)
                        s = j % KD
                        inc(nc.gpsimd.tensor_tensor(gL[:, s, :], gt[:, j % 2, :], gH[:, s, :].bitcast(F32), ALU.subtract), "gL_done")
                    norm_low(0)

        @block.scalar
        def _(act):
            def copy(dst, src, scale=1.0):
                return nc.scalar.activation(dst, src, ACT.Copy, scale=scale)

            def rows(tile, at, src):
                n = src.shape[0]
                inc(act.dma_start(prow[at:at + n, tile, :], src), "params_in", 16)

            for t in range(2):
                inc(act.dma_start(xrow[:, t, :], ctx[0, t * P:(t + 1) * P, :]), "x_in", 16)
                inc(act.dma_start(xrow[:, 2 + t, :], x[0, t * P:(t + 1) * P, :]), "x_in", 16)
            rows(4, R_C, c.rearrange("a (r p) -> (a r) p", p=P))
            rows(4, R_CC, c_ctx.rearrange("(r p) -> r p", p=P))
            rows(4, R_FG, final_g.rearrange("(r p) -> r p", p=P))
            inc(act.dma_start(pos[:, :, :], pos_t.rearrange("(k p) n -> p k n", p=P)), "x_in", 16)
            for l in range(DEPTH):
                v = lambda w: w[l].rearrange("(r p) -> r p", p=P)
                m = lambda w: w[l].rearrange("t (r p) -> (t r) p", p=P)
                rows(2 * l, R_BMOD, v(b_mod))
                rows(2 * l, R_N1, v(norm1_g))
                rows(2 * l, R_N2, v(norm2_g))
                rows(2 * l, R_CW, m(lru_conv_w))
                rows(2 * l, R_CB, v(lru_conv_b))
                rows(2 * l, R_BA, m(lru_ba))
                rows(2 * l, R_BX, m(lru_bx))
                rows(2 * l, R_LAM, m(lru_lambda))
                rows(2 * l, R_DWB, v(conf_dw_b))
                rows(2 * l, R_LNG, v(conf_ln_g))
                rows(2 * l, R_LNB, v(conf_ln_b))
                rows(2 * l + 1, 0, m(conf_dw_w))

            act.wait_ge(sem["params_ready"], 5)
            inc(nc.scalar.activation(sv[:, :], par[:, 4, R_C:R_CC + KD], ACT.Silu), "silu_ready")
            act.wait_ge(sem["silu_ready"], 1)
            act.wait_ge(sem["memset_done"], 3)
            for v_ in range(2):
                inc(copy(smat[:, :, v_], sv[:, v_ * KD:(v_ + 1) * KD]), "cols_ready")
            for l in range(DEPTH):
                inc(nc.scalar.activation(sp_t[:, l, :], layer_par(l, R_LAM, 8), ACT.Abs), "decay_done")
            act.wait_ge(sem["decay_done"], 2)
            for l in range(DEPTH):
                inc(nc.scalar.activation(sp_t[:, 2 + l, :], sp_t[:, l, :], ACT.Exp, scale=-1.0), "decay_exp")

            def hi(u):
                kind, a, _ = UNITS[u]
                n = unit_k(kind, a) * UC
                act.wait_ge(unit_full[u % RING], 16 * (u // RING + 1))
                if u >= RING:
                    act.wait_ge(sem["mm_done"], USED[u - RING])
                inc(copy(wh[u % RING][:, 0:n], raw[u % RING][:, 0:n]), "hi_done")

            cnt = dict(row=0, sq=0, sum=0, h32=0, mm=0, ln=0, gp=0)

            def squares(srcs):
                for src, n in srcs:
                    s = cnt["sq"]
                    if s >= 2:
                        act.wait_ge(sem["sum_mm"], s - 1)
                    inc(nc.scalar.activation(sq[:, s % 2, 0:n], src, ACT.Square), "sq_done")
                    cnt["sq"] += 1

            def round_h(dst, n_sel):
                act.wait_ge(sem["h32_done"], cnt["h32"] + 1)
                inc(copy(dst, h32[:, cnt["h32"] % 2, n_sel]), "hH_done")
                cnt["h32"] += 1

            def norm(l, which, full):
                n = T if full == 0 else C
                if l == 0 and which == 1:
                    act.wait_ge(sem["x_ready"], KD * 2)
                else:
                    act.wait_ge(sem["res_done"], RES[(l, which)])
                squares([(xT[:, :, k, :] if full == 0 else xT[:, 1, k, :], n) for k in range(KD)])
                act.wait_ge(sem["sum_mm"], cnt["sq"])
                r_ = rstd[:, 0:n]
                inc(nc.scalar.activation(r_, bank[B_ST][:, 0:n], ACT.Sqrt, scale=1.0 / D, bias=eps[:, 0:1]), "root_done")
                if (l, which) != (1, 2):
                    for k in range(KD):
                        round_h(hH[:, k, cols(full)], cols(full))

            def row_out(l, q):
                n = l * 24 + q
                act.wait_ge(sem["mm_done"], MM[("ad", l, q)])
                if n >= 2:
                    act.wait_ge(sem["mt_mm"], n - 1)
                inc(copy(mrow[0:4, n % 2, :], bank[B_ROW + n % 2][0:4, 0:UC]), "row_out")

            def mix(l):
                full = side(l, "x")
                n = cols(full)
                for c_ in range(KL):
                    g_ = l * KL + c_
                    act.wait_ge(sem["decay_done"], DECAY_ALL)
                    act.wait_ge(sem["rconv_done"], RTAPS * KL * (l + 1))
                    for kd in range(2):
                        for d in range(2):
                            act.wait_ge(sem["bd_mm"], 4 * g_ + 2 * kd + d + 1)
                            if kd == 0 and d == 0 and g_ > 0:
                                act.wait_ge(sem["scan_done"], 2 * g_)
                            dst = (rg, ig)[kd][:, d, :]
                            b_ = layer_par(l, (R_BA, R_BX)[kd] + d * KL + c_)
                            inc(nc.scalar.activation(dst, bank[2 * kd + d][:, :], ACT.Sigmoid, bias=b_), "sig_done")
                    act.wait_ge(sem["sig_done"], 4 * g_ + 4)
                    for d in range(2):
                        inc(nc.scalar.activation(gate_r[:, d, :], rg[:, d, :], ACT.Exp,
                                                 scale=spn[:, l, 0, d * KL + c_:d * KL + c_ + 1]), "act_step")
                    act.wait_ge(sem["act_step"], 6 * g_ + 2)
                    for d in range(2):
                        inc(nc.scalar.activation(rg[:, d, :], rg[:, d, :], ACT.Tanh,
                                                 scale=spn[:, l, 1, d * KL + c_:d * KL + c_ + 1]), "act_step")
                    for d in range(2):
                        inc(nc.scalar.activation(root[:, d, :], gate_r[:, d, :], ACT.Square), "act_step")
                    for d in range(2):
                        act.wait_ge(sem["root_in"], 2 * g_ + d + 1)
                        inc(nc.scalar.activation(root[:, d, :], root[:, d, :], ACT.Sqrt), "root_done")
                    round_h(hH[:, c_, n], n)
                w = T if full == 0 else C
                act.wait_ge(sem["ln_step"], LN_STEPS * l + KL)
                squares([((cv[:, c_, :, :] if full == 0 else cv[:, c_, 1, :]), w) for c_ in range(KL)])
                act.wait_ge(sem["sum_mm"], cnt["sq"])
                inc(nc.scalar.activation(rstd[:, 0:w], bank[B_ST][:, 0:w], ACT.Sqrt, scale=1.0 / DL, bias=eps[:, 0:1]), "root_done")
                for c_ in range(KL):
                    act.wait_ge(sem["ln_step"], LN_STEPS * l + KL + 1 + c_ + 1)
                    k = cnt["h32"]
                    act.wait_ge(sem["hL_done"], k - 1)
                    src = cv[:, c_, :, :] if full == 0 else cv[:, c_, 1, :]
                    inc(nc.scalar.activation(h32[:, k % 2, n], src, ACT.Silu, scale=layer_par(l, R_LNG + c_),
                                             bias=layer_par(l, R_LNB + c_)), "h32_done")
                    round_h(hH[:, KL + c_, n], n)

            hi(0)
            hi(1)
            for u, (kind, a, i) in enumerate(UNITS):
                if u + 2 < NU:
                    hi(u + 2)
                if kind == "win" and i == 0:
                    norm(a, 1, 0)
                if kind == "wout" and i == 0:
                    mix(a)
                if kind == "f1" and i == 0:
                    norm(0, 2, 0)
                if kind == "ad":
                    row_out(a, i)
                if kind == "win" and win_kind(i) != "values":
                    full = side(a, "rec" if win_kind(i) == "rec" else "x")
                    n = T if full == 0 else C
                    for h in range(2):
                        t = 2 * i + h
                        c_ = t % KL
                        act.wait_ge(sem["mm_done"], MM[("win", a, t)])
                        b_ = bank[t % MM_BANKS][:, 0:n]
                        if win_kind(i) == "gates":
                            dst = cv[:, c_, :, :] if full == 0 else cv[:, c_, 1, :]
                            inc(nc.scalar.activation(dst, b_, ACT.Sigmoid), "gates_done")
                        elif win_kind(i) == "rec":
                            inc(copy(rpad[:, c_, :, RPL:RPL + C], b_.rearrange("p (s n) -> p s n", s=2)), "rec_done")
                        else:
                            inc(nc.scalar.activation(gg[:, c_, cols(full)], b_, ACT.Gelu_apprx_tanh), "gelu_done")
                if kind == "f3":
                    for h in range(2):
                        j = 2 * i + h
                        act.wait_ge(sem["mm_done"], MM[("f1", a if kind == "f3" else 0, j)])
                        if j >= 4:
                            act.wait_ge(sem["g_prod"], j - 3)
                        inc(nc.scalar.activation(sg[:, j % 4, :], bank[h][:, :], ACT.Silu), "silu_out")
                    for h in range(2):
                        j = 2 * i + h
                        act.wait_ge(sem["g_prod"], j + 1)
                        if j % KD == 0 and j:
                            act.wait_ge(sem["mm_done"], MM[("f2", j // KD - 1, 7)])
                        inc(copy(gH[:, j % KD, :], gt[:, j % 2, :]), "gH_done")

            norm(1, 2, 1)
            for t in range(2):
                act.wait_ge(sem["route_step"], 4)
                inc(nc.scalar.activation(pr[:, t, :], lg[:, t, :], ACT.Exp, bias=col[:, t, 0:1]), "route_exp")
            for f in range(4):
                act.wait_ge(sem["tok_tr"], f + 1)
                inc(copy(ftH[:, f // 2, (f % 2) * 512:(f % 2 + 1) * 512], bank[2 + f][:, :]), "tokH")

            def gather_out(g):
                for q in range(4):
                    act.wait_ge(sem["gather_mm"], g * 6 + q + 1)
                    inc(copy(xeH[:, 2 * q:2 * q + 2, :], bank[q % 2][:, :].rearrange("p (k n) -> p k n", k=2)), "xe_hi")
                act.wait_ge(sem["gather_mm"], g * 6 + 5)
                inc(copy(pickT[:, :, :], bank[0][:, :].rearrange("p (e n) -> p e n", e=2)), "xe_hi")

            def e_hi(n, s):
                act.wait_ge(e_full[s], n * 16 + 16)
                act.wait_ge(sem["e_used"], n * 6 + s + 1)
                inc(copy(wh[s][:, :], raw[s][:, :]), "e_hi")

            def e_silu(n, c_):
                act.wait_ge(sem["e_used"], n * 6 + 6 + 2 * (c_ + 1))
                inc(nc.scalar.activation(esg[:, c_, :], bank[2 + c_][:, 0:UC], ACT.Silu), "e_silu")

            def e_gh(n, c_):
                act.wait_ge(sem["g_tr"], n * 2 + c_ + 1)
                inc(copy(egH[:, c_, :], bank[c_][:, 0:UC]), "e_gH")

            def e_body(n):
                e_hi(n, 0)
                e_hi(n, 1)
                e_hi(n, 2)
                e_silu(n, 0)
                e_hi(n, 3)
                e_gh(n, 0)
                e_hi(n, 4)
                e_silu(n, 1)
                e_hi(n, 5)
                e_gh(n, 1)

            def y_out(it, e, h):
                act.wait_ge(sem["y_mm"], it * 2 + e + 1)
                if e == 1:
                    act.wait_ge(sem["comb_mm"], it * 8 + 2 * h + 2)
                inc(copy(yH[:, h, :], bank[4 + 2 * e + h][:, :], scale=cs[:, e:e + 1]), "y_hi")

            act.wait_ge(sem["rounds_done"], 1)
            n_rounds = act.value_load(rounds[0:1, 0:1], min_val=1, max_val=2)
            gather_out(0)
            with act.Fori(0, n_rounds) as r:
                with act.Fori(0, NE // 2) as i:
                    it = r * (NE // 2) + i
                    with act.Fori(0, NPAIR) as j:
                        e_body(it * BODIES + j)
                    e_body(it * BODIES + NPAIR)
                    for h in range(2):
                        y_out(it, 0, h)
                    with act.Fori(0, NPAIR) as j:
                        e_body(it * BODIES + NPAIR + 1 + j)
                    for h in range(2):
                        y_out(it, 1, h)
                    gather_out(it + 1)
            act.wait_ge(sem["acc_done"], n_rounds * (NE // 2 * 8))
            squares([(xT[:, 1, k, :], S) for k in range(KD)])
            act.wait_ge(sem["sum_mm"], cnt["sq"])
            inc(nc.scalar.activation(rstd[:, 0:S], bank[B_ST][:, 0:S], ACT.Sqrt, scale=1.0 / D, bias=eps[:, 0:1]), "root_done")
            for t in range(2):
                for h in range(2):
                    f = 2 * t + h
                    act.wait_ge(sem["fin_tr"], f + 1)
                    inc(copy(orow[:, t, h * 512:(h + 1) * 512], bank[f][:, :]), "fin_out")

        @block.vector
        def _(dve):
            V = nc.vector
            state = dict(step=0, h32=0, cv=0, rs=0)

            def step(ins):
                inc(ins, "dve_step")
                state["step"] += 1
                dve.wait_ge(sem["dve_step"], state["step"])

            for k in range(KD):
                dve.wait_ge(sem["x_tr"], k + 1)
                if k == 0:
                    dve.wait_ge(sem["x_in"], 16 * 5)
                b_ = bank[k % 4]
                inc(V.tensor_copy(xT[:, 0, k, :], b_[:, 0:C]), "x_ready")
                inc(V.tensor_tensor(xT[:, 1, k, :], b_[:, C:T], pos[:, k, :], ALU.add), "x_ready")
            for n, (tile, rows_) in enumerate(ROW_PARTS):
                dve.wait_ge(sem["params_t"], n + 1)
                inc(V.tensor_copy(par[:, tile, 0:rows_], bank[4 + n % 4][:, 0:rows_]), "params_ready")
            dve.wait_ge(sem["params_ready"], 5)
            dve.wait_ge(sem["silu_ready"], 1)
            dve.wait_ge(sem["cols_ready"], 2)
            for v_ in range(2):
                inc(V.tensor_tensor(smat[:, :, 2 + v_], sv[:, v_ * KD:(v_ + 1) * KD],
                                    smat[:, :, v_].bitcast(F32), ALU.subtract), "cols_ready")
            inc(V.tensor_copy(fg[:, :], par[:, 4, R_FG:R_FG + KD]), "cols_ready")
            for l in range(DEPTH):
                dve.wait_ge(sem["decay_exp"], l + 1)
                z, z2, p_ = sp_t[:, l, :], spn[:, l, 0, :], spn[:, l, 1, :]
                v_ = sp_t[:, 2 + l, :]
                step(V.tensor_scalar(z, v_, 2.0, None, ALU.add))
                step(V.reciprocal(z, z))
                step(V.tensor_tensor(z, z, v_, ALU.mult))
                step(V.tensor_tensor(z2, z, z, ALU.mult))
                step(V.tensor_scalar(p_, z2, 1.0 / 17, 1.0 / 15, ALU.mult, ALU.add))
                for o in (13, 11, 9, 7, 5, 3, 1):
                    step(V.tensor_tensor(p_, p_, z2, ALU.mult))
                    step(V.tensor_scalar(p_, p_, 1.0 / o, None, ALU.add))
                step(V.tensor_tensor(p_, p_, z, ALU.mult))
                step(V.tensor_scalar(z, layer_par(l, R_LAM, 8), -1.0, 0.0, ALU.mult, ALU.max))
                step(V.scalar_tensor_tensor(z, p_, 2.0, z, ALU.mult, ALU.add))
                inc(V.tensor_scalar(spn[:, l, 0, :], z, -LRU_C, None, ALU.mult), "decay_done")
                inc(V.tensor_scalar(spn[:, l, 1, :], z, LRU_C, None, ALU.mult), "decay_done")

            def lo(u):
                kind, a, _ = UNITS[u]
                n = unit_k(kind, a) * UC
                s = u % RING
                dve.wait_ge(sem["hi_done"], u + 1)
                inc(V.tensor_tensor(wl[s][:, 0:n], raw[s][:, 0:n], wh[s][:, 0:n].bitcast(F32), ALU.subtract), "lo_done")

            def mods(l, part):
                a, b = ((0, 2 * KD), (2 * KD, NMOD * KD), (0, NMOD * KD))[part]
                dve.wait_ge(sem["mt_mm"], 24 * l + (8 if part == 0 else 24))
                ps = bank[B_MT][:, 0:2 * NMOD * KD].rearrange("p (m v) -> p m v", v=2)
                for v_ in range(2):
                    inc(V.tensor_tensor(mt[l][:, a:b, v_], ps[:, a:b, v_], layer_par(l, R_BMOD + a, b - a), ALU.add), "mod_ready")

            def norm(l, which, full):
                n = T if full == 0 else C
                sh, sc = (0, KD) if which == 1 else (3 * KD, 4 * KD)
                g_ = layer_par(l, R_N1 if which == 1 else R_N2, KD)
                if which == 1:
                    if l == 0:
                        mods(0, 0)
                    dve.wait_ge(sem["mod_ready"], 4 * l + 2)
                else:
                    dve.wait_ge(sem["mod_ready"], 4 + 2 * l)
                for v_ in range(2):
                    step(V.scalar_tensor_tensor(amp[:, :, v_], mt[l][:, sc:sc + KD, v_], 1.0, g_, ALU.add, ALU.mult))
                state["rs"] += 1
                dve.wait_ge(sem["root_done"], ROOT[(l, which)])
                step(V.reciprocal(rstd[:, 0:n], rstd[:, 0:n]))
                for k in range(KD):
                    src = xT[:, :, k, :] if full == 0 else xT[:, 1, k, :]
                    r_ = rstd[:, 0:n].rearrange("p (s n) -> p s n", s=2) if full == 0 else rstd[:, 0:n]
                    t_ = norm_t[:, 0:n].rearrange("p (s n) -> p s n", s=2) if full == 0 else norm_t[:, 0:n]
                    if k:
                        dve.wait_ge(sem["fT_done" if (l, which) == (1, 2) else "h32_done"], k if (l, which) == (1, 2) else state["h32"])
                    step(V.tensor_tensor(t_, src, r_, ALU.mult))
                    if (l, which) == (1, 2):
                        inc(V.tensor_scalar(fT[:, k, :], norm_t[:, 0:n], amp[:, k, 0:1], mt[l][:, sh + k, 0:1], ALU.mult, ALU.add), "fT_done")
                        continue
                    m_ = state["h32"]
                    if m_ >= 2:
                        dve.wait_ge(sem["hL_done"], m_ - 1)
                    if full == 0:
                        step(V.tensor_scalar(h32[:, m_ % 2, 0:C], norm_t[:, 0:C], amp[:, k, 1:2], mt[l][:, sh + k, 1:2], ALU.mult, ALU.add))
                        inc(V.tensor_scalar(h32[:, m_ % 2, C:T], norm_t[:, C:T], amp[:, k, 0:1], mt[l][:, sh + k, 0:1], ALU.mult, ALU.add), "h32_done")
                    state["h32"] += 1

            CONV = [(t, c_) for t in range(TAPS) for c_ in range(KL)]

            def conv(l, a, b):
                full = side(l, "x")
                for m_ in range(a, min(b, len(CONV))):
                    t, c_ = CONV[m_]
                    base = l * len(CONV)
                    g_ = glu[:, c_, :, t:t + C] if full == 0 else glu[:, c_, 1, t:t + C]
                    o_ = cv[:, c_, :, :] if full == 0 else cv[:, c_, 1, :]
                    if t == 0:
                        inc(V.tensor_scalar(o_, g_, tap(l, t, c_), layer_par(l, R_DWB + c_), ALU.mult, ALU.add), "conv_step")
                    else:
                        dve.wait_ge(sem["conv_step"], base + m_ - KL + 1)
                        inc(V.scalar_tensor_tensor(o_, g_, tap(l, t, c_), o_, ALU.mult, ALU.add), "conv_step")

            def mix(l, conv_at):
                full = side(l, "x")
                n = cols(full)
                dve.wait_ge(sem["rec_done"], KL * (l + 1))
                dve.wait_ge(sem["pad_zero"], 4 * (l + 1))
                for t in range(RTAPS):
                    for c_ in range(KL):
                        m_ = RTAPS * KL * l + t * KL + c_
                        src = rpad[:, c_, :, t:t + C]
                        dst = rc[:, c_, :].rearrange("p (s n) -> p s n", s=2)
                        w_ = layer_par(l, R_CW + t * KL + c_)
                        if t == 0:
                            inc(V.tensor_scalar(dst, src, w_, layer_par(l, R_CB + c_), ALU.mult, ALU.add), "rconv_done")
                        else:
                            dve.wait_ge(sem["rconv_done"], m_ - KL + 1)
                            inc(V.scalar_tensor_tensor(dst, src, w_, dst, ALU.mult, ALU.add), "rconv_done")
                per = (len(CONV) - conv_at + KL - 1) // KL
                for c_ in range(KL):
                    g_ = l * KL + c_
                    conv(l, conv_at + per * c_, conv_at + per * (c_ + 1))
                    for d in range(2):
                        dve.wait_ge(sem["act_step"], 6 * g_ + 6)
                        inc(V.scalar_tensor_tensor(root[:, d, :], root[:, d, :], 1.0, rg[:, d, :], ALU.add, ALU.mult), "root_in")
                    for d in range(2):
                        dve.wait_ge(sem["root_done"], ROOT[("mix", l)] + 2 * c_ + d + 1)
                        dve.wait_ge(sem["ig_done"], 2 * g_ + d + 1)
                        step(V.tensor_tensor(ig[:, d, :], ig[:, d, :], root[:, d, :], ALU.mult))
                    inc(V.tensor_tensor_scan(yy[:, c_, :], gate_r[:, 0, :], ig[:, 0, :], 0.0, ALU.mult, ALU.add), "scan_done")
                    step(V.tensor_tensor_scan(root[:, 1, 0:C][:, ::-1], gate_r[:, 1, 0:C][:, ::-1], ig[:, 1, 0:C][:, ::-1], 0.0, ALU.mult, ALU.add))
                    inc(V.tensor_tensor_scan(root[:, 1, C:T][:, ::-1], gate_r[:, 1, C:T][:, ::-1], ig[:, 1, C:T][:, ::-1], root[:, 1, 0:1], ALU.mult, ALU.add), "scan_done")
                    dve.wait_ge(sem["scan_done"], 2 * g_ + 2)
                    step(V.tensor_tensor(yy[:, c_, n], yy[:, c_, n], root[:, 1, n], ALU.add))
                    m_ = state["h32"]
                    if m_ >= 2:
                        dve.wait_ge(sem["hL_done"], m_ - 1)
                    dve.wait_ge(sem["gelu_done"], KL * l + c_ + 1)
                    inc(V.tensor_tensor(h32[:, m_ % 2, n], yy[:, c_, n], gg[:, c_, n], ALU.mult), "h32_done")
                    state["h32"] += 1
                dve.wait_ge(sem["conv_step"], (l + 1) * len(CONV))
                dve.wait_ge(sem["ln_mm"], l + 1)
                w = T if full == 0 else C

                def sel(c_):
                    return cv[:, c_, :, :] if full == 0 else cv[:, c_, 1, :]

                def two(ap):
                    return ap.rearrange("p (s n) -> p s n", s=2) if full == 0 else ap

                for c_ in range(KL):
                    inc(V.scalar_tensor_tensor(sel(c_), two(bank[B_ST][:, 0:w]), -1.0 / DL, sel(c_), ALU.mult, ALU.add), "ln_step")
                dve.wait_ge(sem["root_done"], ROOT[("ln", l)])
                inc(V.reciprocal(rstd[:, 0:w], rstd[:, 0:w]), "ln_step")
                dve.wait_ge(sem["ln_step"], LN_STEPS * l + KL + 1)
                for c_ in range(KL):
                    inc(V.tensor_tensor(sel(c_), sel(c_), two(rstd[:, 0:w]), ALU.mult), "ln_step")
                state["h32"] += KL

            def residual(l, k, b_, full, gate):
                if full == 0:
                    step(V.scalar_tensor_tensor(xT[:, 0, k, :], b_[:, 0:C], mt[l][:, gate + k, 1:2], xT[:, 0, k, :], ALU.mult, ALU.add))
                lat = b_[:, C:T] if full == 0 else b_[:, 0:C]
                inc(V.scalar_tensor_tensor(xT[:, 1, k, :], lat, mt[l][:, gate + k, 0:1], xT[:, 1, k, :], ALU.mult, ALU.add), "res_done")

            lo(0)
            lo(1)
            conv_at = 0
            for u, (kind, a, i) in enumerate(UNITS):
                if u + 2 < NU:
                    lo(u + 2)
                if kind == "win" and i == 0:
                    norm(a, 1, 0)
                    conv_at = 0
                    inc(V.memset(glu[:, :, :, 0:PAD], 0.0), "pad_zero")
                    inc(V.memset(glu[:, :, :, PAD + C:GW], 0.0), "pad_zero")
                    inc(V.memset(rpad[:, :, :, 0:RPL], 0.0), "pad_zero")
                    inc(V.memset(rpad[:, :, :, RPL + C:RW], 0.0), "pad_zero")
                if kind == "wout" and i == 0:
                    mix(a, conv_at)
                if kind == "f1" and i == 0:
                    norm(0, 2, 0)
                if kind == "win" and win_kind(i) == "values":
                    full = side(a, "x")
                    n = T if full == 0 else C
                    for h in range(2):
                        t = 2 * i + h
                        c_ = t % KL
                        dve.wait_ge(sem["mm_done"], MM[("win", a, t)])
                        dve.wait_ge(sem["gates_done"], KL * a + c_ + 1)
                        b_ = bank[t % MM_BANKS][:, 0:n]
                        if full == 0:
                            inc(V.tensor_tensor(glu[:, c_, :, PAD:PAD + C], b_.rearrange("p (s n) -> p s n", s=2), cv[:, c_, :, :], ALU.mult), "glu_done")
                        else:
                            inc(V.tensor_tensor(glu[:, c_, 1, PAD:PAD + C], b_, cv[:, c_, 1, :], ALU.mult), "glu_done")
                    if i == 3:
                        dve.wait_ge(sem["glu_done"], KL * (a + 1))
                        dve.wait_ge(sem["pad_zero"], 4 * (a + 1))
                if kind == "wout":
                    full = side(a, "x")
                    for h in range(2):
                        k = 2 * i + h
                        if k == 0 and a == 0:
                            mods(0, 1)
                        if k == 0:
                            dve.wait_ge(sem["mod_ready"], 4 + 2 * a)
                        dve.wait_ge(sem["mm_done"], MM[("wout", a, k)])
                        residual(a, k, bank[k % MM_BANKS], full, 2 * KD)
                if kind == "f3":
                    for h in range(2):
                        j = 2 * i + h
                        dve.wait_ge(sem["mm_done"], MM[("f3", a, j)])
                        dve.wait_ge(sem["silu_out"], j + 1)
                        if j >= 2:
                            dve.wait_ge(sem["gL_done"], j - 1)
                        inc(V.tensor_tensor(gt[:, j % 2, :], sg[:, j % 4, :], bank[2 + h][:, :], ALU.mult), "g_prod")
                if kind == "f2":
                    for h in range(2):
                        k = 2 * i + h
                        dve.wait_ge(sem["mm_done"], MM[("f2", a, k)])
                        residual(0, k, bank[k % MM_BANKS], 0, 5 * KD)
                if kind == "ad" and a == 1 and i == 23:
                    mods(1, 2)
                for lay, more in ((0, 4), (1, 8)):
                    if AT[("win", lay, 3)] < u < AT[("wout", lay, 0)]:
                        conv(lay, conv_at, conv_at + more)
                        conv_at += more

            inc(V.memset(col[:, 0, 6:7], 0.0), "e_lo", 6)
            norm(1, 2, 1)
            rs = {"n": 0}

            def rstep(ins):
                inc(ins, "route_step")
                rs["n"] += 1
                dve.wait_ge(sem["route_step"], rs["n"])

            dve.wait_ge(sem["logits_mm"], 1)
            rstep(V.tensor_copy(lg[:, :, :], bank[0][:, 0:2 * NE].rearrange("p (t e) -> p t e", t=2)))
            rstep(V.tensor_reduce(col[:, :, 0:1], lg[:, :, :], axis=AX.X, op=ALU.max))
            rstep(V.tensor_scalar(col[:, :, 0:1], col[:, :, 0:1], -1.0, None, ALU.mult))
            rstep(V.memset(tab[:, :, 0, :], 4 * FAR))
            dve.wait_ge(sem["route_exp"], 2)
            rstep(V.tensor_reduce(col[:, :, 1:2], pr[:, :, :], axis=AX.X, op=ALU.add))
            rstep(V.reciprocal(col[:, :, 1:2], col[:, :, 1:2]))
            rstep(V.memset(tab[:, :, 1, :], 0.0))
            for t in range(2):
                rstep(V.tensor_scalar(pr[:, t, :], pr[:, t, :], col[:, t, 1:2], None, ALU.mult))
                rstep(V.max(top[:, t, :], pr[:, t, :]))
                rstep(V.max_index(tix[:, t, :], top[:, t, :], pr[:, t, :]))
                rstep(V.tensor_copy(tif[:, t, :], tix[:, t, :]))
                rstep(V.tensor_tensor(col[:, t, 2:3], top[:, t, 0:1], top[:, t, 1:2], ALU.add))
                rstep(V.reciprocal(col[:, t, 2:3], col[:, t, 2:3]))
                rstep(V.tensor_scalar(col[:, t, 4:6], top[:, t, 0:2], col[:, t, 2:3], None, ALU.mult))
                for j in range(2):
                    rstep(V.tensor_scalar(oh[:, t, j, :], K[:, K_IOTA8:K_IOTA8 + NE], tif[:, t, j:j + 1], None, ALU.is_equal))
                rstep(V.tensor_tensor(mask[:, t, :], oh[:, t, 0, :], oh[:, t, 1, :], ALU.add))
                rstep(V.tensor_scalar(oh[:, t, 0, :], oh[:, t, 0, :], col[:, t, 4:5], None, ALU.mult))
                rstep(V.scalar_tensor_tensor(tab[:, t, 1, 0:NE], oh[:, t, 1, :], col[:, t, 5:6], oh[:, t, 0, :], ALU.mult, ALU.add))
                rstep(V.tensor_copy(tab[:, t, 1, NE:2 * NE], tab[:, t, 1, 0:NE]))
            dve.wait_ge(sem["pos_mm"], 1)
            for t in range(2):
                rstep(V.tensor_scalar(lg[:, t, :], mask[:, t, :], -FAR, FAR, ALU.mult, ALU.add))
                rstep(V.tensor_tensor(tab[:, t, 0, 0:NE], bank[1][:, t * NE:(t + 1) * NE], lg[:, t, :], ALU.add))
                rstep(V.tensor_scalar(tab[:, t, 0, NE:2 * NE], tab[:, t, 0, 0:NE], -float(CAP), None, ALU.add))
            rstep(V.tensor_reduce(flag[:, 0:1], bank[1][:, 2 * NE:3 * NE], axis=AX.X, op=ALU.max))
            rstep(V.tensor_scalar(flag[:, 1:2], flag[:, 0:1], CAP + 0.5, 1.0, ALU.is_gt, ALU.add))
            inc(V.tensor_copy(rounds[:, :], flag[:, 1:2]), "rounds_done")
            assert rs["n"] == ROUTE_ALL, rs["n"]
            for f in range(4):
                dve.wait_ge(sem["tokH"], f + 1)
                half = slice((f % 2) * 512, (f % 2 + 1) * 512)
                inc(V.tensor_tensor(ftL[:, f // 2, half], bank[2 + f][:, :], ftH[:, f // 2, half].bitcast(F32), ALU.subtract), "tokL")

            dve.wait_ge(sem["rounds_done"], 1)
            n_rounds = dve.value_load(rounds[0:1, 0:1], min_val=1, max_val=2)

            def picks(g):
                inc(V.tensor_copy(cur[:, :, :, :].rearrange("p t k e -> p (t k) e"),
                                  tab[:, :, :, bass.ds(g * 2, 2)].rearrange("p t k e -> p (t k) e")), "pick_done")
                dve.wait_ge(sem["pick_done"], g * 5 + 1)
                for t in range(2):
                    for e in range(2):
                        inc(V.tensor_scalar(pick[:, t, e * CAP:(e + 1) * CAP], K[:, K_IOTA:K_IOTA + CAP],
                                            cur[:, t, 0, e:e + 1], None, ALU.is_equal), "pick_done")

            def gather_out(g):
                for q in range(4):
                    dve.wait_ge(sem["xe_hi"], g * 5 + q + 1)
                    xs = slice(2 * q, 2 * q + 2)
                    inc(V.tensor_tensor(xeL[:, xs, :], bank[q % 2][:, :].rearrange("p (k n) -> p k n", k=2),
                                        xeH[:, xs, :].bitcast(F32), ALU.subtract), "xe_lo")
                dve.wait_ge(sem["gather_mm"], g * 6 + 6)
                inc(V.tensor_copy(cs[:, :], bank[1][:, 0:2]), "xe_lo")

            def e_lo(n, s):
                dve.wait_ge(sem["e_hi"], n * 6 + s + 1)
                inc(V.tensor_tensor(wl[s][:, :], raw[s][:, :], wh[s][:, :].bitcast(F32), ALU.subtract), "e_lo")

            def e_prod(n, c_):
                dve.wait_ge(sem["e_silu"], n * 2 + c_ + 1)
                inc(V.tensor_tensor(esg[:, c_, :], esg[:, c_, :], bank[2 + c_][:, UC:2 * UC], ALU.mult), "e_prod")

            def e_gl(n, c_):
                dve.wait_ge(sem["e_gH"], n * 2 + c_ + 1)
                inc(V.tensor_tensor(egL[:, c_, :], bank[c_][:, 0:UC], egH[:, c_, :].bitcast(F32), ALU.subtract), "e_gL")

            def e_body(n):
                e_lo(n, 0)
                e_lo(n, 1)
                e_lo(n, 2)
                e_prod(n, 0)
                e_lo(n, 3)
                e_gl(n, 0)
                e_lo(n, 4)
                e_prod(n, 1)
                e_lo(n, 5)
                e_gl(n, 1)

            def y_low(it, e, h):
                dve.wait_ge(sem["y_hi"], it * 4 + 2 * e + h + 1)
                inc(V.scalar_tensor_tensor(yL[:, h, :], bank[4 + 2 * e + h][:, :], cs[:, e:e + 1],
                                           yH[:, h, :].bitcast(F32), ALU.mult, ALU.subtract), "y_lo")

            def accumulate(it, f):
                dve.wait_ge(sem["comb_mm"], it * 8 + f + 1)
                k = (f % 4) * 2
                V.scalar_tensor_tensor(xT[:, 1, k, :], bank[f % 2][:, 0:S], g2[k], xT[:, 1, k, :], ALU.mult, ALU.add)
                inc(V.scalar_tensor_tensor(xT[:, 1, k + 1, :], bank[f % 2][:, S:2 * S], g2[k + 1], xT[:, 1, k + 1, :], ALU.mult, ALU.add), "acc_done")

            g2 = [mt[1][:, 5 * KD + k, 0:1] for k in range(KD)]
            picks(0)
            gather_out(0)
            with dve.Fori(0, n_rounds) as r:
                with dve.Fori(0, NE // 2) as i:
                    it = r * (NE // 2) + i
                    with dve.Fori(0, NPAIR) as j:
                        e_body(it * BODIES + j)
                    e_body(it * BODIES + NPAIR)
                    for h in range(2):
                        y_low(it, 0, h)
                    with dve.Fori(0, NPAIR) as j:
                        e_body(it * BODIES + NPAIR + 1 + j)
                    picks(it + 1)
                    accumulate(it, 0)
                    accumulate(it, 1)
                    y_low(it, 1, 0)
                    accumulate(it, 2)
                    accumulate(it, 3)
                    y_low(it, 1, 1)
                    for f in range(4, 8):
                        accumulate(it, f)
                    gather_out(it + 1)
            dve.wait_ge(sem["root_done"], ROOT["final"])
            step(V.reciprocal(rstd[:, 0:S], rstd[:, 0:S]))
            for k in range(KD):
                step(V.tensor_tensor(xT[:, 1, k, :], xT[:, 1, k, :], rstd[:, 0:S], ALU.mult))
                inc(V.tensor_scalar(xT[:, 1, k, :], xT[:, 1, k, :], fg[:, k:k + 1], None, ALU.mult), "norm_step")

        @block.tensor
        def _(pe):
            mm = nc.tensor.matmul
            ident = K[:, K_ID:K_ID + P]
            ones = K[:, K_ONE:K_ONE + P]

            pe.wait_ge(sem["consts_in"], 16)
            pe.wait_ge(sem["x_in"], 16 * 5)
            for k in range(KD):
                if k >= 4:
                    pe.wait_ge(sem["x_ready"], 2 * (k - 3))
                for t in range(4):
                    last = nc.tensor.transpose(bank[k % 4][:, t * P:(t + 1) * P], xrow[:, t, k * P:(k + 1) * P], ident)
                inc(last, "x_tr")
            pe.wait_ge(sem["params_in"], 16 * PARAM_DMAS)
            for n, (tile, rows_) in enumerate(ROW_PARTS):
                if n >= 4:
                    pe.wait_ge(sem["params_ready"], n - 3)
                inc(nc.tensor.transpose(bank[4 + n % 4][:, 0:rows_], prow[0:rows_, tile, :], ident[0:rows_, 0:rows_]), "params_t")
            pe.wait_ge(sem["cols_ready"], 4)
            pe.wait_ge(sem["memset_done"], 3)

            pending = []

            def transpose_rows():
                while pending:
                    l, q = pending.pop()
                    n = l * 24 + q
                    pe.wait_ge(sem["row_out"], n + 1)
                    if n == 24:
                        pe.wait_ge(sem["mod_ready"], 4)
                    for h in range(2):
                        o_ = (2 * q + h) * 2
                        last = mm(bank[B_MT][:, o_:o_ + 2], mrow[0:4, n % 2, h * P:(h + 1) * P], K[0:4, K_COMB:K_COMB + 2],
                                  start=True, stop=True)
                    inc(last, "mt_mm")

            st = dict(sq=0, hl=0, norms=0)

            def sums(n, count, w):
                for k in range(count):
                    pe.wait_ge(sem["sq_done"], st["sq"] + 1)
                    inc(mm(bank[B_ST][:, 0:n], w, sq[:, st["sq"] % 2, 0:n], start=(k == 0), stop=(k == count - 1)), "sum_mm")
                    st["sq"] += 1

            def chunk(dst, u, k_n, h, rH, rL, sel):
                s = u % RING
                n = 0
                for k in range(k_n):
                    w_ = slice(k * UC + h * P, k * UC + (h + 1) * P)
                    for l_, r_ in split3(wh[s], wl[s], rH, rL):
                        last = mm(dst, l_[:, w_], r_[:, k, sel], start=(n == 0), stop=(n == 3 * k_n - 1))
                        n += 1
                return last

            def mix(l):
                full = side(l, "x")
                w = T if full == 0 else C
                pe.wait_ge(sem["gelu_done"], KL * (l + 1))
                for c_ in range(KL):
                    g_ = l * KL + c_
                    pe.wait_ge(sem["rconv_done"], RTAPS * KL * l + (RTAPS - 1) * KL + c_ + 1)
                    pe.wait_ge(sem["bd_in"], 16 * 8 * (l + 1))
                    for kd in range(2):
                        for d in range(2):
                            b_ = 2 * kd + d
                            if c_:
                                pe.wait_ge(sem["sig_done"], 4 * (g_ - 1) + b_ + 1)
                            inc(mm(bank[b_][:, :], bdw[:, c_, d, kd, :], rc[:, c_, :], start=True, stop=True), "bd_mm")
                pe.wait_ge(sem["conv_step"], (l + 1) * TAPS * KL)
                for c_ in range(KL):
                    last = mm(bank[B_ST][:, 0:w], ones, cv[:, c_, :, :] if full == 0 else cv[:, c_, 1, :],
                              start=(c_ == 0), stop=(c_ == KL - 1))
                inc(last, "ln_mm")
                pe.wait_ge(sem["ln_step"], LN_STEPS * l + KL)
                sums(w, KL, ones)
                pe.wait_ge(sem["hL_done"], HL[("mix", l)])
                pe.wait_ge(sem["sig_done"], 4 * KL * (l + 1))

            for u, (kind, a, i) in enumerate(UNITS):
                if kind == "win" and i == 0:
                    transpose_rows()
                    sums(T, KD, ones)
                    pe.wait_ge(sem["hL_done"], HL[("norm", a, 1)])
                if kind == "wout" and i == 0:
                    transpose_rows()
                    mix(a)
                if kind == "f1" and i == 0:
                    sums(T, KD, ones)
                    pe.wait_ge(sem["hL_done"], HL[("norm", 0, 2)])
                pe.wait_ge(sem["lo_done"], u + 1)
                s = u % RING
                if kind == "ad":
                    n = a * 24 + i
                    if n >= 2:
                        pe.wait_ge(sem["row_out"], n - 1)
                    b_ = bank[B_ROW + n % 2][:, 0:UC]
                    for k in range(KD):
                        for w_ in (wh[s], wl[s]):
                            last = mm(b_, smat[:, k, :], w_[:, k * UC:(k + 1) * UC], start=(k == 0 and w_ is wh[s]),
                                      stop=(k == KD - 1 and w_ is wl[s]))
                    inc(last, "mm_done")
                elif kind == "win":
                    full = side(a, "rec" if win_kind(i) == "rec" else "x")
                    w = T if full == 0 else C
                    for h in range(2):
                        t = 2 * i + h
                        if t >= MM_BANKS:
                            free = {"gates": "gates_done", "values": "glu_done", "rec": "rec_done"}[win_kind((t - 4) // 2)]
                            pe.wait_ge(sem[free], KL * a + t % KL + 1)
                        last = chunk(bank[t % MM_BANKS][:, 0:w], u, KD, h, hH, hL, cols(full))
                        inc(last, "mm_done")
                elif kind == "wout":
                    full = side(a, "x")
                    w = T if full == 0 else C
                    for h in range(2):
                        k_ = 2 * i + h
                        if k_ >= MM_BANKS:
                            pe.wait_ge(sem["res_done"], RES[("wout", a)] + k_ - MM_BANKS + 1)
                        last = chunk(bank[k_ % MM_BANKS][:, 0:w], u, KD, h, hH, hL, cols(full))
                        inc(last, "mm_done")
                elif kind in ("f1", "f3"):
                    for h in range(2):
                        j = 2 * i + h
                        if j >= 2:
                            pe.wait_ge(sem["silu_out" if kind == "f1" else "g_prod"], j - 1)
                        if kind == "f1" and j % KD < 2 and j >= KD:
                            pe.wait_ge(sem["res_done"], RES[("f2", j // KD - 1)] + 8)
                        last = chunk(bank[(0 if kind == "f1" else 2) + h][:, :], u, KD, h, hH, hL, slice(0, T))
                        inc(last, "mm_done")
                elif kind == "f2":
                    for h in range(2):
                        k_ = 2 * i + h
                        if k_ == 0:
                            pe.wait_ge(sem["gL_done"], 2 * sum(FFN_GROUPS[:a + 1]))
                        if k_ < 2:
                            pe.wait_ge(sem["silu_out"], 2 * sum(FFN_GROUPS[:a + 1]))
                        if k_ >= MM_BANKS:
                            pe.wait_ge(sem["res_done"], RES[("f2", a)] + k_ - MM_BANKS + 1)
                        last = chunk(bank[k_ % MM_BANKS][:, :], u, 2 * FFN_GROUPS[a], h, gH, gL, slice(0, T))
                        inc(last, "mm_done")
                transpose_rows()
                if kind == "ad":
                    pending.append((a, i))

            sums(S, KD, ones)
            pe.wait_ge(sem["fT_done"], KD)
            pe.wait_ge(sem["router_in"], 16)
            for t in range(2):
                tok = slice(t * P, (t + 1) * P)
                for k in range(KD):
                    last = mm(bank[0][:, t * NE:(t + 1) * NE], fT[:, k, tok], rt[:, k, :], start=(k == 0), stop=(k == KD - 1))
            inc(last, "logits_mm")
            for f in range(4):
                t = f // 2
                for k in range(4):
                    last = nc.tensor.transpose(bank[2 + f][:, k * P:(k + 1) * P],
                                               fT[:, (f % 2) * 4 + k, t * P:(t + 1) * P], ident)
                inc(last, "tok_tr")
            pe.wait_ge(sem["route_step"], ROUTE_MASKS)
            up = K[:, K_UP:K_UP + P]
            for o_, parts in ((0, ((up, 0),)), (NE, ((ones, 0), (up, 1))), (2 * NE, ((ones, 0), (ones, 1)))):
                for n, (w_, t) in enumerate(parts):
                    last = mm(bank[1][:, o_:o_ + NE], w_, mask[:, t, :], start=(n == 0), stop=(n == len(parts) - 1))
            inc(last, "pos_mm")

            pe.wait_ge(sem["rounds_done"], 1)
            n_rounds = pe.value_load(rounds[0:1, 0:1], min_val=1, max_val=2)

            def gather(g, after):
                pe.wait_ge(sem["pick_done"], g * 5 + 5)
                for q in range(4):
                    if q >= 2:
                        pe.wait_ge(sem["xe_lo"], g * 5 + q - 1)
                    elif after is not None:
                        pe.wait_ge(sem["acc_done"], after * 8 + 7 + q)
                    for kk in range(2):
                        k = 2 * q + kk
                        n = 0
                        for t in range(2):
                            for ft in (ftH, ftL):
                                last = mm(bank[q % 2][:, kk * 2 * CAP:(kk + 1) * 2 * CAP], ft[:, t, k * P:(k + 1) * P],
                                          pick[:, t, :], start=(n == 0), stop=(n == 3))
                                n += 1
                    inc(last, "gather_mm")
                pe.wait_ge(sem["xe_lo"], g * 5 + 3)
                for e in range(2):
                    for t in range(2):
                        last = nc.tensor.transpose(bank[0][:, e * S + t * P:e * S + (t + 1) * P],
                                                   pick[:, t, e * CAP:(e + 1) * CAP].bitcast(F32), ident)
                inc(last, "gather_mm")
                pe.wait_ge(sem["xe_lo"], g * 5 + 4)
                for e in range(2):
                    for t in range(2):
                        last = mm(bank[1][:, e:e + 1], pick[:, t, e * CAP:(e + 1) * CAP].bitcast(F32), cur[:, t, 1, e:e + 1],
                                  start=(t == 0), stop=(t == 1))
                inc(last, "gather_mm")
                pe.wait_ge(sem["xe_hi"], g * 5 + 5)
                pe.wait_ge(sem["xe_lo"], g * 5 + 5)

            def e_up(n, s, e):
                pe.wait_ge(sem["e_lo"], n * 6 + 6 + s + 1)
                m_ = 0
                dst = bank[2 + s // 2][:, (s % 2) * UC:(s % 2 + 1) * UC]
                for k in range(KD):
                    for l_, r_ in split3(xeH, xeL, wh[s], wl[s]):
                        last = mm(dst, l_[:, k, e * CAP:(e + 1) * CAP], r_[:, k * UC:(k + 1) * UC],
                                  start=(m_ == 0), stop=(m_ == 3 * KD - 1))
                        m_ += 1
                inc(last, "e_used")

            def e_tr(n, c_):
                pe.wait_ge(sem["e_prod"], n * 2 + c_ + 1)
                for f in range(2):
                    last = nc.tensor.transpose(bank[c_][:, f * P:(f + 1) * P], esg[:, c_, f * P:(f + 1) * P], ident)
                inc(last, "g_tr")

            def e_down(n, c_, e, f):
                s = 4 + c_
                if f == 0:
                    pe.wait_ge(sem["e_gL"], n * 2 + c_ + 1)
                    pe.wait_ge(sem["e_lo"], n * 6 + 6 + s + 1)
                for h in range(2):
                    for l_, r_ in split3(egH, egL, wh[s], wl[s]):
                        last = mm(bank[4 + 2 * e + h][:, :], l_[:, c_, f * P:(f + 1) * P],
                                  r_[:, f * D + h * 512:f * D + (h + 1) * 512], start=False, stop=False)
                if f == 1:
                    inc(last, "e_used")

            def e_body(n, ea, eb):
                e_up(n, 0, ea)
                e_up(n, 1, ea)
                e_up(n, 2, eb)
                e_tr(n, 0)
                e_up(n, 3, eb)
                e_down(n, 0, ea, 0)
                e_tr(n, 1)
                e_down(n, 0, ea, 1)
                e_down(n, 1, eb, 0)
                e_down(n, 1, eb, 1)

            def y_open(e):
                for h in range(2):
                    for z in range(2):
                        mm(bank[4 + 2 * e + h][:, z * UC:(z + 1) * UC], zeros[:, 0:P], zeros[:, :], start=(z == 0), stop=False)

            def y_close(e):
                for h in range(2):
                    for z in range(2):
                        last = mm(bank[4 + 2 * e + h][:, z * UC:(z + 1) * UC], zeros[:, 0:P], zeros[:, :], start=False, stop=(z == 1))
                inc(last, "y_mm")

            def combine(it, e, h):
                pe.wait_ge(sem["y_lo"], it * 4 + 2 * e + h + 1)
                for q in range(2):
                    f = 4 * e + 2 * h + q
                    if f >= 2:
                        pe.wait_ge(sem["acc_done"], it * 8 + f - 1)
                    for kk in range(2):
                        k = 2 * q + kk
                        for n, y_ in enumerate((yH, yL)):
                            last = mm(bank[f % 2][:, kk * S:(kk + 1) * S], y_[:, h, k * P:(k + 1) * P], pickT[:, e, :],
                                      start=(n == 0), stop=(n == 1))
                    inc(last, "comb_mm")

            pe.wait_ge(sem["tokL"], 4)
            inc(mm(bank[2][:, 0:UC], zeros[:, 0:P], zeros[:, :], start=True, stop=True), "e_used", 6)
            gather(0, None)
            with pe.Fori(0, n_rounds) as r:
                with pe.Fori(0, NE // 2) as i:
                    it = r * (NE // 2) + i
                    y_open(0)
                    y_open(1)
                    with pe.Fori(0, NPAIR) as j:
                        e_body(it * BODIES + j, 0, 0)
                    e_body(it * BODIES + NPAIR, 0, 1)
                    y_close(0)
                    with pe.Fori(0, NPAIR) as j:
                        e_body(it * BODIES + NPAIR + 1 + j, 1, 1)
                    y_close(1)
                    for e in range(2):
                        for h in range(2):
                            combine(it, e, h)
                    gather(it + 1, it)
            sums(S, KD, ones)
            pe.wait_ge(sem["norm_step"], KD)
            for f in range(4):
                for k in range(4):
                    last = nc.tensor.transpose(bank[f][:, k * P:(k + 1) * P],
                                               xT[:, 1, (f % 2) * 4 + k, (f // 2) * P:(f // 2 + 1) * P], ident)
                inc(last, "fin_tr")


_INS = ["x", "c", "ctx", "c_ctx", "w_mod", "b_mod", "norm1_g", "norm2_g", "w_in", "w_out",
        "lru_conv_w", "lru_conv_b", "lru_wa", "lru_ba", "lru_wx", "lru_bx", "lru_lambda",
        "conf_dw_w", "conf_dw_b", "conf_ln_g", "conf_ln_b",
        "ffn_w1", "ffn_w3", "ffn_w2", "moe_router", "moe_w1", "moe_w3", "moe_w2", "final_g"]
GRID_W = 64


def position_table():
    quarter = D // 4
    omega = (1.0 / (10000.0 ** (np.arange(quarter, dtype=np.float32) / np.float32(quarter)))).astype(np.float32)

    def emb1d(n):
        ang = np.arange(n, dtype=np.float32)[:, None] * omega[None, :]
        return np.concatenate([np.sin(ang), np.cos(ang)], axis=-1)

    n_rows = S // GRID_W
    er = np.broadcast_to(emb1d(n_rows)[:, None, :], (n_rows, GRID_W, D // 2))
    ec = np.broadcast_to(emb1d(GRID_W)[None, :, :], (n_rows, GRID_W, D // 2))
    return np.ascontiguousarray(np.concatenate([er, ec], axis=-1).reshape(S, D).T.astype(np.float32))


def shape_constants():
    k = np.zeros((P, K_W), np.float32)
    k[:, K_ID:K_ID + P] = np.eye(P)
    k[:, K_UP:K_UP + P] = np.triu(np.ones((P, P)), 1)
    k[:, K_ONE:K_ONE + P] = 1.0
    k[:, K_IOTA:K_IOTA + CAP] = np.arange(CAP)
    k[:, K_IOTA8:K_IOTA8 + NE] = np.arange(NE)
    for r in range(4):
        k[r, K_COMB + r % 2] = 1.0
    return k


def kernel(**inputs):
    import concourse.bacc as _bacc
    from concourse.bass_utils import run_bass_kernel_spmd as _run

    nc = _bacc.Bacc("TRN2", target_bir_lowering=False, num_devices=1)
    host = {name: np.ascontiguousarray(inputs[name]) for name in _INS}
    host["pos_t"] = position_table()
    host["consts"] = shape_constants()
    arrays, args = {}, []
    for name, a in host.items():
        arrays[f"in_{name}"] = a
        args.append(nc.dram_tensor(f"in_{name}", a.shape, mybir.dt.from_np(a.dtype), kind="ExternalInput").ap())
    args.append(nc.dram_tensor("out_0", (1, S, D), F32, kind="ExternalOutput").ap())
    dit_kernel(nc, *args)
    r = _run(nc, [arrays], core_ids=[0])
    return r.results[0]["out_0"]
```

```python
import numpy as np
import concourse.bass as bass
from concourse import mybir
from concourse.alu_op_type import AluOpType as ALU

F32 = mybir.dt.float32
F32R = mybir.dt.float32r
I32 = mybir.dt.int32
U32 = mybir.dt.uint32
ACT = mybir.ActivationFunctionType
AX = mybir.AxisListType

P = 128
D = 1024
KD = D // P
S = 256
C = 256
T = S + C
DL = 512
KL = DL // P
NH, DH = 8, 64
TAPS, PAD = 31, 15
RTAPS, RPL, RPR = 4, 2, 1
LRU_C = 8.0
DIN = 4 * DL
DFF = 2816
NE = 8
NMOD = 6
DEPTH = 2
EPS = 1e-6
UC = 256
UW = KD * UC
CAP = 128
FAR = 1000.0
GW = 2 * PAD + C
RW = RPL + RPR + C

K_ID, K_UP, K_ONE, K_IOTA, K_IOTA8, K_COMB, K_W = 0, 128, 256, 384, 512, 520, 522
R_BMOD, R_N1, R_N2, R_CW, R_CB, R_BA, R_BX, R_LAM, R_DWB, R_LNG, R_LNB, R_END = (
    0, 48, 56, 64, 80, 84, 92, 100, 108, 112, 116, 120)
R_C, R_CC, R_FG, R_MEND = 0, 8, 16, 24

WIN_COLS = [1536, 1792, 1024, 1280, 0, 256, 512, 768]
FFN_GROUPS = [4, 4, 3]
NCH = DFF // UC
EUNITS = 3 * NCH
MORE = (2 * S - 1) // (CAP + 1)
ITEMS = NE + MORE
CREDIT = 9


def weight_units():
    units = [("ad", 0, q) for q in range(8)]
    for i in range(8):
        units += [("win", 0, i), ("ad", 0, 8 + 2 * i), ("ad", 0, 9 + 2 * i)]
    units += [("wout", 0, i) for i in range(4)]
    ffn, j = [], 0
    for g, n in enumerate(FFN_GROUPS):
        for _ in range(n):
            ffn += [("f1", g, j), ("f3", g, j)]
            j += 1
        ffn += [("f2", g, i) for i in range(4)]
    for n, unit in enumerate(ffn):
        units.append(unit)
        if n < 24:
            units.append(("ad", 1, n))
    units += [("win", 1, i) for i in range(8)]
    units += [("wout", 1, i) for i in range(4)]
    return units


UNITS = weight_units()


def order(kind, j):
    if kind == "w2":
        return min(3 * j + 4, EUNITS - 1)
    return (0 if j == 0 else 3 * j - 1) + (kind == "w3")


def before(kind, j):
    return order(kind, j - 2) if j >= 2 else order(kind, NCH - (1 if j == 0 else 2)) - EUNITS


def slot(kind, j):
    return ("w1", "w3", "w2").index(kind) + 3 * (j % 2)


def uses(j):
    return (NCH + 1) // 2 if j % 2 == 0 else NCH // 2
RING = 3
RING2 = 6
MM_BANKS = 4


def dit_kernel(nc, x, c, ctx, c_ctx, w_mod, b_mod, norm1_g, norm2_g, w_in, w_out,
               lru_conv_w, lru_conv_b, lru_wa, lru_ba, lru_wx, lru_bx, lru_lambda,
               conf_dw_w, conf_dw_b, conf_ln_g, conf_ln_b,
               ffn_w1, ffn_w3, ffn_w2, moe_router, moe_w1, moe_w3, moe_w2, final_g,
               pos_t, consts, out):
    tokens_in = x
    place = {"at": 16512}

    def sb(name, shape, dt=F32, at=None):
        size = int(np.prod(shape[1:])) * 4
        size = (size + 31) // 32 * 32
        off = place["at"] if at is None else at
        if at is None:
            place["at"] += size
        assert off + size <= 229368, (name, off + size)
        t = nc.alloc_sbuf_tensor_at(name, [P] + list(shape[1:]), dt, offset=off)
        return t, off, off + size

    K, _, _ = sb("shape_consts", [P, K_W])
    eps, _, _ = sb("eps", [P, 1])
    fg, _, _ = sb("final_g_t", [P, KD])
    mt = [sb(f"mod_t{l}", [P, NMOD * KD, 2])[0] for l in range(DEPTH)]
    amp, _, _ = sb("norm_scale", [P, KD, 2])
    n_items_t, _, _ = sb("n_items", [P, 1], I32)
    item_e, _, _ = sb("item_expert", [P, ITEMS + 1], I32)
    rt, _, _ = sb("router", [P, KD, NE])
    spn, _, _ = sb("decay_rate", [P, DEPTH, 2, 8])
    sp_t, _, _ = sb("softplus_tmp", [P, 4, 8])
    zeros, _, _ = sb("zeros", [P, UC], F32R)
    xT, xT_at, _ = sb("x_t", [P, 2, KD, C])
    raw = [sb(f"raw{s}", [P, UW])[0] for s in range(RING)]
    wh = [sb(f"w_hi{s}", [P, UW], F32R)[0] for s in range(RING)]
    wl = [sb(f"w_lo{s}", [P, UW], F32R)[0] for s in range(RING)]
    scratch = place["at"]
    gate_r, nb_at, _ = sb("decay_a", [P, 2, T])
    root, _, _ = sb("root", [P, 2, T])
    h32, _, _ = sb("h32", [P, 2, T])
    sq, _, _ = sb("squares", [P, 2, T], at=nb_at)
    rstd, _, _ = sb("rstd", [P, T], at=nb_at + 4096)
    norm_t, _, _ = sb("norm_tmp", [P, T], at=nb_at + 6144)
    par, _, par_end = sb("params_t", [P, 2 * DEPTH + 1, P])
    mrow, _, _ = sb("mod_rows", [P, 2, UC])
    smat, _, _ = sb("silu_c_cols", [P, KD, P], F32R)
    sv, _, _ = sb("silu_c", [P, 2 * KD])
    experts_at = place["at"]
    hH, hH_at, _ = sb("h_hi", [P, KD, T], F32R)
    hL, _, _ = sb("h_lo", [P, KD, T], F32R)
    bdw, _, _ = sb("block_diag", [P, KL, 2, 2, P])
    mix_at = place["at"]
    glu, _, _ = sb("glu_pad", [P, KL, 2, GW])
    cv, _, _ = sb("conv_out", [P, KL, 2, C])
    rpad, rpad_at, _ = sb("rec_pad", [P, KL, 2, RW])
    rc, _, _ = sb("rec_conv", [P, KL, T])
    gg, _, _ = sb("gelu_gate", [P, KL, T])
    yy, _, _ = sb("scan_sum", [P, KL, T])
    rg, _, _ = sb("rec_gate", [P, 2, T], at=rpad_at)
    ig, _, _ = sb("in_gate", [P, 2, T], at=rpad_at + 4096)
    assert 2 * RW * KL * 4 >= 8192
    gH, _, e_ = sb("g_hi", [P, KD, T], F32R, at=mix_at)
    gL, _, e_ = sb("g_lo", [P, KD, T], F32R, at=e_)
    sg, _, e_ = sb("silu_out", [P, 4, T], at=e_)
    gt, _, e_ = sb("g_prod", [P, 2, T], at=nb_at)
    prow, _, e_ = sb("param_rows", [P, 2 * DEPTH + 1, P], at=mix_at)
    xrow, _, e_ = sb("x_rows", [P, 4, D], at=e_)
    pos, _, e_ = sb("pos_t", [P, KD, S], at=e_)
    esg, _, e_ = sb("e_silu", [P, UC], at=scratch)
    egH, _, e_ = sb("e_g_hi", [P, UC], F32R, at=e_)
    egL, _, e_ = sb("e_g_lo", [P, UC], F32R, at=e_)
    yH, _, e_ = sb("y_hi", [P, 2, 512], F32R, at=e_)
    yL, _, e_ = sb("y_lo", [P, 2, 512], F32R, at=e_)
    e_ = max(e_, par_end)
    pick, _, e_ = sb("pick", [P, 2, CAP], F32R, at=e_)
    pickT, _, e_ = sb("pick_t", [P, S], F32R, at=e_)
    tab, _, e_ = sb("slot_table", [P, 2, 2, ITEMS + 1], at=e_)
    cur, _, e_ = sb("slot_now", [P, 2, 2, 1], at=e_)
    cs, _, e_ = sb("slot_weight", [P, 1], at=e_)
    assert e_ >= par_end
    for s in range(RING, RING2):
        t, _, e_ = sb(f"raw{s}", [P, UW], at=e_)
        raw.append(t)
        t, _, e_ = sb(f"w_hi{s}", [P, UW], F32R, at=e_)
        wh.append(t)
        t, _, e_ = sb(f"w_lo{s}", [P, UW], F32R, at=e_)
        wl.append(t)
    ftH, _, _ = sb("f_tok_hi", [P, 2, D], F32R, at=xT_at)
    orow, _, _ = sb("out_rows", [P, 2, D], at=e_)
    ftL, _, e_ = sb("f_tok_lo", [P, 2, D], F32R, at=e_)
    xe_at = e_
    xeH, _, e_ = sb("xe_hi", [P, KD, CAP], F32R, at=e_)
    xeL, _, e_ = sb("xe_lo", [P, KD, CAP], F32R, at=e_)
    fT, _, e3 = sb("f_t", [P, KD, S], at=xe_at)
    lg, _, e3 = sb("logits", [P, 2, NE], at=e3)
    pr, _, e3 = sb("probs", [P, 2, NE], at=e3)
    top, _, e3 = sb("top8", [P, 2, 8], at=e3)
    tix, _, e3 = sb("top8_index", [P, 2, 8], U32, at=e3)
    tif, _, e3 = sb("top8_index_f", [P, 2, 8], at=e3)
    oh, _, e3 = sb("one_hots", [P, 2, 2, NE], at=e3)
    mask, _, e3 = sb("mask", [P, 2, NE], at=e3)
    col, _, e3 = sb("route_cols", [P, 2, 8], at=e3)
    over, _, e3 = sb("overflow", [P, 2, NE], at=e3)
    sel, _, e3 = sb("selected", [P, 2, NE], at=e3)
    onesf, _, e3 = sb("ones8", [P, NE], at=e3)
    item_f, _, e3 = sb("item_expert_f", [P, ITEMS + 1], at=e3)
    num_f, _, e3 = sb("n_items_f", [P, 1], at=e3)
    assert e3 <= 229368

    bank = [nc.alloc_psum_tensor(f"bank{b}", [P, 512], F32) for b in range(8)]
    B_H, B_T, B_Y, B_G, B_C = 0, 2, 3, 5, 7
    B_ROW, B_MT, B_ST = 4, 6, 7

    names = """consts_in params_in x_in bd_in x_out params_t x_tr x_ready params_ready silu_ready cols_ready
        memset_done hi_done lo_done row_out mt_mm mod_ready decay_done decay_exp
        sq_done sum_mm root_done norm_step h32_done hH_done hL_done
        mm_done gates_done glu_done rec_done gelu_done rconv_done conv_step
        bd_mm sig_done act_step dve_step ig_done root_in scan_done lru_done ln_mm ln_step ln_act
        res_done silu_out g_prod gH_done gL_done fT_done
        router_in logits_mm route_step route_exp pos_mm items_done tok_tr tokH tokL
        e_hi e_lo e_used e_silu e_prod g_tr e_gH e_gL y_mm y_hi y_lo comb_mm acc_done
        pick_done gather_mm pick_mm pickT_done cs_done xe_hi xe_lo fin_tr fin_out pad_zero bd_zero""".split()
    sem = {n: nc.alloc_semaphore(n) for n in names}
    unit_full = [nc.alloc_semaphore(f"unit_full{s}") for s in range(RING)]
    e_full = [nc.alloc_semaphore(f"e_full{s}") for s in range(RING2)]

    def inc(ins, name, n=1):
        return ins.then_inc(sem[name], n)

    def split3(hi_l, lo_l, hi_r, lo_r):
        return ((hi_l, hi_r), (hi_l, lo_r), (lo_l, hi_r))

    def layer_par(l, row, n=1):
        return par[:, 2 * l, row:row + n]

    def tap(l, t, c_):
        return par[:, 2 * l + 1, t * KL + c_:t * KL + c_ + 1]

    def side(l, kind):
        return 0 if l == 0 or kind == "rec" else 1

    def cols(full):
        return slice(0, T) if full == 0 else slice(C, T)

    NU = len(UNITS)

    def win_kind(i):
        return ("gates", "values", "rec", "gelu")[i // 2]

    MM, USED, n = {}, [], 0
    for kind, a, i in UNITS:
        for h in range(1 if kind == "ad" else 2):
            n += 1
            MM[(kind, a, i if kind == "ad" else 2 * i + h)] = n
        USED.append(n)
    AT = {unit: u for u, unit in enumerate(UNITS)}
    RES = {("wout", 0): 0, ("f2", 0): KD, ("f2", 1): 2 * KD, ("f2", 2): 3 * KD, ("wout", 1): 4 * KD,
           (0, 2): KD, (1, 1): 4 * KD, (1, 2): 5 * KD}
    HL = {("norm", 0, 1): KD, ("mix", 0): 2 * KD, ("norm", 0, 2): 3 * KD, ("norm", 1, 1): 4 * KD, ("mix", 1): 5 * KD}
    ROOT = {(0, 1): 1, ("mix", 0): 1, ("ln", 0): 2 + 2 * KL, (0, 2): 3 + 2 * KL, (1, 1): 4 + 2 * KL, ("mix", 1): 4 + 2 * KL,
            ("ln", 1): 5 + 4 * KL, (1, 2): 6 + 4 * KL, "final": 7 + 4 * KL}
    LN_STEPS = 2 * KL + 1
    DECAY_ALL = 3 * DEPTH
    ROUTE_MASKS = 7 + 12 * 2
    ROUTE_ALL = ROUTE_MASKS + 2 * 2 + 5 + MORE * (3 + 5 * 2) + 1

    def unit_src(kind, a, i):
        if kind == "ad":
            return w_mod[a, :, i * UC:(i + 1) * UC].rearrange("(k p) n -> p k n", p=P)
        if kind == "win":
            return w_in[a, :, WIN_COLS[i]:WIN_COLS[i] + UC].rearrange("(k p) n -> p k n", p=P)
        if kind == "wout":
            return w_out[a, :, i * UC:(i + 1) * UC].rearrange("(k p) n -> p k n", p=P)
        if kind in ("f1", "f3"):
            w = ffn_w1 if kind == "f1" else ffn_w3
            return w[0, :, i * UC:(i + 1) * UC].rearrange("(k p) n -> p k n", p=P)
        r0 = sum(FFN_GROUPS[:a]) * UC
        r1 = r0 + FFN_GROUPS[a] * UC
        return ffn_w2[0, r0:r1, i * UC:(i + 1) * UC].rearrange("(k p) n -> p k n", p=P)

    def unit_k(kind, a):
        return 2 * FFN_GROUPS[a] if kind == "f2" else KD

    PARAM_DMAS = 11 * DEPTH + DEPTH + 3
    ROW_PARTS = [(2 * l, R_END) for l in range(DEPTH)] + [(2 * l + 1, TAPS * KL) for l in range(DEPTH)] + [(4, R_MEND)]

    block = nc.Block()
    with block:
        @block.sync
        def _(sp):
            inc(sp.dma_start(K[:, :], consts), "consts_in", 16)
            inc(sp.dma_start(rt[:, :, :], moe_router[0].rearrange("(k p) e -> p k e", p=P)), "router_in", 16)
            for u, (kind, a, i) in enumerate(UNITS):
                if u >= RING:
                    sp.wait_ge(sem["lo_done"], u - RING + 1)
                nk = unit_k(kind, a)
                sp.dma_start(raw[u % RING][:, 0:nk * UC].rearrange("p (k n) -> p k n", n=UC),
                             unit_src(kind, a, i)).then_inc(unit_full[u % RING], 16)

            def load(x, t, kind, j, e):
                s = slot(kind, j)
                sp.wait_ge(sem["e_lo"], x * EUNITS + t * 6 + before(kind, j) + 1 + CREDIT)
                f = bass.ds(t * (2 * UC) + j * UC, UC)
                w = {"w1": moe_w1, "w3": moe_w3, "w2": moe_w2}[kind]
                if kind == "w2":
                    src = w[0, bass.ds(e, 1), f, :].rearrange("a (k p) n -> p (a k) n", p=P)
                    dst = raw[s][:, :].rearrange("p (k n) -> p k n", k=2)
                else:
                    src = w[0, bass.ds(e, 1), :, f].rearrange("a (k p) n -> p (a k) n", p=P)
                    dst = raw[s][:, :].rearrange("p (k n) -> p k n", k=KD)
                sp.dma_start(dst, src).then_inc(e_full[s], 16)

            def load_step(x, t, j, e):
                load(x, t, "w1", j, e)
                load(x, t, "w3", j, e)
                load(x, t, "w2", j - 1, e)

            def load_head(x, e):
                load(x, 0, "w1", 0, e)
                load(x, 0, "w3", 0, e)
                load_step(x, 0, 1, e)

            load_head(0, 0)
            sp.wait_ge(sem["items_done"], 2)
            n_items = sp.value_load(n_items_t[0:1, 0:1], min_val=NE, max_val=ITEMS)
            with sp.Fori(0, n_items) as x:
                e = sp.value_load(item_e[0:1, bass.ds(x, 1)], min_val=0, max_val=NE - 1)
                load_step(x, 0, 2, e)
                with sp.Fori(0, 4) as t:
                    load_step(x, t, 3, e)
                    load_step(x, t, 4, e)
                load(x, 0, "w2", NCH - 1, e)
                e_next = sp.value_load(item_e[0:1, bass.ds(x + 1, 1)], min_val=0, max_val=NE - 1)
                load_head(x + 1, e_next)
            for t in range(2):
                sp.wait_ge(sem["fin_out"], 2 * (t + 1))
                inc(sp.dma_start(out[0, t * P:(t + 1) * P, :], orow[:, t, :]), "x_out", 16)
            sp.wait_ge(sem["x_out"], 32)

        @block.gpsimd
        def _(pool):
            inc(nc.gpsimd.memset(zeros[:, :].bitcast(F32), 0.0), "memset_done")
            inc(nc.gpsimd.memset(smat[:, :, :].bitcast(F32), 0.0), "memset_done")
            inc(nc.gpsimd.memset(eps[:, :], EPS), "memset_done")
            inc(nc.gpsimd.memset(bdw[:, :, :, :, :], 0.0), "bd_zero")

            def load_block_diag(l):
                for kind, w in enumerate((lru_wa, lru_wx)):
                    for d in range(2):
                        for odd in range(2):
                            src = w[l, d, odd:NH:2, :, :].rearrange("c i j -> i c j")
                            dst = bdw[DH * odd:DH * (odd + 1), :, d, kind, DH * odd:DH * (odd + 1)]
                            inc(pool.dma_start(dst, src), "bd_in", 16)

            pool.wait_ge(sem["bd_zero"], 1)
            load_block_diag(0)

            counts = {"low": 0}

            def low(dst, hi, k):
                pool.wait_ge(sem["hH_done"], counts["low"] + 1)
                inc(nc.gpsimd.tensor_tensor(dst, h32[:, counts["low"] % 2, k], hi.bitcast(F32), ALU.subtract), "hL_done")
                counts["low"] += 1

            def norm_low(full):
                for k in range(KD):
                    low(hL[:, k, cols(full)], hH[:, k, cols(full)], cols(full))

            norm_low(0)
            for l in range(DEPTH):
                full = side(l, "x")
                for c_ in range(KL):
                    for d in range(2):
                        n = (l * KL + c_) * 2 + d
                        pool.wait_ge(sem["sig_done"], 4 * (l * KL + c_) + 4)
                        inc(nc.gpsimd.tensor_tensor(ig[:, d, :], ig[:, d, :], rc[:, c_, :], ALU.mult), "ig_done")
                    low(hL[:, c_, cols(full)], hH[:, c_, cols(full)], cols(full))
                if l == 0:
                    pool.wait_ge(sem["bd_mm"], 4 * KL)
                    load_block_diag(1)
                for c_ in range(KL):
                    low(hL[:, KL + c_, cols(full)], hH[:, KL + c_, cols(full)], cols(full))
                if l == 0:
                    norm_low(0)
                    for j in range(2 * sum(FFN_GROUPS)):
                        pool.wait_ge(sem["gH_done"], j + 1)
                        s = j % KD
                        inc(nc.gpsimd.tensor_tensor(gL[:, s, :], gt[:, j % 2, :], gH[:, s, :].bitcast(F32), ALU.subtract), "gL_done")
                    norm_low(0)

        @block.scalar
        def _(act):
            def copy(dst, src, scale=1.0):
                return nc.scalar.activation(dst, src, ACT.Copy, scale=scale)

            def rows(tile, at, src):
                n = src.shape[0]
                inc(act.dma_start(prow[at:at + n, tile, :], src), "params_in", 16)

            for t in range(2):
                inc(act.dma_start(xrow[:, t, :], ctx[0, t * P:(t + 1) * P, :]), "x_in", 16)
                inc(act.dma_start(xrow[:, 2 + t, :], tokens_in[0, t * P:(t + 1) * P, :]), "x_in", 16)
            rows(4, R_C, c.rearrange("a (r p) -> (a r) p", p=P))
            rows(4, R_CC, c_ctx.rearrange("(r p) -> r p", p=P))
            rows(4, R_FG, final_g.rearrange("(r p) -> r p", p=P))
            inc(act.dma_start(pos[:, :, :], pos_t.rearrange("(k p) n -> p k n", p=P)), "x_in", 16)
            for l in range(DEPTH):
                v = lambda w: w[l].rearrange("(r p) -> r p", p=P)
                m = lambda w: w[l].rearrange("t (r p) -> (t r) p", p=P)
                rows(2 * l, R_BMOD, v(b_mod))
                rows(2 * l, R_N1, v(norm1_g))
                rows(2 * l, R_N2, v(norm2_g))
                rows(2 * l, R_CW, m(lru_conv_w))
                rows(2 * l, R_CB, v(lru_conv_b))
                rows(2 * l, R_BA, m(lru_ba))
                rows(2 * l, R_BX, m(lru_bx))
                rows(2 * l, R_LAM, m(lru_lambda))
                rows(2 * l, R_DWB, v(conf_dw_b))
                rows(2 * l, R_LNG, v(conf_ln_g))
                rows(2 * l, R_LNB, v(conf_ln_b))
                rows(2 * l + 1, 0, m(conf_dw_w))

            act.wait_ge(sem["params_ready"], 5)
            inc(nc.scalar.activation(sv[:, :], par[:, 4, R_C:R_CC + KD], ACT.Silu), "silu_ready")
            act.wait_ge(sem["silu_ready"], 1)
            act.wait_ge(sem["memset_done"], 3)
            for v_ in range(2):
                inc(copy(smat[:, :, v_], sv[:, v_ * KD:(v_ + 1) * KD]), "cols_ready")
            for l in range(DEPTH):
                inc(nc.scalar.activation(sp_t[:, l, :], layer_par(l, R_LAM, 8), ACT.Abs), "decay_done")
            act.wait_ge(sem["decay_done"], 2)
            for l in range(DEPTH):
                inc(nc.scalar.activation(sp_t[:, 2 + l, :], sp_t[:, l, :], ACT.Exp, scale=-1.0), "decay_exp")

            def hi(u):
                kind, a, _ = UNITS[u]
                n = unit_k(kind, a) * UC
                act.wait_ge(unit_full[u % RING], 16 * (u // RING + 1))
                if u >= RING:
                    act.wait_ge(sem["mm_done"], USED[u - RING])
                inc(copy(wh[u % RING][:, 0:n], raw[u % RING][:, 0:n]), "hi_done")

            cnt = dict(row=0, sq=0, sum=0, h32=0, mm=0, ln=0, gp=0)

            def squares(srcs):
                for src, n in srcs:
                    s = cnt["sq"]
                    if s >= 2:
                        act.wait_ge(sem["sum_mm"], s - 1)
                    inc(nc.scalar.activation(sq[:, s % 2, 0:n], src, ACT.Square), "sq_done")
                    cnt["sq"] += 1

            def round_h(dst, n_sel):
                act.wait_ge(sem["h32_done"], cnt["h32"] + 1)
                inc(copy(dst, h32[:, cnt["h32"] % 2, n_sel]), "hH_done")
                cnt["h32"] += 1

            def norm(l, which, full):
                n = T if full == 0 else C
                if l == 0 and which == 1:
                    act.wait_ge(sem["x_ready"], KD * 2)
                else:
                    act.wait_ge(sem["res_done"], RES[(l, which)])
                squares([(xT[:, :, k, :] if full == 0 else xT[:, 1, k, :], n) for k in range(KD)])
                act.wait_ge(sem["sum_mm"], cnt["sq"])
                r_ = rstd[:, 0:n]
                inc(nc.scalar.activation(r_, bank[B_ST][:, 0:n], ACT.Sqrt, scale=1.0 / D, bias=eps[:, 0:1]), "root_done")
                if (l, which) != (1, 2):
                    for k in range(KD):
                        round_h(hH[:, k, cols(full)], cols(full))

            def row_out(l, q):
                n = l * 24 + q
                act.wait_ge(sem["mm_done"], MM[("ad", l, q)])
                if n >= 2:
                    act.wait_ge(sem["mt_mm"], n - 1)
                inc(copy(mrow[0:4, n % 2, :], bank[B_ROW + n % 2][0:4, 0:UC]), "row_out")

            def mix(l):
                full = side(l, "x")
                n = cols(full)
                for c_ in range(KL):
                    g_ = l * KL + c_
                    act.wait_ge(sem["decay_done"], DECAY_ALL)
                    act.wait_ge(sem["rconv_done"], RTAPS * KL * (l + 1))
                    for kd in range(2):
                        for d in range(2):
                            act.wait_ge(sem["bd_mm"], 4 * g_ + 2 * kd + d + 1)
                            if kd == 0 and d == 0 and g_ > 0:
                                act.wait_ge(sem["scan_done"], 2 * g_)
                            dst = (rg, ig)[kd][:, d, :]
                            b_ = layer_par(l, (R_BA, R_BX)[kd] + d * KL + c_)
                            inc(nc.scalar.activation(dst, bank[2 * kd + d][:, :], ACT.Sigmoid, bias=b_), "sig_done")
                    act.wait_ge(sem["sig_done"], 4 * g_ + 4)
                    for d in range(2):
                        inc(nc.scalar.activation(gate_r[:, d, :], rg[:, d, :], ACT.Exp,
                                                 scale=spn[:, l, 0, d * KL + c_:d * KL + c_ + 1]), "act_step")
                    act.wait_ge(sem["act_step"], 6 * g_ + 2)
                    for d in range(2):
                        inc(nc.scalar.activation(rg[:, d, :], rg[:, d, :], ACT.Tanh,
                                                 scale=spn[:, l, 1, d * KL + c_:d * KL + c_ + 1]), "act_step")
                    for d in range(2):
                        inc(nc.scalar.activation(root[:, d, :], gate_r[:, d, :], ACT.Square), "act_step")
                    for d in range(2):
                        act.wait_ge(sem["root_in"], 2 * g_ + d + 1)
                        inc(nc.scalar.activation(root[:, d, :], root[:, d, :], ACT.Sqrt), "root_done")
                    round_h(hH[:, c_, n], n)
                w = T if full == 0 else C
                act.wait_ge(sem["ln_step"], LN_STEPS * l + KL)
                squares([((cv[:, c_, :, :] if full == 0 else cv[:, c_, 1, :]), w) for c_ in range(KL)])
                act.wait_ge(sem["sum_mm"], cnt["sq"])
                inc(nc.scalar.activation(rstd[:, 0:w], bank[B_ST][:, 0:w], ACT.Sqrt, scale=1.0 / DL, bias=eps[:, 0:1]), "root_done")
                for c_ in range(KL):
                    act.wait_ge(sem["ln_step"], LN_STEPS * l + KL + 1 + c_ + 1)
                    k = cnt["h32"]
                    act.wait_ge(sem["hL_done"], k - 1)
                    src = cv[:, c_, :, :] if full == 0 else cv[:, c_, 1, :]
                    inc(nc.scalar.activation(h32[:, k % 2, n], src, ACT.Silu, scale=layer_par(l, R_LNG + c_),
                                             bias=layer_par(l, R_LNB + c_)), "h32_done")
                    round_h(hH[:, KL + c_, n], n)

            hi(0)
            hi(1)
            for u, (kind, a, i) in enumerate(UNITS):
                if u + 2 < NU:
                    hi(u + 2)
                if kind == "win" and i == 0:
                    norm(a, 1, 0)
                if kind == "wout" and i == 0:
                    mix(a)
                if kind == "f1" and i == 0:
                    norm(0, 2, 0)
                if kind == "ad":
                    row_out(a, i)
                if kind == "win" and win_kind(i) != "values":
                    full = side(a, "rec" if win_kind(i) == "rec" else "x")
                    n = T if full == 0 else C
                    for h in range(2):
                        t = 2 * i + h
                        c_ = t % KL
                        act.wait_ge(sem["mm_done"], MM[("win", a, t)])
                        b_ = bank[t % MM_BANKS][:, 0:n]
                        if win_kind(i) == "gates":
                            dst = cv[:, c_, :, :] if full == 0 else cv[:, c_, 1, :]
                            inc(nc.scalar.activation(dst, b_, ACT.Sigmoid), "gates_done")
                        elif win_kind(i) == "rec":
                            inc(copy(rpad[:, c_, :, RPL:RPL + C], b_.rearrange("p (s n) -> p s n", s=2)), "rec_done")
                        else:
                            inc(nc.scalar.activation(gg[:, c_, cols(full)], b_, ACT.Gelu_apprx_tanh), "gelu_done")
                if kind == "f3":
                    for h in range(2):
                        j = 2 * i + h
                        act.wait_ge(sem["mm_done"], MM[("f1", a if kind == "f3" else 0, j)])
                        if j >= 4:
                            act.wait_ge(sem["g_prod"], j - 3)
                        inc(nc.scalar.activation(sg[:, j % 4, :], bank[h][:, :], ACT.Silu), "silu_out")
                    for h in range(2):
                        j = 2 * i + h
                        act.wait_ge(sem["g_prod"], j + 1)
                        if j % KD == 0 and j:
                            act.wait_ge(sem["mm_done"], MM[("f2", j // KD - 1, 7)])
                        inc(copy(gH[:, j % KD, :], gt[:, j % 2, :]), "gH_done")

            norm(1, 2, 1)
            for t in range(2):
                act.wait_ge(sem["route_step"], 4)
                inc(nc.scalar.activation(pr[:, t, :], lg[:, t, :], ACT.Exp, bias=col[:, t, 0:1]), "route_exp")
            for f in range(4):
                act.wait_ge(sem["tok_tr"], f + 1)
                inc(copy(ftH[:, f // 2, (f % 2) * 512:(f % 2 + 1) * 512], bank[2 + f][:, :]), "tokH")

            def gather_out(g):
                for q in range(2):
                    act.wait_ge(sem["gather_mm"], g * 2 + q + 1)
                    inc(copy(xeH[:, 4 * q:4 * q + 4, :], bank[B_G + q][:, :].rearrange("p (k n) -> p k n", k=4)), "xe_hi")

            def e_hi(x, t, kind, j):
                s = slot(kind, j)
                act.wait_ge(e_full[s], (x * uses(j) + t + (j // 2 + 1)) * 16)
                act.wait_ge(sem["e_used"], x * EUNITS + t * 6 + before(kind, j) + 1 + CREDIT)
                inc(copy(wh[s][:, :], raw[s][:, :]), "e_hi")

            def e_silu(x, t, j):
                act.wait_ge(sem["e_used"], x * EUNITS + t * 6 + order("w3", j) + 1 + CREDIT)
                inc(nc.scalar.activation(esg[:, :], bank[B_H + j % 2][:, 0:UC], ACT.Silu), "e_silu")

            def e_gh(x, t, j):
                act.wait_ge(sem["g_tr"], x * NCH + t * 2 + j + 1)
                inc(copy(egH[:, :], bank[B_T][:, 0:UC]), "e_gH")

            def e_step(x, t, j):
                if j < NCH - 1:
                    e_hi(x, t, "w1", j + 1)
                if j == 0:
                    for h in range(2):
                        act.wait_ge(sem["e_used"], x * EUNITS + CREDIT)
                        inc(copy(yH[:, h, :], bank[B_Y + h][:, :], scale=cs[:, 0:1]), "y_hi")
                else:
                    e_gh(x, t, j - 1)
                if j < NCH - 1:
                    e_hi(x, t, "w3", j + 1)
                e_silu(x, t, j)
                e_hi(x, t, "w2", j)

            act.wait_ge(sem["items_done"], 2)
            n_items = act.value_load(n_items_t[0:1, 0:1], min_val=NE, max_val=ITEMS)
            act.wait_ge(sem["acc_done"], 4)
            gather_out(0)
            e_hi(0, 0, "w1", 0)
            e_hi(0, 0, "w3", 0)
            with act.Fori(0, n_items) as x:
                e_step(x, 0, 0)
                e_step(x, 0, 1)
                e_step(x, 0, 2)
                act.wait_ge(sem["pick_mm"], x * 2 + 1)
                inc(copy(pickT[:, :], bank[B_G][:, 0:S]), "pickT_done")
                with act.Fori(0, 3) as t:
                    e_step(x, t, 3)
                    e_step(x, t, 4)
                e_step(x, 0, NCH - 2)
                e_step(x, 0, NCH - 1)
                e_gh(x, 0, NCH - 1)
                e_hi(x + 1, 0, "w1", 0)
                gather_out(x + 1)
                e_hi(x + 1, 0, "w3", 0)
            for h in range(2):
                act.wait_ge(sem["e_used"], n_items * EUNITS + CREDIT)
                inc(copy(yH[:, h, :], bank[B_Y + h][:, :], scale=cs[:, 0:1]), "y_hi")
            act.wait_ge(sem["acc_done"], n_items * 8 + 4 + 8)
            squares([(xT[:, 1, k, :], S) for k in range(KD)])
            act.wait_ge(sem["sum_mm"], cnt["sq"])
            inc(nc.scalar.activation(rstd[:, 0:S], bank[B_ST][:, 0:S], ACT.Sqrt, scale=1.0 / D, bias=eps[:, 0:1]), "root_done")
            for t in range(2):
                for h in range(2):
                    f = 2 * t + h
                    act.wait_ge(sem["fin_tr"], f + 1)
                    inc(copy(orow[:, t, h * 512:(h + 1) * 512], bank[f][:, :]), "fin_out")

        @block.vector
        def _(dve):
            V = nc.vector
            state = dict(step=0, h32=0, cv=0, rs=0)

            def step(ins):
                inc(ins, "dve_step")
                state["step"] += 1
                dve.wait_ge(sem["dve_step"], state["step"])

            for k in range(KD):
                dve.wait_ge(sem["x_tr"], k + 1)
                if k == 0:
                    dve.wait_ge(sem["x_in"], 16 * 5)
                b_ = bank[k % 4]
                inc(V.tensor_copy(xT[:, 0, k, :], b_[:, 0:C]), "x_ready")
                inc(V.tensor_tensor(xT[:, 1, k, :], b_[:, C:T], pos[:, k, :], ALU.add), "x_ready")
            for n, (tile, rows_) in enumerate(ROW_PARTS):
                dve.wait_ge(sem["params_t"], n + 1)
                inc(V.tensor_copy(par[:, tile, 0:rows_], bank[4 + n % 4][:, 0:rows_]), "params_ready")
            dve.wait_ge(sem["params_ready"], 5)
            dve.wait_ge(sem["silu_ready"], 1)
            dve.wait_ge(sem["cols_ready"], 2)
            for v_ in range(2):
                inc(V.tensor_tensor(smat[:, :, 2 + v_], sv[:, v_ * KD:(v_ + 1) * KD],
                                    smat[:, :, v_].bitcast(F32), ALU.subtract), "cols_ready")
            inc(V.tensor_copy(fg[:, :], par[:, 4, R_FG:R_FG + KD]), "cols_ready")
            for l in range(DEPTH):
                dve.wait_ge(sem["decay_exp"], l + 1)
                z, z2, p_ = sp_t[:, l, :], spn[:, l, 0, :], spn[:, l, 1, :]
                v_ = sp_t[:, 2 + l, :]
                step(V.tensor_scalar(z, v_, 2.0, None, ALU.add))
                step(V.reciprocal(z, z))
                step(V.tensor_tensor(z, z, v_, ALU.mult))
                step(V.tensor_tensor(z2, z, z, ALU.mult))
                step(V.tensor_scalar(p_, z2, 1.0 / 17, 1.0 / 15, ALU.mult, ALU.add))
                for o in (13, 11, 9, 7, 5, 3, 1):
                    step(V.tensor_tensor(p_, p_, z2, ALU.mult))
                    step(V.tensor_scalar(p_, p_, 1.0 / o, None, ALU.add))
                step(V.tensor_tensor(p_, p_, z, ALU.mult))
                step(V.tensor_scalar(z, layer_par(l, R_LAM, 8), -1.0, 0.0, ALU.mult, ALU.max))
                step(V.scalar_tensor_tensor(z, p_, 2.0, z, ALU.mult, ALU.add))
                inc(V.tensor_scalar(spn[:, l, 0, :], z, -LRU_C, None, ALU.mult), "decay_done")
                inc(V.tensor_scalar(spn[:, l, 1, :], z, LRU_C, None, ALU.mult), "decay_done")

            def lo(u):
                kind, a, _ = UNITS[u]
                n = unit_k(kind, a) * UC
                s = u % RING
                dve.wait_ge(sem["hi_done"], u + 1)
                inc(V.tensor_tensor(wl[s][:, 0:n], raw[s][:, 0:n], wh[s][:, 0:n].bitcast(F32), ALU.subtract), "lo_done")

            def mods(l, part):
                a, b = ((0, 2 * KD), (2 * KD, NMOD * KD), (0, NMOD * KD))[part]
                dve.wait_ge(sem["mt_mm"], 24 * l + (8 if part == 0 else 24))
                ps = bank[B_MT][:, 0:2 * NMOD * KD].rearrange("p (m v) -> p m v", v=2)
                for v_ in range(2):
                    inc(V.tensor_tensor(mt[l][:, a:b, v_], ps[:, a:b, v_], layer_par(l, R_BMOD + a, b - a), ALU.add), "mod_ready")

            def norm(l, which, full):
                n = T if full == 0 else C
                sh, sc = (0, KD) if which == 1 else (3 * KD, 4 * KD)
                g_ = layer_par(l, R_N1 if which == 1 else R_N2, KD)
                if which == 1:
                    if l == 0:
                        mods(0, 0)
                    dve.wait_ge(sem["mod_ready"], 4 * l + 2)
                else:
                    dve.wait_ge(sem["mod_ready"], 4 + 2 * l)
                for v_ in range(2):
                    step(V.scalar_tensor_tensor(amp[:, :, v_], mt[l][:, sc:sc + KD, v_], 1.0, g_, ALU.add, ALU.mult))
                state["rs"] += 1
                dve.wait_ge(sem["root_done"], ROOT[(l, which)])
                step(V.reciprocal(rstd[:, 0:n], rstd[:, 0:n]))
                for k in range(KD):
                    src = xT[:, :, k, :] if full == 0 else xT[:, 1, k, :]
                    r_ = rstd[:, 0:n].rearrange("p (s n) -> p s n", s=2) if full == 0 else rstd[:, 0:n]
                    t_ = norm_t[:, 0:n].rearrange("p (s n) -> p s n", s=2) if full == 0 else norm_t[:, 0:n]
                    if k:
                        dve.wait_ge(sem["fT_done" if (l, which) == (1, 2) else "h32_done"], k if (l, which) == (1, 2) else state["h32"])
                    step(V.tensor_tensor(t_, src, r_, ALU.mult))
                    if (l, which) == (1, 2):
                        inc(V.tensor_scalar(fT[:, k, :], norm_t[:, 0:n], amp[:, k, 0:1], mt[l][:, sh + k, 0:1], ALU.mult, ALU.add), "fT_done")
                        continue
                    m_ = state["h32"]
                    if m_ >= 2:
                        dve.wait_ge(sem["hL_done"], m_ - 1)
                    if full == 0:
                        step(V.tensor_scalar(h32[:, m_ % 2, 0:C], norm_t[:, 0:C], amp[:, k, 1:2], mt[l][:, sh + k, 1:2], ALU.mult, ALU.add))
                        inc(V.tensor_scalar(h32[:, m_ % 2, C:T], norm_t[:, C:T], amp[:, k, 0:1], mt[l][:, sh + k, 0:1], ALU.mult, ALU.add), "h32_done")
                    state["h32"] += 1

            CONV = [(t, c_) for t in range(TAPS) for c_ in range(KL)]

            def conv(l, a, b):
                full = side(l, "x")
                for m_ in range(a, min(b, len(CONV))):
                    t, c_ = CONV[m_]
                    base = l * len(CONV)
                    g_ = glu[:, c_, :, t:t + C] if full == 0 else glu[:, c_, 1, t:t + C]
                    o_ = cv[:, c_, :, :] if full == 0 else cv[:, c_, 1, :]
                    if t == 0:
                        inc(V.tensor_scalar(o_, g_, tap(l, t, c_), layer_par(l, R_DWB + c_), ALU.mult, ALU.add), "conv_step")
                    else:
                        dve.wait_ge(sem["conv_step"], base + m_ - KL + 1)
                        inc(V.scalar_tensor_tensor(o_, g_, tap(l, t, c_), o_, ALU.mult, ALU.add), "conv_step")

            def mix(l, conv_at):
                full = side(l, "x")
                n = cols(full)
                dve.wait_ge(sem["rec_done"], KL * (l + 1))
                dve.wait_ge(sem["pad_zero"], 4 * (l + 1))
                for t in range(RTAPS):
                    for c_ in range(KL):
                        m_ = RTAPS * KL * l + t * KL + c_
                        src = rpad[:, c_, :, t:t + C]
                        dst = rc[:, c_, :].rearrange("p (s n) -> p s n", s=2)
                        w_ = layer_par(l, R_CW + t * KL + c_)
                        if t == 0:
                            inc(V.tensor_scalar(dst, src, w_, layer_par(l, R_CB + c_), ALU.mult, ALU.add), "rconv_done")
                        else:
                            dve.wait_ge(sem["rconv_done"], m_ - KL + 1)
                            inc(V.scalar_tensor_tensor(dst, src, w_, dst, ALU.mult, ALU.add), "rconv_done")
                per = (len(CONV) - conv_at + KL - 1) // KL
                for c_ in range(KL):
                    g_ = l * KL + c_
                    conv(l, conv_at + per * c_, conv_at + per * (c_ + 1))
                    for d in range(2):
                        dve.wait_ge(sem["act_step"], 6 * g_ + 6)
                        inc(V.scalar_tensor_tensor(root[:, d, :], root[:, d, :], 1.0, rg[:, d, :], ALU.add, ALU.mult), "root_in")
                    for d in range(2):
                        dve.wait_ge(sem["root_done"], ROOT[("mix", l)] + 2 * c_ + d + 1)
                        dve.wait_ge(sem["ig_done"], 2 * g_ + d + 1)
                        step(V.tensor_tensor(ig[:, d, :], ig[:, d, :], root[:, d, :], ALU.mult))
                    inc(V.tensor_tensor_scan(yy[:, c_, :], gate_r[:, 0, :], ig[:, 0, :], 0.0, ALU.mult, ALU.add), "scan_done")
                    step(V.tensor_tensor_scan(root[:, 1, 0:C][:, ::-1], gate_r[:, 1, 0:C][:, ::-1], ig[:, 1, 0:C][:, ::-1], 0.0, ALU.mult, ALU.add))
                    inc(V.tensor_tensor_scan(root[:, 1, C:T][:, ::-1], gate_r[:, 1, C:T][:, ::-1], ig[:, 1, C:T][:, ::-1], root[:, 1, 0:1], ALU.mult, ALU.add), "scan_done")
                    dve.wait_ge(sem["scan_done"], 2 * g_ + 2)
                    step(V.tensor_tensor(yy[:, c_, n], yy[:, c_, n], root[:, 1, n], ALU.add))
                    m_ = state["h32"]
                    if m_ >= 2:
                        dve.wait_ge(sem["hL_done"], m_ - 1)
                    dve.wait_ge(sem["gelu_done"], KL * l + c_ + 1)
                    inc(V.tensor_tensor(h32[:, m_ % 2, n], yy[:, c_, n], gg[:, c_, n], ALU.mult), "h32_done")
                    state["h32"] += 1
                dve.wait_ge(sem["conv_step"], (l + 1) * len(CONV))
                dve.wait_ge(sem["ln_mm"], l + 1)
                w = T if full == 0 else C

                def sel(c_):
                    return cv[:, c_, :, :] if full == 0 else cv[:, c_, 1, :]

                def two(ap):
                    return ap.rearrange("p (s n) -> p s n", s=2) if full == 0 else ap

                for c_ in range(KL):
                    inc(V.scalar_tensor_tensor(sel(c_), two(bank[B_ST][:, 0:w]), -1.0 / DL, sel(c_), ALU.mult, ALU.add), "ln_step")
                dve.wait_ge(sem["root_done"], ROOT[("ln", l)])
                inc(V.reciprocal(rstd[:, 0:w], rstd[:, 0:w]), "ln_step")
                dve.wait_ge(sem["ln_step"], LN_STEPS * l + KL + 1)
                for c_ in range(KL):
                    inc(V.tensor_tensor(sel(c_), sel(c_), two(rstd[:, 0:w]), ALU.mult), "ln_step")
                state["h32"] += KL

            def residual(l, k, b_, full, gate):
                if full == 0:
                    step(V.scalar_tensor_tensor(xT[:, 0, k, :], b_[:, 0:C], mt[l][:, gate + k, 1:2], xT[:, 0, k, :], ALU.mult, ALU.add))
                lat = b_[:, C:T] if full == 0 else b_[:, 0:C]
                inc(V.scalar_tensor_tensor(xT[:, 1, k, :], lat, mt[l][:, gate + k, 0:1], xT[:, 1, k, :], ALU.mult, ALU.add), "res_done")

            lo(0)
            lo(1)
            conv_at = 0
            for u, (kind, a, i) in enumerate(UNITS):
                if u + 2 < NU:
                    lo(u + 2)
                if kind == "win" and i == 0:
                    norm(a, 1, 0)
                    conv_at = 0
                    inc(V.memset(glu[:, :, :, 0:PAD], 0.0), "pad_zero")
                    inc(V.memset(glu[:, :, :, PAD + C:GW], 0.0), "pad_zero")
                    inc(V.memset(rpad[:, :, :, 0:RPL], 0.0), "pad_zero")
                    inc(V.memset(rpad[:, :, :, RPL + C:RW], 0.0), "pad_zero")
                if kind == "wout" and i == 0:
                    mix(a, conv_at)
                if kind == "f1" and i == 0:
                    norm(0, 2, 0)
                if kind == "win" and win_kind(i) == "values":
                    full = side(a, "x")
                    n = T if full == 0 else C
                    for h in range(2):
                        t = 2 * i + h
                        c_ = t % KL
                        dve.wait_ge(sem["mm_done"], MM[("win", a, t)])
                        dve.wait_ge(sem["gates_done"], KL * a + c_ + 1)
                        b_ = bank[t % MM_BANKS][:, 0:n]
                        if full == 0:
                            inc(V.tensor_tensor(glu[:, c_, :, PAD:PAD + C], b_.rearrange("p (s n) -> p s n", s=2), cv[:, c_, :, :], ALU.mult), "glu_done")
                        else:
                            inc(V.tensor_tensor(glu[:, c_, 1, PAD:PAD + C], b_, cv[:, c_, 1, :], ALU.mult), "glu_done")
                    if i == 3:
                        dve.wait_ge(sem["glu_done"], KL * (a + 1))
                        dve.wait_ge(sem["pad_zero"], 4 * (a + 1))
                if kind == "wout":
                    full = side(a, "x")
                    for h in range(2):
                        k = 2 * i + h
                        if k == 0 and a == 0:
                            mods(0, 1)
                        if k == 0:
                            dve.wait_ge(sem["mod_ready"], 4 + 2 * a)
                        dve.wait_ge(sem["mm_done"], MM[("wout", a, k)])
                        residual(a, k, bank[k % MM_BANKS], full, 2 * KD)
                if kind == "f3":
                    for h in range(2):
                        j = 2 * i + h
                        dve.wait_ge(sem["mm_done"], MM[("f3", a, j)])
                        dve.wait_ge(sem["silu_out"], j + 1)
                        if j >= 2:
                            dve.wait_ge(sem["gL_done"], j - 1)
                        inc(V.tensor_tensor(gt[:, j % 2, :], sg[:, j % 4, :], bank[2 + h][:, :], ALU.mult), "g_prod")
                if kind == "f2":
                    for h in range(2):
                        k = 2 * i + h
                        dve.wait_ge(sem["mm_done"], MM[("f2", a, k)])
                        residual(0, k, bank[k % MM_BANKS], 0, 5 * KD)
                if kind == "ad" and a == 1 and i == 23:
                    mods(1, 2)
                for lay, more in ((0, 4), (1, 8)):
                    if AT[("win", lay, 3)] < u < AT[("wout", lay, 0)]:
                        conv(lay, conv_at, conv_at + more)
                        conv_at += more

            inc(V.memset(col[:, 0, 6:7], 0.0), "e_lo", CREDIT)
            norm(1, 2, 1)
            rs = {"n": 0}

            def rstep(ins):
                inc(ins, "route_step")
                rs["n"] += 1
                dve.wait_ge(sem["route_step"], rs["n"])

            dve.wait_ge(sem["logits_mm"], 1)
            rstep(V.tensor_copy(lg[:, :, :], bank[0][:, 0:2 * NE].rearrange("p (t e) -> p t e", t=2)))
            rstep(V.tensor_reduce(col[:, :, 0:1], lg[:, :, :], axis=AX.X, op=ALU.max))
            rstep(V.tensor_scalar(col[:, :, 0:1], col[:, :, 0:1], -1.0, None, ALU.mult))
            rstep(V.memset(tab[:, :, 0, :], 4 * FAR))
            dve.wait_ge(sem["route_exp"], 2)
            rstep(V.tensor_reduce(col[:, :, 1:2], pr[:, :, :], axis=AX.X, op=ALU.add))
            rstep(V.reciprocal(col[:, :, 1:2], col[:, :, 1:2]))
            rstep(V.memset(tab[:, :, 1, :], 0.0))
            for t in range(2):
                rstep(V.tensor_scalar(pr[:, t, :], pr[:, t, :], col[:, t, 1:2], None, ALU.mult))
                rstep(V.max(top[:, t, :], pr[:, t, :]))
                rstep(V.max_index(tix[:, t, :], top[:, t, :], pr[:, t, :]))
                rstep(V.tensor_copy(tif[:, t, :], tix[:, t, :]))
                rstep(V.tensor_tensor(col[:, t, 2:3], top[:, t, 0:1], top[:, t, 1:2], ALU.add))
                rstep(V.reciprocal(col[:, t, 2:3], col[:, t, 2:3]))
                rstep(V.tensor_scalar(col[:, t, 4:6], top[:, t, 0:2], col[:, t, 2:3], None, ALU.mult))
                for j in range(2):
                    rstep(V.tensor_scalar(oh[:, t, j, :], K[:, K_IOTA8:K_IOTA8 + NE], tif[:, t, j:j + 1], None, ALU.is_equal))
                rstep(V.tensor_tensor(mask[:, t, :], oh[:, t, 0, :], oh[:, t, 1, :], ALU.add))
                rstep(V.tensor_scalar(oh[:, t, 0, :], oh[:, t, 0, :], col[:, t, 4:5], None, ALU.mult))
                rstep(V.scalar_tensor_tensor(tab[:, t, 1, 0:NE], oh[:, t, 1, :], col[:, t, 5:6], oh[:, t, 0, :], ALU.mult, ALU.add))
            dve.wait_ge(sem["pos_mm"], 1)
            for t in range(2):
                rstep(V.tensor_scalar(lg[:, t, :], mask[:, t, :], -FAR, FAR, ALU.mult, ALU.add))
                rstep(V.tensor_tensor(tab[:, t, 0, 0:NE], bank[1][:, t * NE:(t + 1) * NE], lg[:, t, :], ALU.add))
            rstep(V.tensor_scalar(over[:, 0, :], bank[1][:, 2 * NE:3 * NE], CAP + 0.5, None, ALU.is_gt))
            rstep(V.memset(onesf[:, :], 1.0))
            rstep(V.tensor_tensor_scan(over[:, 1, :], onesf[:, :], over[:, 0, :], 0.0, ALU.mult, ALU.add))
            rstep(V.memset(item_f[:, :], 0.0))
            rstep(V.tensor_copy(item_f[:, 0:NE], K[:, K_IOTA8:K_IOTA8 + NE]))
            for m_ in range(MORE):
                it_ = slice(NE + m_, NE + m_ + 1)
                rstep(V.scalar_tensor_tensor(sel[:, 0, :], over[:, 1, :], float(m_ + 1), over[:, 0, :], ALU.is_equal, ALU.mult))
                rstep(V.tensor_tensor(sel[:, 1, :], sel[:, 0, :], K[:, K_IOTA8:K_IOTA8 + NE], ALU.mult))
                rstep(V.tensor_reduce(item_f[:, it_], sel[:, 1, :], axis=AX.X, op=ALU.add))
                for t in range(2):
                    for kd in range(2):
                        rstep(V.tensor_tensor(sel[:, 1, :], sel[:, 0, :], tab[:, t, kd, 0:NE], ALU.mult))
                        rstep(V.tensor_reduce(tab[:, t, kd, it_], sel[:, 1, :], axis=AX.X, op=ALU.add))
                    rstep(V.tensor_scalar(tab[:, t, 0, it_], tab[:, t, 0, it_], -float(CAP), None, ALU.add))
            rstep(V.tensor_scalar(num_f[:, :], over[:, 1, NE - 1:NE], float(NE), None, ALU.add))
            inc(V.tensor_copy(item_e[:, :], item_f[:, :]), "items_done")
            inc(V.tensor_copy(n_items_t[:, :], num_f[:, :]), "items_done")
            assert rs["n"] == ROUTE_ALL, rs["n"]
            for f in range(4):
                dve.wait_ge(sem["tokH"], f + 1)
                half = slice((f % 2) * 512, (f % 2 + 1) * 512)
                inc(V.tensor_tensor(ftL[:, f // 2, half], bank[2 + f][:, :], ftH[:, f // 2, half].bitcast(F32), ALU.subtract), "tokL")

            dve.wait_ge(sem["items_done"], 2)
            n_items = dve.value_load(n_items_t[0:1, 0:1], min_val=NE, max_val=ITEMS)

            def picks(g):
                inc(V.tensor_copy(cur[:, :, :, :].rearrange("p t k e -> p (t k) e"),
                                  tab[:, :, :, bass.ds(g, 1)].rearrange("p t k e -> p (t k) e")), "pick_done")
                dve.wait_ge(sem["pick_done"], g * 3 + 1)
                for t in range(2):
                    inc(V.tensor_scalar(pick[:, t, :], K[:, K_IOTA:K_IOTA + CAP], cur[:, t, 0, :], None, ALU.is_equal), "pick_done")

            def gather_out(g):
                for q in range(2):
                    dve.wait_ge(sem["xe_hi"], g * 2 + q + 1)
                    xs = slice(4 * q, 4 * q + 4)
                    inc(V.tensor_tensor(xeL[:, xs, :], bank[B_G + q][:, :].rearrange("p (k n) -> p k n", k=4),
                                        xeH[:, xs, :].bitcast(F32), ALU.subtract), "xe_lo")

            def e_lo(x, t, kind, j):
                s = slot(kind, j)
                dve.wait_ge(sem["e_hi"], x * EUNITS + t * 6 + order(kind, j) + 1)
                inc(V.tensor_tensor(wl[s][:, :], raw[s][:, :], wh[s][:, :].bitcast(F32), ALU.subtract), "e_lo")

            def e_prod(x, t, j):
                dve.wait_ge(sem["e_silu"], x * NCH + t * 2 + j + 1)
                inc(V.tensor_tensor(esg[:, :], esg[:, :], bank[B_H + j % 2][:, UC:2 * UC], ALU.mult), "e_prod")

            def e_gl(x, t, j):
                dve.wait_ge(sem["e_gH"], x * NCH + t * 2 + j + 1)
                inc(V.tensor_tensor(egL[:, :], bank[B_T][:, 0:UC], egH[:, :].bitcast(F32), ALU.subtract), "e_gL")

            def y_low(x):
                for h in range(2):
                    dve.wait_ge(sem["y_hi"], x * 2 + h + 1)
                    inc(V.scalar_tensor_tensor(yL[:, h, :], bank[B_Y + h][:, :], cs[:, 0:1],
                                               yH[:, h, :].bitcast(F32), ALU.mult, ALU.subtract), "y_lo")

            g2 = [mt[1][:, 5 * KD + k, 0:1] for k in range(KD)]
            C_BANKS = (B_C, B_G, B_G + 1, B_C)

            def accumulate(x, f):
                dve.wait_ge(sem["comb_mm"], x * 4 + f + 1)
                b_ = bank[C_BANKS[f]]
                for kk in range(2):
                    k = 2 * f + kk
                    inc(V.scalar_tensor_tensor(xT[:, 1, k, :], b_[:, kk * S:(kk + 1) * S], g2[k], xT[:, 1, k, :],
                                               ALU.mult, ALU.add), "acc_done")

            def e_step(x, t, j):
                if j < NCH - 1:
                    e_lo(x, t, "w1", j + 1)
                if j == 0:
                    y_low(x)
                else:
                    e_gl(x, t, j - 1)
                if j < NCH - 1:
                    e_lo(x, t, "w3", j + 1)
                e_prod(x, t, j)
                e_lo(x, t, "w2", j)

            for zero in (egH, egL, pickT):
                inc(V.memset(zero[:, :].bitcast(F32), 0.0), "acc_done")
            inc(V.memset(cs[:, :], 0.0), "acc_done")
            picks(0)
            gather_out(0)
            e_lo(0, 0, "w1", 0)
            e_lo(0, 0, "w3", 0)
            with dve.Fori(0, n_items) as x:
                e_step(x, 0, 0)
                e_step(x, 0, 1)
                accumulate(x, 0)
                accumulate(x, 1)
                e_step(x, 0, 2)
                accumulate(x, 2)
                accumulate(x, 3)
                dve.wait_ge(sem["pick_mm"], x * 2 + 2)
                inc(V.tensor_copy(cs[:, :], bank[B_G + 1][:, 0:1]), "cs_done")
                picks(x + 1)
                with dve.Fori(0, 3) as t:
                    e_step(x, t, 3)
                    e_step(x, t, 4)
                e_step(x, 0, NCH - 2)
                e_step(x, 0, NCH - 1)
                e_gl(x, 0, NCH - 1)
                e_lo(x + 1, 0, "w1", 0)
                gather_out(x + 1)
                e_lo(x + 1, 0, "w3", 0)
            y_low(n_items)
            for f in range(4):
                accumulate(n_items, f)
            dve.wait_ge(sem["root_done"], ROOT["final"])
            step(V.reciprocal(rstd[:, 0:S], rstd[:, 0:S]))
            for k in range(KD):
                step(V.tensor_tensor(xT[:, 1, k, :], xT[:, 1, k, :], rstd[:, 0:S], ALU.mult))
                inc(V.tensor_scalar(xT[:, 1, k, :], xT[:, 1, k, :], fg[:, k:k + 1], None, ALU.mult), "norm_step")

        @block.tensor
        def _(pe):
            mm = nc.tensor.matmul
            ident = K[:, K_ID:K_ID + P]
            ones = K[:, K_ONE:K_ONE + P]

            pe.wait_ge(sem["consts_in"], 16)
            pe.wait_ge(sem["x_in"], 16 * 5)
            for k in range(KD):
                if k >= 4:
                    pe.wait_ge(sem["x_ready"], 2 * (k - 3))
                for t in range(4):
                    last = nc.tensor.transpose(bank[k % 4][:, t * P:(t + 1) * P], xrow[:, t, k * P:(k + 1) * P], ident)
                inc(last, "x_tr")
            pe.wait_ge(sem["params_in"], 16 * PARAM_DMAS)
            for n, (tile, rows_) in enumerate(ROW_PARTS):
                if n >= 4:
                    pe.wait_ge(sem["params_ready"], n - 3)
                inc(nc.tensor.transpose(bank[4 + n % 4][:, 0:rows_], prow[0:rows_, tile, :], ident[0:rows_, 0:rows_]), "params_t")
            pe.wait_ge(sem["cols_ready"], 4)
            pe.wait_ge(sem["memset_done"], 3)

            pending = []

            def transpose_rows():
                while pending:
                    l, q = pending.pop()
                    n = l * 24 + q
                    pe.wait_ge(sem["row_out"], n + 1)
                    if n == 24:
                        pe.wait_ge(sem["mod_ready"], 4)
                    for h in range(2):
                        o_ = (2 * q + h) * 2
                        last = mm(bank[B_MT][:, o_:o_ + 2], mrow[0:4, n % 2, h * P:(h + 1) * P], K[0:4, K_COMB:K_COMB + 2],
                                  start=True, stop=True)
                    inc(last, "mt_mm")

            st = dict(sq=0, hl=0, norms=0)

            def sums(n, count, w):
                for k in range(count):
                    pe.wait_ge(sem["sq_done"], st["sq"] + 1)
                    inc(mm(bank[B_ST][:, 0:n], w, sq[:, st["sq"] % 2, 0:n], start=(k == 0), stop=(k == count - 1)), "sum_mm")
                    st["sq"] += 1

            def chunk(dst, u, k_n, h, rH, rL, sel):
                s = u % RING
                n = 0
                for k in range(k_n):
                    w_ = slice(k * UC + h * P, k * UC + (h + 1) * P)
                    for l_, r_ in split3(wh[s], wl[s], rH, rL):
                        last = mm(dst, l_[:, w_], r_[:, k, sel], start=(n == 0), stop=(n == 3 * k_n - 1))
                        n += 1
                return last

            def mix(l):
                full = side(l, "x")
                w = T if full == 0 else C
                pe.wait_ge(sem["gelu_done"], KL * (l + 1))
                for c_ in range(KL):
                    g_ = l * KL + c_
                    pe.wait_ge(sem["rconv_done"], RTAPS * KL * l + (RTAPS - 1) * KL + c_ + 1)
                    pe.wait_ge(sem["bd_in"], 16 * 8 * (l + 1))
                    for kd in range(2):
                        for d in range(2):
                            b_ = 2 * kd + d
                            if c_:
                                pe.wait_ge(sem["sig_done"], 4 * (g_ - 1) + b_ + 1)
                            inc(mm(bank[b_][:, :], bdw[:, c_, d, kd, :], rc[:, c_, :], start=True, stop=True), "bd_mm")
                pe.wait_ge(sem["conv_step"], (l + 1) * TAPS * KL)
                for c_ in range(KL):
                    last = mm(bank[B_ST][:, 0:w], ones, cv[:, c_, :, :] if full == 0 else cv[:, c_, 1, :],
                              start=(c_ == 0), stop=(c_ == KL - 1))
                inc(last, "ln_mm")
                pe.wait_ge(sem["ln_step"], LN_STEPS * l + KL)
                sums(w, KL, ones)
                pe.wait_ge(sem["hL_done"], HL[("mix", l)])
                pe.wait_ge(sem["sig_done"], 4 * KL * (l + 1))

            for u, (kind, a, i) in enumerate(UNITS):
                if kind == "win" and i == 0:
                    transpose_rows()
                    sums(T, KD, ones)
                    pe.wait_ge(sem["hL_done"], HL[("norm", a, 1)])
                if kind == "wout" and i == 0:
                    transpose_rows()
                    mix(a)
                if kind == "f1" and i == 0:
                    sums(T, KD, ones)
                    pe.wait_ge(sem["hL_done"], HL[("norm", 0, 2)])
                pe.wait_ge(sem["lo_done"], u + 1)
                s = u % RING
                if kind == "ad":
                    n = a * 24 + i
                    if n >= 2:
                        pe.wait_ge(sem["row_out"], n - 1)
                    b_ = bank[B_ROW + n % 2][:, 0:UC]
                    for k in range(KD):
                        for w_ in (wh[s], wl[s]):
                            last = mm(b_, smat[:, k, :], w_[:, k * UC:(k + 1) * UC], start=(k == 0 and w_ is wh[s]),
                                      stop=(k == KD - 1 and w_ is wl[s]))
                    inc(last, "mm_done")
                elif kind == "win":
                    full = side(a, "rec" if win_kind(i) == "rec" else "x")
                    w = T if full == 0 else C
                    for h in range(2):
                        t = 2 * i + h
                        if t >= MM_BANKS:
                            free = {"gates": "gates_done", "values": "glu_done", "rec": "rec_done"}[win_kind((t - 4) // 2)]
                            pe.wait_ge(sem[free], KL * a + t % KL + 1)
                        last = chunk(bank[t % MM_BANKS][:, 0:w], u, KD, h, hH, hL, cols(full))
                        inc(last, "mm_done")
                elif kind == "wout":
                    full = side(a, "x")
                    w = T if full == 0 else C
                    for h in range(2):
                        k_ = 2 * i + h
                        if k_ >= MM_BANKS:
                            pe.wait_ge(sem["res_done"], RES[("wout", a)] + k_ - MM_BANKS + 1)
                        last = chunk(bank[k_ % MM_BANKS][:, 0:w], u, KD, h, hH, hL, cols(full))
                        inc(last, "mm_done")
                elif kind in ("f1", "f3"):
                    for h in range(2):
                        j = 2 * i + h
                        if j >= 2:
                            pe.wait_ge(sem["silu_out" if kind == "f1" else "g_prod"], j - 1)
                        if kind == "f1" and j % KD < 2 and j >= KD:
                            pe.wait_ge(sem["res_done"], RES[("f2", j // KD - 1)] + 8)
                        last = chunk(bank[(0 if kind == "f1" else 2) + h][:, :], u, KD, h, hH, hL, slice(0, T))
                        inc(last, "mm_done")
                elif kind == "f2":
                    for h in range(2):
                        k_ = 2 * i + h
                        if k_ == 0:
                            pe.wait_ge(sem["gL_done"], 2 * sum(FFN_GROUPS[:a + 1]))
                        if k_ < 2:
                            pe.wait_ge(sem["silu_out"], 2 * sum(FFN_GROUPS[:a + 1]))
                        if k_ >= MM_BANKS:
                            pe.wait_ge(sem["res_done"], RES[("f2", a)] + k_ - MM_BANKS + 1)
                        last = chunk(bank[k_ % MM_BANKS][:, :], u, 2 * FFN_GROUPS[a], h, gH, gL, slice(0, T))
                        inc(last, "mm_done")
                transpose_rows()
                if kind == "ad":
                    pending.append((a, i))

            sums(S, KD, ones)
            pe.wait_ge(sem["fT_done"], KD)
            pe.wait_ge(sem["router_in"], 16)
            for t in range(2):
                tok = slice(t * P, (t + 1) * P)
                for k in range(KD):
                    last = mm(bank[0][:, t * NE:(t + 1) * NE], fT[:, k, tok], rt[:, k, :], start=(k == 0), stop=(k == KD - 1))
            inc(last, "logits_mm")
            for f in range(4):
                t = f // 2
                for k in range(4):
                    last = nc.tensor.transpose(bank[2 + f][:, k * P:(k + 1) * P],
                                               fT[:, (f % 2) * 4 + k, t * P:(t + 1) * P], ident)
                inc(last, "tok_tr")
            pe.wait_ge(sem["route_step"], ROUTE_MASKS)
            up = K[:, K_UP:K_UP + P]
            for o_, parts in ((0, ((up, 0),)), (NE, ((ones, 0), (up, 1))), (2 * NE, ((ones, 0), (ones, 1)))):
                for n, (w_, t) in enumerate(parts):
                    last = mm(bank[1][:, o_:o_ + NE], w_, mask[:, t, :], start=(n == 0), stop=(n == len(parts) - 1))
            inc(last, "pos_mm")

            pe.wait_ge(sem["items_done"], 2)
            n_items = pe.value_load(n_items_t[0:1, 0:1], min_val=NE, max_val=ITEMS)

            def gather(g):
                pe.wait_ge(sem["pick_done"], g * 3 + 3)
                for q in range(2):
                    for kk in range(4):
                        k = 4 * q + kk
                        n = 0
                        for t in range(2):
                            for ft in (ftH, ftL):
                                last = mm(bank[B_G + q][:, kk * CAP:(kk + 1) * CAP], ft[:, t, k * P:(k + 1) * P],
                                          pick[:, t, :], start=(n == 0), stop=(n == 3))
                                n += 1
                    inc(last, "gather_mm")

            def slots(x):
                pe.wait_ge(sem["acc_done"], x * 8 + 4 + 4)
                for t in range(2):
                    last = nc.tensor.transpose(bank[B_G][:, t * P:(t + 1) * P], pick[:, t, :].bitcast(F32), ident)
                inc(last, "pick_mm")
                pe.wait_ge(sem["acc_done"], x * 8 + 6 + 4)
                for t in range(2):
                    last = mm(bank[B_G + 1][:, 0:1], pick[:, t, :].bitcast(F32), cur[:, t, 1, :], start=(t == 0), stop=(t == 1))
                inc(last, "pick_mm")

            def e_up(x, t, kind, j):
                s = slot(kind, j)
                pe.wait_ge(sem["e_lo"], x * EUNITS + t * 6 + order(kind, j) + 1 + CREDIT)
                m_ = 0
                h = ("w1", "w3").index(kind)
                dst = bank[B_H + j % 2][:, h * UC:(h + 1) * UC]
                for k in range(KD):
                    for l_, r_ in split3(xeH, xeL, wh[s], wl[s]):
                        last = mm(dst, l_[:, k, :], r_[:, k * UC:(k + 1) * UC], start=(m_ == 0), stop=(m_ == 3 * KD - 1))
                        m_ += 1
                inc(last, "e_used")

            def e_tr(x, t, j):
                pe.wait_ge(sem["e_prod"], x * NCH + t * 2 + j + 1)
                for f in range(2):
                    last = nc.tensor.transpose(bank[B_T][:, f * P:(f + 1) * P], esg[:, f * P:(f + 1) * P], ident)
                inc(last, "g_tr")

            def e_down(x, t, j):
                s = slot("w2", j)
                pe.wait_ge(sem["e_gL"], x * NCH + t * 2 + j + 1)
                pe.wait_ge(sem["e_lo"], x * EUNITS + t * 6 + order("w2", j) + 1 + CREDIT)
                for f in range(2):
                    for h in range(2):
                        for n, (l_, r_) in enumerate(split3(egH, egL, wh[s], wl[s])):
                            last = mm(bank[B_Y + h][:, :], l_[:, f * P:(f + 1) * P],
                                      r_[:, f * D + h * 512:f * D + (h + 1) * 512],
                                      start=(j == 0 and f == 0 and n == 0), stop=(j == NCH - 1 and f == 1 and n == 2))
                inc(last, "e_used")

            def e_step(x, t, j):
                e_up(x, t, "w1", j)
                if j:
                    e_tr(x, t, j - 1)
                e_up(x, t, "w3", j)
                if j == 1:
                    pe.wait_ge(sem["y_lo"], x * 2 + 2)
                if j:
                    e_down(x, t, j - 1)

            def combine(x, h):
                pe.wait_ge(sem["y_lo"], x * 2 + h + 1)
                for q in range(2):
                    f = 2 * h + q
                    if f == 3:
                        pe.wait_ge(sem["acc_done"], x * 8 + 2 + 4)
                    for kk in range(2):
                        k = 2 * q + kk
                        for n, y_ in enumerate((yH, yL)):
                            last = mm(bank[C_BANKS[f]][:, kk * S:(kk + 1) * S], y_[:, h, k * P:(k + 1) * P], pickT[:, :],
                                      start=(n == 0), stop=(n == 1))
                    inc(last, "comb_mm")

            C_BANKS = (B_C, B_G, B_G + 1, B_C)
            pe.wait_ge(sem["tokL"], 4)
            for h in range(2):
                for z in range(2):
                    last = mm(bank[B_Y + h][:, z * UC:(z + 1) * UC], zeros[:, 0:P], zeros[:, :], start=(z == 0), stop=(z == 1))
            inc(last, "e_used", CREDIT)
            gather(0)
            with pe.Fori(0, n_items) as x:
                pe.wait_ge(sem["xe_lo"], x * 2 + 2)
                e_step(x, 0, 0)
                e_step(x, 0, 1)
                pe.wait_ge(sem["acc_done"], x * 8 + 4)
                combine(x, 0)
                e_step(x, 0, 2)
                combine(x, 1)
                slots(x)
                with pe.Fori(0, 4) as t:
                    e_step(x, t, 3)
                    e_step(x, t, 4)
                e_tr(x, 0, NCH - 1)
                pe.wait_ge(sem["pickT_done"], x + 1)
                pe.wait_ge(sem["cs_done"], x + 1)
                gather(x + 1)
                e_down(x, 0, NCH - 1)
            pe.wait_ge(sem["xe_lo"], n_items * 2 + 2)
            pe.wait_ge(sem["acc_done"], n_items * 8 + 4)
            combine(n_items, 0)
            combine(n_items, 1)
            pe.wait_ge(sem["acc_done"], n_items * 8 + 4 + 8)
            sums(S, KD, ones)
            pe.wait_ge(sem["norm_step"], KD)
            for f in range(4):
                for k in range(4):
                    last = nc.tensor.transpose(bank[f][:, k * P:(k + 1) * P],
                                               xT[:, 1, (f % 2) * 4 + k, (f // 2) * P:(f // 2 + 1) * P], ident)
                inc(last, "fin_tr")


_INS = ["x", "c", "ctx", "c_ctx", "w_mod", "b_mod", "norm1_g", "norm2_g", "w_in", "w_out",
        "lru_conv_w", "lru_conv_b", "lru_wa", "lru_ba", "lru_wx", "lru_bx", "lru_lambda",
        "conf_dw_w", "conf_dw_b", "conf_ln_g", "conf_ln_b",
        "ffn_w1", "ffn_w3", "ffn_w2", "moe_router", "moe_w1", "moe_w3", "moe_w2", "final_g"]
GRID_W = 64


def position_table():
    quarter = D // 4
    omega = (1.0 / (10000.0 ** (np.arange(quarter, dtype=np.float32) / np.float32(quarter)))).astype(np.float32)

    def emb1d(n):
        ang = np.arange(n, dtype=np.float32)[:, None] * omega[None, :]
        return np.concatenate([np.sin(ang), np.cos(ang)], axis=-1)

    n_rows = S // GRID_W
    er = np.broadcast_to(emb1d(n_rows)[:, None, :], (n_rows, GRID_W, D // 2))
    ec = np.broadcast_to(emb1d(GRID_W)[None, :, :], (n_rows, GRID_W, D // 2))
    return np.ascontiguousarray(np.concatenate([er, ec], axis=-1).reshape(S, D).T.astype(np.float32))


def shape_constants():
    k = np.zeros((P, K_W), np.float32)
    k[:, K_ID:K_ID + P] = np.eye(P)
    k[:, K_UP:K_UP + P] = np.triu(np.ones((P, P)), 1)
    k[:, K_ONE:K_ONE + P] = 1.0
    k[:, K_IOTA:K_IOTA + CAP] = np.arange(CAP)
    k[:, K_IOTA8:K_IOTA8 + NE] = np.arange(NE)
    for r in range(4):
        k[r, K_COMB + r % 2] = 1.0
    return k


def kernel(**inputs):
    import concourse.bacc as _bacc
    from concourse.bass_utils import run_bass_kernel_spmd as _run

    nc = _bacc.Bacc("TRN2", target_bir_lowering=False, num_devices=1)
    host = {name: np.ascontiguousarray(inputs[name]) for name in _INS}
    host["pos_t"] = position_table()
    host["consts"] = shape_constants()
    arrays, args = {}, []
    for name, a in host.items():
        arrays[f"in_{name}"] = a
        args.append(nc.dram_tensor(f"in_{name}", a.shape, mybir.dt.from_np(a.dtype), kind="ExternalInput").ap())
    args.append(nc.dram_tensor("out_0", (1, S, D), F32, kind="ExternalOutput").ap())
    dit_kernel(nc, *args)
    r = _run(nc, [arrays], core_ids=[0])
    return r.results[0]["out_0"]
```

```python
import numpy as np
import concourse.bass as bass
from concourse import mybir
from concourse.alu_op_type import AluOpType as ALU

F32 = mybir.dt.float32
F32R = mybir.dt.float32r
I32 = mybir.dt.int32
U32 = mybir.dt.uint32
ACT = mybir.ActivationFunctionType
AX = mybir.AxisListType

P = 128
D = 1024
KD = D // P
S = 256
C = 256
T = S + C
DL = 512
KL = DL // P
NH, DH = 8, 64
TAPS, PAD = 31, 15
POOL_CHUNK, DVE_CHUNKS, PE_CHUNKS = 0, ((0, 1, 2), (0, 1)), ((3,), (2, 3))
DIAGS = 4
DVE_ITEMS = (5, 10)
PE_TAPS = (3, 8)
PE_FROM = (5, 4)
WIN_BANKS = 3
RTAPS, RPL, RPR = 4, 2, 1
LRU_C = 8.0
DFF = 2816
NE = 8
NMOD = 6
DEPTH = 2
EPS = 1e-6
UC = 256
UW = KD * UC
CAP = 128
FAR = 1000.0
GW = 2 * PAD + C
RW = RPL + RPR + C

K_ID, K_UP, K_ONE, K_IOTA, K_IOTA8, K_COMB, K_W = 0, 128, 256, 384, 512, 520, 522
R_BMOD, R_N1, R_N2, R_CW, R_CB, R_BA, R_BX, R_LAM, R_DWB, R_LNG, R_LNB, R_END = (
    0, 48, 56, 64, 80, 84, 92, 100, 108, 112, 116, 120)
R_C, R_CC, R_FG, R_MEND = 0, 8, 16, 24

WIN_BASE = {"rec": 0, "gelu": DL, "values": 2 * DL, "gates": 3 * DL}
WIN = [("gates", 0), ("values", 0), ("rec", 0), ("gates", 1), ("values", 1), ("rec", 1), ("gelu", 0), ("gelu", 1)]
LRU_AT = {3: 0, 5: 1, 6: 2, 7: 3}
FFN_GROUPS = [4, 4, 3]
NCH = DFF // UC
EUNITS = 3 * NCH
MORE = (2 * S - 1) // (CAP + 1)
ITEMS = NE + MORE
CREDIT = 9


def weight_units():
    units = [("ad", 0, q) for q in range(8)]
    for i in range(8):
        units += [("win", 0, i), ("ad", 0, 8 + 2 * i), ("ad", 0, 9 + 2 * i)]
    units += [("wout", 0, i) for i in range(4)]
    ffn, j = [], 0
    for g, n in enumerate(FFN_GROUPS):
        for _ in range(n):
            ffn += [("f1", g, j), ("f3", g, j)]
            j += 1
        ffn += [("f2", g, i) for i in range(4)]
    for n, unit in enumerate(ffn):
        units.append(unit)
        if n < 16 and n % 2 == 0:
            units.append(("ad", 1, n // 2))
        elif 16 <= n < 32:
            units.append(("ad", 1, n - 8))
    units += [("win", 1, i) for i in range(8)]
    units += [("wout", 1, i) for i in range(4)]
    return units


UNITS = weight_units()


def order(kind, j):
    if kind == "w2":
        return min(3 * j + 4, EUNITS - 1)
    return (0 if j == 0 else 3 * j - 1) + (kind == "w3")


def before(kind, j):
    return order(kind, j - 2) if j >= 2 else order(kind, NCH - (1 if j == 0 else 2)) - EUNITS


def slot(kind, j):
    return ("w1", "w3", "w2").index(kind) + 3 * (j % 2)


def uses(j):
    return (NCH + 1) // 2 if j % 2 == 0 else NCH // 2


SUMMED = KD - 2
RING = 3
RING2 = 6
MM_BANKS = 4


def dit_kernel(nc, x, c, ctx, c_ctx, w_mod, b_mod, norm1_g, norm2_g, w_in, w_out,
               lru_conv_w, lru_conv_b, lru_wa, lru_ba, lru_wx, lru_bx, lru_lambda,
               conf_dw_w, conf_dw_b, conf_ln_g, conf_ln_b,
               ffn_w1, ffn_w3, ffn_w2, moe_router, moe_w1, moe_w3, moe_w2, final_g,
               pos_t, consts, out):
    tokens_in = x
    place = {"at": 16512}

    def sb(name, shape, dt=F32, at=None):
        size = int(np.prod(shape[1:])) * 4
        size = (size + 31) // 32 * 32
        off = place["at"] if at is None else at
        if at is None:
            place["at"] += size
        assert off + size <= 229368, (name, off + size)
        t = nc.alloc_sbuf_tensor_at(name, [P] + list(shape[1:]), dt, offset=off)
        return t, off, off + size

    K, _, _ = sb("shape_consts", [P, K_W])
    eps, _, _ = sb("eps", [P, 1])
    table, _, _ = sb("table_load", [P, 1])
    fg, _, _ = sb("final_g_t", [P, KD])
    mt = [sb(f"mod_t{l}", [P, NMOD * KD, 2])[0] for l in range(DEPTH)]
    amp, _, _ = sb("norm_scale", [P, KD, 2])
    n_items_t, _, _ = sb("n_items", [P, 1], I32)
    item_e, _, _ = sb("item_expert", [P, ITEMS + 1], I32)
    rt, _, _ = sb("router", [P, KD, NE])
    spn, _, _ = sb("decay_rate", [P, DEPTH, 2, 8])
    sp_t, _, _ = sb("softplus_tmp", [P, 4, 8])
    zeros, _, _ = sb("zeros", [P, UC], F32R)
    xT, xT_at, _ = sb("x_t", [P, 2, KD, C])
    raw = [sb(f"raw{s}", [P, UW])[0] for s in range(RING)]
    wh = [sb(f"w_hi{s}", [P, UW], F32R)[0] for s in range(RING)]
    wl = [sb(f"w_lo{s}", [P, UW], F32R)[0] for s in range(RING)]
    scratch = place["at"]
    gate_r, nb_at, _ = sb("decay_a", [P, 2, T])
    root, _, _ = sb("root", [P, 2, T])
    h32, h32_at, _ = sb("h32", [P, 2, T])
    assert DIAGS * P + C <= 2 * T
    sq, _, _ = sb("squares", [P, 2, T], at=nb_at)
    rstd, _, _ = sb("rstd", [P, T], at=nb_at + 4096)
    norm_t, _, _ = sb("norm_tmp", [P, 4, T], at=nb_at)
    diag, _, _ = sb("tap_diags", [P, DIAGS, P], at=h32_at)
    par, _, par_end = sb("params_t", [P, 2 * DEPTH + 1, P])
    mrow, _, _ = sb("mod_rows", [P, 2, UC])
    smat, _, _ = sb("silu_c_cols", [P, KD, P], F32R)
    sv, _, _ = sb("silu_c", [P, 2 * KD])
    hH, _, _ = sb("h_hi", [P, KD, T], F32R)
    hL, _, _ = sb("h_lo", [P, KD, T], F32R)
    bdw, _, _ = sb("block_diag", [P, KL, 2, 2, P])
    mix_at = place["at"]
    glu, _, _ = sb("glu_pad", [P, KL, 2, GW])
    cv, _, _ = sb("conv_out", [P, KL, 2, C])
    rpad, _, _ = sb("rec_pad", [P, 2, 2, RW])
    rc, _, _ = sb("rec_conv", [P, KL, T])
    gg, _, _ = sb("gelu_gate", [P, KL, T])
    yy, _, _ = sb("scan_sum", [P, KL, T])
    pv, _, _ = sb("pool_product", [P, C], at=h32_at + DIAGS * P * 4)
    rg, _, _ = sb("rec_gate", [P, 2, T])
    ig, _, _ = sb("in_gate", [P, 2, T])
    gH, _, e_ = sb("g_hi", [P, KD, T], F32R, at=mix_at)
    gL, _, e_ = sb("g_lo", [P, KD, T], F32R, at=e_)
    sg, _, e_ = sb("silu_out", [P, 4, T], at=e_)
    macc, _, _ = sb("mod_sums", [P, 2, 2, UC], at=e_)
    gt, _, e_ = sb("g_prod", [P, 2, T], at=nb_at)
    prow, _, e_ = sb("param_rows", [P, 2 * DEPTH + 1, P], at=mix_at)
    xrow, _, e_ = sb("x_rows", [P, 4, D], at=e_)
    pos, _, e_ = sb("pos_t", [P, KD, S], at=e_)
    esg, _, e_ = sb("e_silu", [P, UC], at=scratch)
    egH, _, e_ = sb("e_g_hi", [P, UC], F32R, at=e_)
    egL, _, e_ = sb("e_g_lo", [P, UC], F32R, at=e_)
    yH, _, e_ = sb("y_hi", [P, 2, 512], F32R, at=e_)
    yL, _, e_ = sb("y_lo", [P, 2, 512], F32R, at=e_)
    e_ = max(e_, par_end)
    pick, _, e_ = sb("pick", [P, 2, CAP], F32R, at=e_)
    pickT, _, e_ = sb("pick_t", [P, S], F32R, at=e_)
    tab, _, e_ = sb("slot_table", [P, 2, 2, ITEMS + 1], at=e_)
    cur, _, e_ = sb("slot_now", [P, 2, 2, 1], at=e_)
    cs, _, e_ = sb("slot_weight", [P, 1], at=e_)
    assert e_ >= par_end
    for s in range(RING, RING2):
        t, _, e_ = sb(f"raw{s}", [P, UW], at=e_)
        raw.append(t)
        t, _, e_ = sb(f"w_hi{s}", [P, UW], F32R, at=e_)
        wh.append(t)
        t, _, e_ = sb(f"w_lo{s}", [P, UW], F32R, at=e_)
        wl.append(t)
    ftH, _, _ = sb("f_tok_hi", [P, 2, D], F32R, at=xT_at)
    orow, _, _ = sb("out_rows", [P, 2, D], at=e_)
    ftL, _, e_ = sb("f_tok_lo", [P, 2, D], F32R, at=e_)
    xe_at = e_
    xeH, _, e_ = sb("xe_hi", [P, KD, CAP], F32R, at=e_)
    xeL, _, e_ = sb("xe_lo", [P, KD, CAP], F32R, at=e_)
    fT, _, e3 = sb("f_t", [P, KD, S], at=xe_at)
    lg, _, e3 = sb("logits", [P, 2, NE], at=e3)
    pr, _, e3 = sb("probs", [P, 2, NE], at=e3)
    top, _, e3 = sb("top8", [P, 2, 8], at=e3)
    tix, _, e3 = sb("top8_index", [P, 2, 8], U32, at=e3)
    tif, _, e3 = sb("top8_index_f", [P, 2, 8], at=e3)
    oh, _, e3 = sb("one_hots", [P, 2, 2, NE], at=e3)
    mask, _, e3 = sb("mask", [P, 2, NE], at=e3)
    col, _, e3 = sb("route_cols", [P, 2, 8], at=e3)
    over, _, e3 = sb("overflow", [P, 2, NE], at=e3)
    sel, _, e3 = sb("selected", [P, 2, NE], at=e3)
    onesf, _, e3 = sb("ones8", [P, NE], at=e3)
    item_f, _, e3 = sb("item_expert_f", [P, ITEMS + 1], at=e3)
    num_f, _, e3 = sb("n_items_f", [P, 1], at=e3)
    assert e3 <= 229368

    bank = [nc.alloc_psum_tensor(f"bank{b}", [P, 512], F32) for b in range(8)]
    B_H, B_T, B_Y, B_G, B_C = 0, 2, 3, 5, 7
    B_ROW, B_MT, B_ST = 4, 6, 7
    B_TOK = (2, 5, 6, 7)
    B_GATE = (5, B_ST)

    names = """consts_in params_in x_in bd_in x_out params_t misc_in misc_t misc_ready pos_in x_tr x_ready params_ready silu_ready cols_ready
        memset_done hi_done lo_done row_out mt_mm mod_ready ctx_done scaled table_in mod_step mod_sum0 decay_done decay_exp
        sq_done sum_mm root_done norm_step h32_done hH_done hL_done
        mm_done gates_done glu_done rec_done gelu_done rconv_done conv_step pool_conv pe_conv diag_done pe_conv_out
        bd_mm sig_done act_step dve_step ig_done root_in scan_done lru_done ln_mm ln_step
        res_done silu_out g_prod gH_done gL_done fT_done
        router_in logits_mm route_step route_exp pos_mm items_done tok_tr tokH tokL
        e_hi e_lo e_used e_silu e_prod g_tr e_gH e_gL y_hi y_lo comb_mm acc_done
        pick_done gather_mm pick_mm pickT_done cs_done xe_hi xe_lo fin_tr fin_out pad_zero bd_zero""".split()
    sem = {n: nc.alloc_semaphore(n) for n in names}
    unit_full = [nc.alloc_semaphore(f"unit_full{s}") for s in range(RING)]
    e_full = [nc.alloc_semaphore(f"e_full{s}") for s in range(RING2)]

    def inc(ins, name, n=1):
        return ins.then_inc(sem[name], n)

    def split3(hi_l, lo_l, hi_r, lo_r):
        return ((hi_l, hi_r), (hi_l, lo_r), (lo_l, hi_r))

    def layer_par(l, row, n=1):
        return par[:, 2 * l, row:row + n]

    def tap(l, t, c_):
        return par[:, 2 * l + 1, t * KL + c_:t * KL + c_ + 1]

    def side(l, kind):
        return 0 if l == 0 or kind == "rec" else 1

    def cols(full):
        return slice(0, T) if full == 0 else slice(C, T)

    NU = len(UNITS)

    def win_kind(i):
        return WIN[i][0]

    def win_chunk(t):
        return 2 * WIN[t // 2][1] + t % 2

    def win_col(i):
        return WIN_BASE[WIN[i][0]] + WIN[i][1] * UC

    def conv_part(l, c_, t, pool=False):
        if l == 0:
            if c_ == POOL_CHUNK:
                s_ = 0 if pool else 1
                return glu[:, c_, s_, t:t + C], cv[:, c_, s_, :]
            return glu[:, c_, :, t:t + C], cv[:, c_, :, :]
        if c_ == POOL_CHUNK:
            a, b = (0, C // 2) if pool else (C // 2, C)
            return glu[:, c_, 1, t + a:t + b], cv[:, c_, 1, a:b]
        return glu[:, c_, 1, t:t + C], cv[:, c_, 1, :]

    def pe_taps(u):
        for l in range(DEPTH):
            n = u - AT[("win", l, PE_FROM[l])]
            if n >= 0 and u < AT[("wout", l, 0)]:
                return l, *(min(m_ * PE_TAPS[l], len(PE_CONV[l])) for m_ in (n, n + 1))
        return None

    def pe_bank(c_):
        return WIN_BANKS + KL - 1 - c_

    def lru_at(u, behind):
        found = []
        for l in range(DEPTH):
            for i, c_ in LRU_AT.items():
                if min(AT[("win", l, i)] + behind, AT[("wout", l, 0)]) == u:
                    found.append((l, c_))
        return found

    def by_dve(unit):
        return unit[0] == "ad" and unit[1] == 1

    def mod_vectors(l, q):
        return 2 if l == 0 or q < KD else 1

    PE_CONV, DVE_CONV = ([[(t, c_) for c_ in chunks[l] for t in range(TAPS)] for l in range(DEPTH)]
                         for chunks in (PE_CHUNKS, DVE_CHUNKS))
    PE_BASE, DVE_BASE = ([0, len(w[0]), len(w[0]) + len(w[1])] for w in (PE_CONV, DVE_CONV))

    MM, USED, HI, n = {}, [], [], 0
    for kind, a, i in UNITS:
        HI.append((HI[-1] if HI else 0) + (not by_dve((kind, a, i))))
        for h in range(0 if by_dve((kind, a, i)) else 1 if kind == "ad" else 2):
            n += 1
            MM[(kind, a, i if kind == "ad" else 2 * i + h)] = n
        USED.append(n)
    AT = {unit: u for u, unit in enumerate(UNITS)}
    RES = {("wout", 0): 0, ("f2", 0): KD, ("f2", 1): 2 * KD, ("f2", 2): 3 * KD, ("wout", 1): 4 * KD,
           (0, 2): KD, (1, 1): 4 * KD, (1, 2): 5 * KD}
    HL = {("norm", 0, 1): KD, ("mix", 0): 2 * KD, ("norm", 0, 2): 3 * KD, ("norm", 1, 1): 4 * KD, ("mix", 1): 5 * KD}
    ROOT = {(0, 1): 1, ("mix", 0): 1, ("ln", 0): 2 + 2 * KL, (0, 2): 3 + 2 * KL, (1, 1): 4 + 2 * KL, ("mix", 1): 4 + 2 * KL,
            ("ln", 1): 5 + 4 * KL, (1, 2): 6 + 4 * KL, "final": 7 + 4 * KL}
    LN_STEPS = 2 * KL + 1
    DECAY_ALL = 3 * DEPTH
    ROUTE_MASKS = 8 + 2 + 2 + 3 + 2 + 4 + 1
    ROUTE_ALL = ROUTE_MASKS + 3 + 2 + 2 + 2 + 5 + MORE * (3 + 9) + 1

    def unit_src(kind, a, i):
        if kind == "ad":
            return w_mod[a, :, i * UC:(i + 1) * UC].rearrange("(k p) n -> p k n", p=P)
        if kind == "win":
            return w_in[a, :, win_col(i):win_col(i) + UC].rearrange("(k p) n -> p k n", p=P)
        if kind == "wout":
            return w_out[a, :, i * UC:(i + 1) * UC].rearrange("(k p) n -> p k n", p=P)
        if kind in ("f1", "f3"):
            w = ffn_w1 if kind == "f1" else ffn_w3
            return w[0, :, i * UC:(i + 1) * UC].rearrange("(k p) n -> p k n", p=P)
        r0 = sum(FFN_GROUPS[:a]) * UC
        r1 = r0 + FFN_GROUPS[a] * UC
        return ffn_w2[0, r0:r1, i * UC:(i + 1) * UC].rearrange("(k p) n -> p k n", p=P)

    def unit_k(kind, a):
        return 2 * FFN_GROUPS[a] if kind == "f2" else KD

    PARAM_ROWS = []
    for l in range(DEPTH):
        for row, w in ((R_BMOD, b_mod), (R_N1, norm1_g), (R_N2, norm2_g), (R_CB, lru_conv_b), (R_DWB, conf_dw_b),
                       (R_LNG, conf_ln_g), (R_LNB, conf_ln_b)):
            PARAM_ROWS.append((2 * l, row, w[l].rearrange("(r p) -> r p", p=P)))
        for row, w in ((R_CW, lru_conv_w), (R_BA, lru_ba), (R_BX, lru_bx), (R_LAM, lru_lambda)):
            PARAM_ROWS.append((2 * l, row, w[l].rearrange("t (r p) -> (t r) p", p=P)))
        PARAM_ROWS.append((2 * l + 1, 0, conf_dw_w[l].rearrange("t (r p) -> (t r) p", p=P)))
    PARAM_BATCH = 6
    ROW_PARTS = [(0, R_END), (2, R_END), (1, TAPS * KL), (3, TAPS * KL)]
    B_MISC = 5

    block = nc.Block()
    with block:
        @block.sync
        def _(sp):
            inc(sp.dma_start(K[:, :], consts), "consts_in", 16)
            for u, (kind, a, i) in enumerate(UNITS):
                for tile, at, src in PARAM_ROWS[max(u - RING, 0) * PARAM_BATCH:max(u - RING + 1, 0) * PARAM_BATCH]:
                    inc(sp.dma_start(prow[at:at + src.shape[0], tile, :], src), "params_in", 16)
                if u == KD:
                    inc(sp.dma_start(rt[:, :, :], moe_router[0].rearrange("(k p) e -> p k e", p=P)), "router_in", 16)
                if u >= RING:
                    sp.wait_ge(sem["lo_done"], u - RING + 1)
                nk = unit_k(kind, a)
                sp.dma_start(raw[u % RING][:, 0:nk * UC].rearrange("p (k n) -> p k n", n=UC),
                             unit_src(kind, a, i)).then_inc(unit_full[u % RING], 16)

            def load(x, t, kind, j, e):
                s = slot(kind, j)
                sp.wait_ge(sem["e_lo"], x * EUNITS + t * 6 + before(kind, j) + 1 + CREDIT)
                f = bass.ds(t * (2 * UC) + j * UC, UC)
                w = {"w1": moe_w1, "w3": moe_w3, "w2": moe_w2}[kind]
                if kind == "w2":
                    src = w[0, bass.ds(e, 1), f, :].rearrange("a (k p) n -> p (a k) n", p=P)
                    dst = raw[s][:, :].rearrange("p (k n) -> p k n", k=2)
                else:
                    src = w[0, bass.ds(e, 1), :, f].rearrange("a (k p) n -> p (a k) n", p=P)
                    dst = raw[s][:, :].rearrange("p (k n) -> p k n", k=KD)
                sp.dma_start(dst, src).then_inc(e_full[s], 16)

            def load_step(x, t, j, e):
                load(x, t, "w1", j, e)
                load(x, t, "w3", j, e)
                load(x, t, "w2", j - 1, e)

            def load_head(x, e):
                load(x, 0, "w1", 0, e)
                load(x, 0, "w3", 0, e)
                load_step(x, 0, 1, e)

            load_head(0, 0)
            sp.wait_ge(sem["items_done"], 2)
            n_items = sp.value_load(n_items_t[0:1, 0:1], min_val=NE, max_val=ITEMS)
            with sp.Fori(0, n_items) as x:
                e = sp.value_load(item_e[0:1, bass.ds(x, 1)], min_val=0, max_val=NE - 1)
                load_step(x, 0, 2, e)
                with sp.Fori(0, 4) as t:
                    load_step(x, t, 3, e)
                    load_step(x, t, 4, e)
                e_next = sp.value_load(item_e[0:1, bass.ds(x + 1, 1)], min_val=0, max_val=NE - 1)
                load(x, 0, "w2", NCH - 1, e)
                load_head(x + 1, e_next)
            for n, (h, t) in enumerate(((0, 0), (0, 1), (1, 0), (1, 1))):
                sp.wait_ge(sem["fin_out"], n + 1)
                half = slice(h * 512, (h + 1) * 512)
                inc(sp.dma_start(out[0, t * P:(t + 1) * P, half], orow[:, t, half]), "x_out", 16)
            sp.wait_ge(sem["x_out"], 4 * 16)

        @block.gpsimd
        def _(pool):
            inc(nc.gpsimd.memset(zeros[:, :].bitcast(F32), 0.0), "memset_done")
            inc(nc.gpsimd.memset(smat[:, :, :].bitcast(F32), 0.0), "memset_done")
            inc(nc.gpsimd.memset(eps[:, :], EPS), "memset_done")
            inc(nc.gpsimd.memset(bdw[:, :, :, :, :], 0.0), "bd_zero")

            def load_block_diag(l):
                for kind, w in enumerate((lru_wa, lru_wx)):
                    for d in range(2):
                        for odd in range(2):
                            src = w[l, d, odd:NH:2, :, :].rearrange("c i j -> i c j")
                            dst = bdw[DH * odd:DH * (odd + 1), :, d, kind, DH * odd:DH * (odd + 1)]
                            inc(pool.dma_start(dst, src), "bd_in", 16)

            pool.wait_ge(sem["bd_zero"], 1)
            load_block_diag(0)

            counts = {"low": 0}

            def low(dst, hi, k):
                pool.wait_ge(sem["hH_done"], counts["low"] + 1)
                inc(nc.gpsimd.tensor_tensor(dst, h32[:, counts["low"] % 2, k], hi.bitcast(F32), ALU.subtract), "hL_done")
                counts["low"] += 1

            def norm_low(full):
                for k in range(KD):
                    low(hL[:, k, cols(full)], hH[:, k, cols(full)], cols(full))

            def conv(l):
                c_ = POOL_CHUNK
                v_ = pv[:, 0:C if l == 0 else C // 2]
                pool.wait_ge(sem["hL_done"], counts["low"])
                pool.wait_ge(sem["glu_done"], KL * l + c_ + 1)
                pool.wait_ge(sem["pad_zero"], 4 * (l + 1))
                for t in range(TAPS):
                    done = l * (2 * TAPS - 1) + 2 * t
                    g_, o_ = conv_part(l, c_, t, pool=True)
                    if t == 0:
                        inc(nc.gpsimd.tensor_scalar(o_, g_, tap(l, t, c_), layer_par(l, R_DWB + c_), ALU.mult, ALU.add), "pool_conv")
                    else:
                        pool.wait_ge(sem["pool_conv"], done - 1)
                        inc(nc.gpsimd.tensor_tensor(v_, g_, tap(l, t, c_).to_broadcast([P, C if l == 0 else C // 2]), ALU.mult), "pool_conv")
                        pool.wait_ge(sem["pool_conv"], done)
                        inc(nc.gpsimd.tensor_tensor(o_, o_, v_, ALU.add), "pool_conv")

            def diagonals(l):
                for m_, (t, c_) in enumerate(PE_CONV[l]):
                    if m_ < DIAGS:
                        pool.wait_ge(sem["hL_done"], counts["low"])
                    else:
                        pool.wait_ge(sem["pe_conv"], PE_BASE[l] + m_ - DIAGS + 1)
                    inc(nc.gpsimd.tensor_tensor(diag[:, m_ % DIAGS, :], K[:, K_ID:K_ID + P],
                                                tap(l, t, c_).to_broadcast([P, P]), ALU.mult), "diag_done")

            norm_low(0)
            for l in range(DEPTH):
                full = side(l, "x")
                conv(l)
                diagonals(l)
                if l == 0:
                    pool.wait_ge(sem["bd_mm"], 4 * KL)
                    load_block_diag(1)
                for k in range(KD):
                    low(hL[:, k, cols(full)], hH[:, k, cols(full)], cols(full))
                if l == 0:
                    norm_low(0)
                    for j in range(2 * sum(FFN_GROUPS)):
                        pool.wait_ge(sem["gH_done"], j + 1)
                        s = j % KD
                        inc(nc.gpsimd.tensor_tensor(gL[:, s, :], gt[:, j % 2, :], gH[:, s, :].bitcast(F32), ALU.subtract), "gL_done")
                    norm_low(0)

        @block.scalar
        def _(act):
            def copy(dst, src, scale=1.0):
                return nc.scalar.activation(dst, src, ACT.Copy, scale=scale)

            for at, src in ((R_C, c.rearrange("a (r p) -> (a r) p", p=P)), (R_CC, c_ctx.rearrange("(r p) -> r p", p=P)),
                            (R_FG, final_g.rearrange("(r p) -> r p", p=P))):
                inc(act.dma_start(prow[at:at + src.shape[0], 4, :], src), "misc_in", 16)
            for t in range(2):
                inc(act.dma_start(xrow[:, t, :], ctx[0, t * P:(t + 1) * P, :]), "x_in", 16)
                inc(act.dma_start(xrow[:, 2 + t, :], tokens_in[0, t * P:(t + 1) * P, :]), "x_in", 16)
            inc(act.dma_start(pos[:, :, :], pos_t.rearrange("(k p) n -> p k n", p=P)), "pos_in", 16)

            def hi(u):
                kind, a, _ = UNITS[u]
                if by_dve(UNITS[u]):
                    return
                n = unit_k(kind, a) * UC
                act.wait_ge(unit_full[u % RING], 16 * (u // RING + 1))
                if u >= RING:
                    act.wait_ge(sem["mm_done"], USED[u - RING])
                inc(copy(wh[u % RING][:, 0:n], raw[u % RING][:, 0:n]), "hi_done")

            cnt = dict(table=0, sq=0, h32=0)

            def squares(srcs):
                for src, n in srcs:
                    s = cnt["sq"]
                    if s >= 2:
                        act.wait_ge(sem["sum_mm"], s - 1)
                    inc(nc.scalar.activation(sq[:, s % 2, 0:n], src, ACT.Square), "sq_done")
                    cnt["sq"] += 1

            def sqrt_table():
                if cnt["table"]:
                    act.wait_ge(sem["table_in"], cnt["table"])
                inc(nc.scalar.activation(table[:, :], eps[:, :], ACT.Sqrt), "table_in")
                cnt["table"] += 1

            def round_h(dst, n_sel):
                act.wait_ge(sem["h32_done"], cnt["h32"] + 1)
                inc(copy(dst, h32[:, cnt["h32"] % 2, n_sel]), "hH_done")
                cnt["h32"] += 1

            def x_squares(l, which, full, ks):
                n = T if full == 0 else C
                for k in ks:
                    if (l, which) == (0, 1):
                        act.wait_ge(sem["x_ready"], 2 * (k + 1))
                    else:
                        act.wait_ge(sem["res_done"], RES[(l, which)] - KD + k + 1)
                    squares([(xT[:, :, k, :] if full == 0 else xT[:, 1, k, :], n)])

            def norm(l, which, full):
                n = T if full == 0 else C
                sqrt_table()
                x_squares(l, which, full, range(KD if (l, which) == (0, 1) else SUMMED, KD))
                act.wait_ge(sem["sum_mm"], cnt["sq"])
                r_ = rstd[:, 0:n]
                inc(nc.scalar.activation(r_, bank[B_ST][:, 0:n], ACT.Sqrt, scale=1.0 / D, bias=eps[:, 0:1]), "root_done")
                if (l, which) != (1, 2):
                    for k in range(KD):
                        round_h(hH[:, k, cols(full)], cols(full))

            def squares_behind(kind, a, i):
                if i and (kind == "wout" or (kind == "f2" and a == 2)):
                    if kind == "f2" and i == 1:
                        act.wait_ge(sem["gL_done"], 2 * sum(FFN_GROUPS))
                    l, which = (a, 2) if kind == "wout" else (1, 1)
                    x_squares(l, which, 1 if (l, which) == (1, 2) else 0, range(2 * i - 2, 2 * i))

            def row_out(l, q):
                n = l * 24 + q
                act.wait_ge(sem["mm_done"], MM[("ad", l, q)])
                if n >= 2:
                    act.wait_ge(sem["mt_mm"], n - 1)
                inc(copy(mrow[0:4, n % 2, :], bank[B_ROW][0:4, 0:UC]), "row_out")

            def gate_sigmoids(l, c_, kd):
                g_ = l * KL + c_
                if g_ > 0:
                    act.wait_ge(sem["scan_done" if kd else "root_in"], 2 * g_)
                for d in range(2):
                    act.wait_ge(sem["bd_mm"], 4 * g_ + 2 * kd + d + 1)
                    b_ = layer_par(l, (R_BA, R_BX)[kd] + d * KL + c_)
                    inc(nc.scalar.activation((rg, ig)[kd][:, d, :], bank[B_GATE[d]][:, :], ACT.Sigmoid, bias=b_), "sig_done")

            def decays(l, c_):
                g_ = l * KL + c_
                act.wait_ge(sem["decay_done"], DECAY_ALL)
                act.wait_ge(sem["sig_done"], 4 * g_ + 2)
                for d in range(2):
                    inc(nc.scalar.activation(gate_r[:, d, :], rg[:, d, :], ACT.Exp,
                                             scale=spn[:, l, 0, d * KL + c_:d * KL + c_ + 1]), "act_step")
                act.wait_ge(sem["act_step"], 6 * g_ + 2)
                for d in range(2):
                    inc(nc.scalar.activation(rg[:, d, :], rg[:, d, :], ACT.Tanh,
                                             scale=spn[:, l, 1, d * KL + c_:d * KL + c_ + 1]), "act_step")
                if g_ > 0:
                    act.wait_ge(sem["lru_done"], g_)
                for d in range(2):
                    inc(nc.scalar.activation(root[:, d, :], gate_r[:, d, :], ACT.Square), "act_step")
                for d in range(2):
                    act.wait_ge(sem["root_in"], 2 * g_ + d + 1)
                    inc(nc.scalar.activation(root[:, d, :], root[:, d, :], ACT.Sqrt), "root_done")

            def mix(l):
                full = side(l, "x")
                n = cols(full)
                for c_ in range(KL):
                    round_h(hH[:, c_, n], n)
                w = T if full == 0 else C
                sqrt_table()
                act.wait_ge(sem["ln_step"], LN_STEPS * l + KL)
                squares([((cv[:, c_, :, :] if full == 0 else cv[:, c_, 1, :]), w) for c_ in range(KL)])
                act.wait_ge(sem["sum_mm"], cnt["sq"])
                inc(nc.scalar.activation(rstd[:, 0:w], bank[B_ST][:, 0:w], ACT.Sqrt, scale=1.0 / DL, bias=eps[:, 0:1]), "root_done")
                for c_ in range(KL):
                    act.wait_ge(sem["ln_step"], LN_STEPS * l + KL + 1 + c_ + 1)
                    k = cnt["h32"]
                    act.wait_ge(sem["hL_done"], k - 1)
                    src = cv[:, c_, :, :] if full == 0 else cv[:, c_, 1, :]
                    inc(nc.scalar.activation(h32[:, k % 2, n], src, ACT.Silu, scale=layer_par(l, R_LNG + c_),
                                             bias=layer_par(l, R_LNB + c_)), "h32_done")
                    round_h(hH[:, KL + c_, n], n)

            act.wait_ge(sem["misc_ready"], 1)
            inc(nc.scalar.activation(sv[:, :], par[:, 4, R_C:R_CC + KD], ACT.Silu), "silu_ready")
            act.wait_ge(sem["silu_ready"], 1)
            act.wait_ge(sem["memset_done"], 3)
            for v_ in range(2):
                inc(copy(smat[:, :, v_], sv[:, v_ * KD:(v_ + 1) * KD]), "cols_ready")
            hi(0)
            hi(1)
            for u, (kind, a, i) in enumerate(UNITS):
                if u + 2 < NU:
                    hi(u + 2)
                if kind == "ad" and a == 0 and KD // 2 <= i < KD:
                    x_squares(0, 1, 0, range(2 * i - KD, 2 * i - KD + 2))
                if u == AT[("ad", 0, KD)]:
                    act.wait_ge(sem["params_ready"], len(ROW_PARTS))
                    for l in range(DEPTH):
                        inc(nc.scalar.activation(sp_t[:, l, :], layer_par(l, R_LAM, 8), ACT.Abs), "decay_done")
                    act.wait_ge(sem["decay_done"], 2)
                    for l in range(DEPTH):
                        inc(nc.scalar.activation(sp_t[:, 2 + l, :], sp_t[:, l, :], ACT.Exp, scale=-1.0), "decay_exp")
                if kind == "win" and i == 0:
                    norm(a, 1, 0)
                for l, c_ in lru_at(u, 1):
                    gate_sigmoids(l, c_, 1)
                if kind == "ad" and a == 0:
                    row_out(a, i)
                for l, c_ in lru_at(u, 1):
                    decays(l, c_)
                if kind == "wout" and i == 0:
                    mix(a)
                if kind == "f1" and i == 0:
                    norm(0, 2, 0)
                if kind == "win" and win_kind(i) == "values" and i in LRU_AT:
                    gate_sigmoids(a, LRU_AT[i], 0)
                if kind == "win" and win_kind(i) != "values":
                    full = side(a, "rec" if win_kind(i) == "rec" else "x")
                    n = T if full == 0 else C
                    for h in range(2):
                        t = 2 * i + h
                        c_ = win_chunk(t)
                        act.wait_ge(sem["mm_done"], MM[("win", a, t)])
                        b_ = bank[t % WIN_BANKS][:, 0:n]
                        if win_kind(i) == "gates":
                            dst = cv[:, c_, :, :] if full == 0 else cv[:, c_, 1, :]
                            inc(nc.scalar.activation(dst, b_, ACT.Sigmoid), "gates_done")
                        elif win_kind(i) == "rec":
                            if c_ >= 2:
                                act.wait_ge(sem["rconv_done"], RTAPS * (KL * a + 2))
                            inc(copy(rpad[:, c_ % 2, :, RPL:RPL + C], b_.rearrange("p (s n) -> p s n", s=2)), "rec_done")
                        else:
                            inc(nc.scalar.activation(gg[:, c_, cols(full)], b_, ACT.Gelu_apprx_tanh), "gelu_done")
                        if h == 0 and i in LRU_AT:
                            gate_sigmoids(a, LRU_AT[i], 0)
                squares_behind(kind, a, i)
                if kind == "f3":
                    for h in range(2):
                        j = 2 * i + h
                        act.wait_ge(sem["mm_done"], MM[("f1", a if kind == "f3" else 0, j)])
                        if j >= 4:
                            act.wait_ge(sem["g_prod"], j - 3)
                        inc(nc.scalar.activation(sg[:, j % 4, :], bank[h][:, :], ACT.Silu), "silu_out")
                    for h in range(2):
                        j = 2 * i + h
                        act.wait_ge(sem["g_prod"], j + 1)
                        if j % KD == 0 and j:
                            act.wait_ge(sem["mm_done"], MM[("f2", j // KD - 1, 7)])
                        inc(copy(gH[:, j % KD, :], gt[:, j % 2, :]), "gH_done")

            norm(1, 2, 1)
            for t in range(2):
                act.wait_ge(sem["route_step"], 4)
                inc(nc.scalar.activation(pr[:, t, :], lg[:, t, :], ACT.Exp, bias=col[:, t, 0:1]), "route_exp")
            for f in range(4):
                act.wait_ge(sem["tok_tr"], f + 1)
                inc(copy(ftH[:, f // 2, (f % 2) * 512:(f % 2 + 1) * 512], bank[B_TOK[f]][:, :]), "tokH")

            def gather_out(g):
                for q in range(2):
                    act.wait_ge(sem["gather_mm"], g * 2 + q + 1)
                    inc(copy(xeH[:, 4 * q:4 * q + 4, :], bank[B_G + q][:, :].rearrange("p (k n) -> p k n", k=4)), "xe_hi")

            def e_hi(x, t, kind, j):
                s = slot(kind, j)
                act.wait_ge(e_full[s], (x * uses(j) + t + (j // 2 + 1)) * 16)
                act.wait_ge(sem["e_used"], x * EUNITS + t * 6 + before(kind, j) + 1 + CREDIT)
                inc(copy(wh[s][:, :], raw[s][:, :]), "e_hi")

            def e_silu(x, t, j):
                act.wait_ge(sem["e_used"], x * EUNITS + t * 6 + order("w3", j) + 1 + CREDIT)
                inc(nc.scalar.activation(esg[:, :], bank[B_H + j % 2][:, 0:UC], ACT.Silu), "e_silu")

            def e_gh(x, t, j):
                act.wait_ge(sem["g_tr"], x * NCH + t * 2 + j + 1)
                inc(copy(egH[:, :], bank[B_T][:, 0:UC]), "e_gH")

            def e_step(x, t, j):
                if j < NCH - 1:
                    e_hi(x, t, "w1", j + 1)
                if j == 0:
                    for h in range(2):
                        act.wait_ge(sem["e_used"], x * EUNITS + CREDIT)
                        inc(copy(yH[:, h, :], bank[B_Y + h][:, :], scale=cs[:, 0:1]), "y_hi")
                else:
                    e_gh(x, t, j - 1)
                if j < NCH - 1:
                    e_hi(x, t, "w3", j + 1)
                e_silu(x, t, j)
                e_hi(x, t, "w2", j)

            e_hi(0, 0, "w1", 0)
            e_hi(0, 0, "w3", 0)
            act.wait_ge(sem["acc_done"], 4)
            gather_out(0)
            act.wait_ge(sem["items_done"], 2)
            n_items = act.value_load(n_items_t[0:1, 0:1], min_val=NE, max_val=ITEMS)
            with act.Fori(0, n_items) as x:
                e_step(x, 0, 0)
                e_step(x, 0, 1)
                e_step(x, 0, 2)
                act.wait_ge(sem["pick_mm"], x * 2 + 1)
                inc(copy(pickT[:, :], bank[B_G][:, 0:S]), "pickT_done")
                with act.Fori(0, 3) as t:
                    e_step(x, t, 3)
                    e_step(x, t, 4)
                e_step(x, 0, NCH - 2)
                e_step(x, 0, NCH - 1)
                e_hi(x + 1, 0, "w1", 0)
                e_gh(x, 0, NCH - 1)
                gather_out(x + 1)
                e_hi(x + 1, 0, "w3", 0)
            for h in range(2):
                act.wait_ge(sem["e_used"], n_items * EUNITS + CREDIT)
                inc(copy(yH[:, h, :], bank[B_Y + h][:, :], scale=cs[:, 0:1]), "y_hi")
            sqrt_table()
            for k in range(KD):
                act.wait_ge(sem["acc_done"], n_items * 8 + 4 + k + 1)
                squares([(xT[:, 1, k, :], S)])
            act.wait_ge(sem["sum_mm"], cnt["sq"])
            inc(nc.scalar.activation(rstd[:, 0:S], bank[B_H][:, 0:S], ACT.Sqrt, scale=1.0 / D, bias=eps[:, 0:1]), "root_done")
            for n, (h, t) in enumerate(((0, 0), (0, 1), (1, 0), (1, 1))):
                act.wait_ge(sem["fin_tr"], n + 1)
                inc(copy(orow[:, t, h * 512:(h + 1) * 512], bank[2 * t + h][:, :]), "fin_out")

        @block.vector
        def _(dve):
            V = nc.vector
            state = dict(step=0, h32=0, mod=0, norm=0, scaled=0)

            def step(ins):
                inc(ins, "dve_step")
                state["step"] += 1
                dve.wait_ge(sem["dve_step"], state["step"])

            dve.wait_ge(sem["misc_t"], 1)
            inc(V.tensor_copy(par[:, 4, 0:R_MEND], bank[B_MISC][:, 0:R_MEND]), "misc_ready")
            dve.wait_ge(sem["misc_ready"], 1)
            dve.wait_ge(sem["silu_ready"], 1)
            dve.wait_ge(sem["cols_ready"], 2)
            for v_ in range(2):
                inc(V.tensor_tensor(smat[:, :, 2 + v_], sv[:, v_ * KD:(v_ + 1) * KD],
                                    smat[:, :, v_].bitcast(F32), ALU.subtract), "cols_ready")
            inc(V.tensor_copy(fg[:, :], par[:, 4, R_FG:R_FG + KD]), "cols_ready")
            def mod_sums(u):
                _, l, q = UNITS[u]
                s, slot_, vectors = u % RING, q % 2, range(mod_vectors(l, q))
                dve.wait_ge(unit_full[s], 16 * (u // RING + 1))
                if q >= 2:
                    dve.wait_ge(sem["mt_mm"], 24 * l + q - 1)
                for k in range(KD):
                    w_ = raw[s][:, k * UC:(k + 1) * UC]
                    for v_ in vectors:
                        o_ = macc[:, slot_, v_, :]
                        s_ = sv[:, v_ * KD + k:v_ * KD + k + 1]
                        if k == 0:
                            ins = V.tensor_scalar(o_, w_, s_, None, ALU.mult)
                        else:
                            dve.wait_ge(sem["mod_step"], state["mod"] - len(vectors) + 1 + (v_ if k == KD - 1 else 0))
                            ins = V.scalar_tensor_tensor(o_, w_, s_, o_, ALU.mult, ALU.add)
                        if k < KD - 1:
                            inc(ins, "mod_step")
                            state["mod"] += 1
                        else:
                            inc(ins, "lo_done" if v_ == vectors[-1] else "mod_sum0")

            def lo(u):
                kind, a, _ = UNITS[u]
                n = unit_k(kind, a) * UC
                s = u % RING
                if by_dve(UNITS[u]):
                    return mod_sums(u)
                dve.wait_ge(sem["hi_done"], HI[u])
                inc(V.tensor_tensor(wl[s][:, 0:n], raw[s][:, 0:n], wh[s][:, 0:n].bitcast(F32), ALU.subtract), "lo_done")

            def tokens(ks):
                for k in ks:
                    dve.wait_ge(sem["x_tr"], k + 1)
                    if k == 0:
                        dve.wait_ge(sem["pos_in"], 16)
                    b_ = bank[k % 4]
                    inc(V.tensor_copy(xT[:, 0, k, :], b_[:, 0:C]), "x_ready")
                    inc(V.tensor_tensor(xT[:, 1, k, :], b_[:, C:T], pos[:, k, :], ALU.add), "x_ready")

            def params():
                for n, (tile, rows_) in enumerate(ROW_PARTS):
                    dve.wait_ge(sem["params_t"], n + 1)
                    inc(V.tensor_copy(par[:, tile, 0:rows_], bank[n][:, 0:rows_]), "params_ready")
                dve.wait_ge(sem["params_ready"], len(ROW_PARTS))

            def decay_rates(l):
                dve.wait_ge(sem["decay_exp"], l + 1)
                z, z2, p_ = sp_t[:, l, :], spn[:, l, 0, :], spn[:, l, 1, :]
                v_ = sp_t[:, 2 + l, :]
                step(V.tensor_scalar(z, v_, 2.0, None, ALU.add))
                step(V.reciprocal(z, z))
                step(V.tensor_tensor(z, z, v_, ALU.mult))
                step(V.tensor_tensor(z2, z, z, ALU.mult))
                step(V.tensor_scalar(p_, z2, 1.0 / 17, 1.0 / 15, ALU.mult, ALU.add))
                for o in (13, 11, 9, 7, 5, 3, 1):
                    step(V.tensor_tensor(p_, p_, z2, ALU.mult))
                    step(V.tensor_scalar(p_, p_, 1.0 / o, None, ALU.add))
                step(V.tensor_tensor(p_, p_, z, ALU.mult))
                step(V.tensor_scalar(z, layer_par(l, R_LAM, 8), -1.0, 0.0, ALU.mult, ALU.max))
                step(V.scalar_tensor_tensor(z, p_, 2.0, z, ALU.mult, ALU.add))
                inc(V.tensor_scalar(spn[:, l, 0, :], z, -LRU_C, None, ALU.mult), "decay_done")
                inc(V.tensor_scalar(spn[:, l, 1, :], z, LRU_C, None, ALU.mult), "decay_done")

            def mods(l, part):
                a, b = ((0, 2 * KD), (2 * KD, NMOD * KD), (0, NMOD * KD))[part]
                dve.wait_ge(sem["mt_mm"], 24 * l + (8 if part == 0 else 24))
                ps = bank[B_MT][:, 0:2 * NMOD * KD].rearrange("p (m v) -> p m v", v=2)
                for v_ in range(2):
                    if l == 1 and v_ == 1:
                        b = 2 * KD
                    inc(V.tensor_tensor(mt[l][:, a:b, v_], ps[:, a:b, v_], layer_par(l, R_BMOD + a, b - a), ALU.add), "mod_ready")

            def norm(l, which, full):
                n = T if full == 0 else C
                sh, sc = (0, KD) if which == 1 else (3 * KD, 4 * KD)
                g_ = layer_par(l, R_N1 if which == 1 else R_N2, KD)
                if which == 1:
                    if l == 0:
                        mods(0, 0)
                    dve.wait_ge(sem["mod_ready"], 4 * l + 2)
                else:
                    dve.wait_ge(sem["mod_ready"], 4 + 2 * l)
                for v_ in range(mod_vectors(l, (which - 1) * 3 * KD // 2)):
                    step(V.scalar_tensor_tensor(amp[:, :, v_], mt[l][:, sc:sc + KD, v_], 1.0, g_, ALU.add, ALU.mult))
                dve.wait_ge(sem["root_done"], ROOT[(l, which)])
                step(V.reciprocal(rstd[:, 0:n], rstd[:, 0:n]))
                base, last = state["norm"], (l, which) == (1, 2)

                def buffer(k):
                    return norm_t[:, (0, 1, 3)[k % 3], :]

                def scaled(k):
                    src = xT[:, :, k, :] if full == 0 else xT[:, 1, k, :]
                    r_ = rstd[:, 0:n].rearrange("p (s n) -> p s n", s=2) if full == 0 else rstd[:, 0:n]
                    t_ = buffer(k)[:, 0:n].rearrange("p (s n) -> p s n", s=2) if full == 0 else buffer(k)[:, 0:n]
                    if k >= 3:
                        if last:
                            dve.wait_ge(sem["fT_done"], k - 2)
                        else:
                            dve.wait_ge(sem["h32_done"], state["h32"] - 1)
                            dve.wait_ge(sem["ctx_done"], base + k - 2)
                    inc(V.tensor_tensor(t_, src, r_, ALU.mult), "scaled")
                    state["scaled"] += 1

                scaled(0)
                for k in range(KD):
                    t_ = buffer(k)
                    if k + 1 < KD:
                        scaled(k + 1)
                    dve.wait_ge(sem["scaled"], state["scaled"] - (k + 1 < KD))
                    if last:
                        inc(V.tensor_scalar(fT[:, k, :], t_[:, 0:n], amp[:, k, 0:1], mt[l][:, sh + k, 0:1], ALU.mult, ALU.add), "fT_done")
                        continue
                    m_ = state["h32"]
                    if m_ >= 2:
                        dve.wait_ge(sem["hL_done"], m_ - 1)
                    inc(V.tensor_scalar(h32[:, m_ % 2, 0:C], t_[:, 0:C], amp[:, k, 1:2], mt[l][:, sh + k, 1:2], ALU.mult, ALU.add), "ctx_done")
                    state["norm"] += 1
                    inc(V.tensor_scalar(h32[:, m_ % 2, C:T], t_[:, C:T], amp[:, k, 0:1], mt[l][:, sh + k, 0:1], ALU.mult, ALU.add), "h32_done")
                    state["h32"] += 1

            def conv(l, a, b):
                for m_ in range(a, min(b, len(DVE_CONV[l]))):
                    t, c_ = DVE_CONV[l][m_]
                    base = DVE_BASE[l]
                    if t == 0:
                        dve.wait_ge(sem["glu_done"], KL * l + c_ + 1)
                    g_, o_ = conv_part(l, c_, t)
                    if t == 0:
                        inc(V.tensor_scalar(o_, g_, tap(l, t, c_), layer_par(l, R_DWB + c_), ALU.mult, ALU.add), "conv_step")
                    else:
                        dve.wait_ge(sem["conv_step"], base + m_)
                        inc(V.scalar_tensor_tensor(o_, g_, tap(l, t, c_), o_, ALU.mult, ALU.add), "conv_step")

            def rec_conv(l, pair):
                dve.wait_ge(sem["rec_done"], KL * l + 2 * pair + 2)
                dve.wait_ge(sem["pad_zero"], 4 * (l + 1))
                for t in range(RTAPS):
                    for h in range(2):
                        c_ = 2 * pair + h
                        src = rpad[:, h, :, t:t + C]
                        dst = rc[:, c_, :].rearrange("p (s n) -> p s n", s=2)
                        w_ = layer_par(l, R_CW + t * KL + c_)
                        if t == 0:
                            inc(V.tensor_scalar(dst, src, w_, layer_par(l, R_CB + c_), ALU.mult, ALU.add), "rconv_done")
                        else:
                            dve.wait_ge(sem["rconv_done"], RTAPS * (KL * l + 2 * pair) + 2 * (t - 1) + h + 1)
                            inc(V.scalar_tensor_tensor(dst, src, w_, dst, ALU.mult, ALU.add), "rconv_done")

            def scan_inputs(l, c_):
                g_ = l * KL + c_
                for d in range(2):
                    dve.wait_ge(sem["sig_done"], 4 * g_ + 3 + d)
                    inc(V.tensor_tensor(ig[:, d, :], ig[:, d, :], rc[:, c_, :], ALU.mult), "ig_done")
                for d in range(2):
                    dve.wait_ge(sem["act_step"], 6 * g_ + 5 + d)
                    inc(V.scalar_tensor_tensor(root[:, d, :], root[:, d, :], 1.0, rg[:, d, :], ALU.add, ALU.mult), "root_in")

            def recurrence(l, c_):
                n = cols(side(l, "x"))
                g_ = l * KL + c_
                for d in range(2):
                    dve.wait_ge(sem["root_done"], ROOT[("mix", l)] + 2 * c_ + d + 1)
                    dve.wait_ge(sem["ig_done"], 2 * g_ + d + 1)
                    step(V.tensor_tensor(ig[:, d, :], ig[:, d, :], root[:, d, :], ALU.mult))
                inc(V.tensor_tensor_scan(yy[:, c_, :], gate_r[:, 0, :], ig[:, 0, :], 0.0, ALU.mult, ALU.add), "scan_done")
                step(V.tensor_tensor_scan(root[:, 1, 0:C][:, ::-1], gate_r[:, 1, 0:C][:, ::-1], ig[:, 1, 0:C][:, ::-1], 0.0, ALU.mult, ALU.add))
                inc(V.tensor_tensor_scan(root[:, 1, C:T][:, ::-1], gate_r[:, 1, C:T][:, ::-1], ig[:, 1, C:T][:, ::-1], root[:, 1, 0:1], ALU.mult, ALU.add), "scan_done")
                dve.wait_ge(sem["scan_done"], 2 * g_ + 2)
                inc(V.tensor_tensor(yy[:, c_, n], yy[:, c_, n], root[:, 1, n], ALU.add), "lru_done")

            def mix(l, conv_at):
                full = side(l, "x")
                n = cols(full)
                dve.wait_ge(sem["lru_done"], KL * (l + 1))
                dve.wait_ge(sem["pe_conv"], PE_BASE[l + 1])
                dve.wait_ge(sem["pool_conv"], (l + 1) * (2 * TAPS - 1))
                for c_ in PE_CHUNKS[l]:
                    o_ = cv[:, c_, :, :] if full == 0 else cv[:, c_, 1, :]
                    b_ = bank[pe_bank(c_)]
                    b_ = b_[:, :].rearrange("p (s n) -> p s n", s=2) if full == 0 else b_[:, 0:C]
                    inc(V.tensor_scalar(o_, b_, layer_par(l, R_DWB + c_), None, ALU.add), "pe_conv_out")
                for c_ in range(KL):
                    m_ = state["h32"]
                    if m_ >= 2:
                        dve.wait_ge(sem["hL_done"], m_ - 1)
                    dve.wait_ge(sem["gelu_done"], KL * l + c_ + 1)
                    inc(V.tensor_tensor(h32[:, m_ % 2, n], yy[:, c_, n], gg[:, c_, n], ALU.mult), "h32_done")
                    state["h32"] += 1
                conv(l, conv_at, len(DVE_CONV[l]))
                dve.wait_ge(sem["conv_step"], DVE_BASE[l + 1])
                dve.wait_ge(sem["pool_conv"], (l + 1) * (2 * TAPS - 1))
                dve.wait_ge(sem["pe_conv_out"], sum(len(w) for w in PE_CHUNKS[:l + 1]))
                dve.wait_ge(sem["ln_mm"], l + 1)
                w = T if full == 0 else C

                def sel(c_):
                    return cv[:, c_, :, :] if full == 0 else cv[:, c_, 1, :]

                def two(ap):
                    return ap.rearrange("p (s n) -> p s n", s=2) if full == 0 else ap

                for c_ in range(KL):
                    inc(V.scalar_tensor_tensor(sel(c_), two(bank[B_ST][:, 0:w]), -1.0 / DL, sel(c_), ALU.mult, ALU.add), "ln_step")
                dve.wait_ge(sem["root_done"], ROOT[("ln", l)])
                inc(V.reciprocal(rstd[:, 0:w], rstd[:, 0:w]), "ln_step")
                dve.wait_ge(sem["ln_step"], LN_STEPS * l + KL + 1)
                for c_ in range(KL):
                    inc(V.tensor_tensor(sel(c_), sel(c_), two(rstd[:, 0:w]), ALU.mult), "ln_step")
                state["h32"] += KL

            def residual(l, k, b_, full, gate):
                if full == 0:
                    step(V.scalar_tensor_tensor(xT[:, 0, k, :], b_[:, 0:C], mt[l][:, gate + k, 1:2], xT[:, 0, k, :], ALU.mult, ALU.add))
                lat = b_[:, C:T] if full == 0 else b_[:, 0:C]
                inc(V.scalar_tensor_tensor(xT[:, 1, k, :], lat, mt[l][:, gate + k, 0:1], xT[:, 1, k, :], ALU.mult, ALU.add), "res_done")

            lo(0)
            lo(1)
            conv_at = 0
            for u, (kind, a, i) in enumerate(UNITS):
                if u + 2 < NU:
                    lo(u + 2)
                if kind == "ad" and a == 0 and i < KD // 2:
                    tokens((2 * i, 2 * i + 1))
                if kind == "ad" and a == 0 and i == KD - 1:
                    params()
                if kind == "ad" and a == 0 and i in (KD + 1, KD + 2):
                    decay_rates(i - KD - 1)
                if kind == "win" and i == 0:
                    norm(a, 1, 0)
                    conv_at = 0
                    inc(V.memset(glu[:, :, :, 0:PAD], 0.0), "pad_zero")
                    inc(V.memset(glu[:, :, :, PAD + C:GW], 0.0), "pad_zero")
                    inc(V.memset(rpad[:, :, :, 0:RPL], 0.0), "pad_zero")
                    inc(V.memset(rpad[:, :, :, RPL + C:RW], 0.0), "pad_zero")
                if kind == "wout" and i == 0:
                    for l, c_ in lru_at(u, 1 if a else 2):
                        if (l, c_) in lru_at(u, 1):
                            scan_inputs(l, c_)
                        recurrence(l, c_)
                    mix(a, conv_at)
                elif a == 0:
                    for l, c_ in lru_at(u, 2):
                        recurrence(l, c_)
                if u and UNITS[u - 1][0] == "win" and win_kind(UNITS[u - 1][2]) == "rec":
                    rec_conv(UNITS[u - 1][1], WIN[UNITS[u - 1][2]][1])
                if kind == "f1" and i == 0:
                    norm(0, 2, 0)
                if kind == "win" and win_kind(i) == "values":
                    full = side(a, "x")
                    n = T if full == 0 else C
                    for h in range(2):
                        t = 2 * i + h
                        c_ = win_chunk(t)
                        dve.wait_ge(sem["mm_done"], MM[("win", a, t)])
                        dve.wait_ge(sem["gates_done"], KL * a + c_ + 1)
                        b_ = bank[t % WIN_BANKS][:, 0:n]
                        if full == 0:
                            inc(V.tensor_tensor(glu[:, c_, :, PAD:PAD + C], b_.rearrange("p (s n) -> p s n", s=2), cv[:, c_, :, :], ALU.mult), "glu_done")
                        else:
                            inc(V.tensor_tensor(glu[:, c_, 1, PAD:PAD + C], b_, cv[:, c_, 1, :], ALU.mult), "glu_done")
                    if i == 1:
                        dve.wait_ge(sem["pad_zero"], 4 * (a + 1))
                if kind == "wout":
                    full = side(a, "x")
                    for h in range(2):
                        k = 2 * i + h
                        if k == 0 and a == 0:
                            mods(0, 1)
                        if k == 0:
                            dve.wait_ge(sem["mod_ready"], 4 + 2 * a)
                        dve.wait_ge(sem["mm_done"], MM[("wout", a, k)])
                        residual(a, k, bank[k % MM_BANKS], full, 2 * KD)
                if kind == "f3":
                    for h in range(2):
                        j = 2 * i + h
                        dve.wait_ge(sem["mm_done"], MM[("f3", a, j)])
                        dve.wait_ge(sem["silu_out"], j + 1)
                        if j >= 2:
                            dve.wait_ge(sem["gL_done"], j - 1)
                        inc(V.tensor_tensor(gt[:, j % 2, :], sg[:, j % 4, :], bank[2 + h][:, :], ALU.mult), "g_prod")
                if kind == "f2":
                    for h in range(2):
                        k = 2 * i + h
                        dve.wait_ge(sem["mm_done"], MM[("f2", a, k)])
                        residual(0, k, bank[k % MM_BANKS], 0, 5 * KD)
                if kind == "ad" and a == 1 and i == 23:
                    mods(1, 2)
                if kind != "wout":
                    for l, c_ in lru_at(u, 1):
                        scan_inputs(l, c_)
                for lay, more in enumerate(DVE_ITEMS):
                    if AT[("win", lay, 1)] < u < AT[("wout", lay, 0)]:
                        most = 2 * TAPS if u < AT[("win", lay, 4)] else len(DVE_CONV[lay])
                        to = min(conv_at + more, most)
                        conv(lay, conv_at, to)
                        conv_at = max(conv_at, to)
                if kind != "wout" and a == 1:
                    for l, c_ in lru_at(u, 1):
                        recurrence(l, c_)

            inc(V.memset(col[:, 0, 6:7], 0.0), "e_lo", CREDIT)
            norm(1, 2, 1)
            rs = {"n": 0}

            def rsteps(*all_ins):
                for ins in all_ins:
                    inc(ins, "route_step")
                    rs["n"] += 1
                dve.wait_ge(sem["route_step"], rs["n"])

            dve.wait_ge(sem["fT_done"], KD)
            for zero in (egH, egL, pickT):
                inc(V.memset(zero[:, :].bitcast(F32), 0.0), "acc_done")
            inc(V.memset(cs[:, :], 0.0), "acc_done")
            dve.wait_ge(sem["logits_mm"], 1)
            rsteps(*[V.tensor_copy(lg[:, t, :], bank[t][:, 0:NE]) for t in range(2)])
            rsteps(V.tensor_reduce(col[:, :, 0:1], lg[:, :, :], axis=AX.X, op=ALU.max))
            rsteps(V.tensor_scalar(col[:, :, 0:1], col[:, :, 0:1], -1.0, None, ALU.mult))
            rsteps(V.memset(tab[:, :, 0, :], 4 * FAR))
            dve.wait_ge(sem["route_exp"], 2)
            rsteps(V.tensor_reduce(col[:, :, 1:2], pr[:, :, :], axis=AX.X, op=ALU.add))
            rsteps(V.reciprocal(col[:, :, 1:2], col[:, :, 1:2]))
            rsteps(V.memset(tab[:, :, 1, :], 0.0))
            two = range(2)
            rsteps(*[V.tensor_scalar(pr[:, t, :], pr[:, t, :], col[:, t, 1:2], None, ALU.mult) for t in two])
            rsteps(*[V.max(top[:, t, :], pr[:, t, :]) for t in two])
            rsteps(*[V.max_index(tix[:, t, :], top[:, t, :], pr[:, t, :]) for t in two],
                   V.tensor_tensor(col[:, :, 2:3], top[:, :, 0:1], top[:, :, 1:2], ALU.add))
            rsteps(V.tensor_copy(tif[:, :, :], tix[:, :, :]), V.reciprocal(col[:, :, 2:3], col[:, :, 2:3]))
            rsteps(*[V.tensor_scalar(oh[:, t, j, :], K[:, K_IOTA8:K_IOTA8 + NE], tif[:, t, j:j + 1], None, ALU.is_equal)
                     for t in two for j in range(2)])
            rsteps(V.tensor_tensor(mask[:, :, :], oh[:, :, 0, :], oh[:, :, 1, :], ALU.add))
            assert rs["n"] == ROUTE_MASKS, rs["n"]
            rsteps(*[V.tensor_scalar(col[:, t, 4:6], top[:, t, 0:2], col[:, t, 2:3], None, ALU.mult) for t in two],
                   V.tensor_scalar(lg[:, :, :], mask[:, :, :], -FAR, FAR, ALU.mult, ALU.add))
            rsteps(*[V.tensor_scalar(oh[:, t, 0, :], oh[:, t, 0, :], col[:, t, 4:5], None, ALU.mult) for t in two])
            rsteps(*[V.scalar_tensor_tensor(tab[:, t, 1, 0:NE], oh[:, t, 1, :], col[:, t, 5:6], oh[:, t, 0, :],
                                            ALU.mult, ALU.add) for t in two])
            for f in range(4):
                dve.wait_ge(sem["tokH"], f + 1)
                half = slice((f % 2) * 512, (f % 2 + 1) * 512)
                inc(V.tensor_tensor(ftL[:, f // 2, half], bank[B_TOK[f]][:, :], ftH[:, f // 2, half].bitcast(F32), ALU.subtract), "tokL")
            dve.wait_ge(sem["pos_mm"], 1)
            rsteps(*[V.tensor_tensor(tab[:, t, 0, 0:NE], bank[0][:, t * NE:(t + 1) * NE], lg[:, t, :], ALU.add) for t in two])

            def picks(g):
                inc(V.tensor_copy(cur[:, :, :, :].rearrange("p t k e -> p (t k) e"),
                                  tab[:, :, :, bass.ds(g, 1)].rearrange("p t k e -> p (t k) e")), "pick_done")
                dve.wait_ge(sem["pick_done"], g * 3 + 1)
                for t in range(2):
                    inc(V.tensor_scalar(pick[:, t, :], K[:, K_IOTA:K_IOTA + CAP], cur[:, t, 0, :], None, ALU.is_equal), "pick_done")

            picks(0)
            rsteps(V.tensor_scalar(over[:, 0, :], bank[0][:, 2 * NE:3 * NE], CAP + 0.5, None, ALU.is_gt))
            rsteps(V.memset(onesf[:, :], 1.0))
            rsteps(V.tensor_tensor_scan(over[:, 1, :], onesf[:, :], over[:, 0, :], 0.0, ALU.mult, ALU.add))
            rsteps(V.memset(item_f[:, :], 0.0))
            rsteps(V.tensor_copy(item_f[:, 0:NE], K[:, K_IOTA8:K_IOTA8 + NE]))
            for m_ in range(MORE):
                it_ = slice(NE + m_, NE + m_ + 1)
                rsteps(V.scalar_tensor_tensor(sel[:, 0, :], over[:, 1, :], float(m_ + 1), over[:, 0, :], ALU.is_equal, ALU.mult))
                rsteps(V.tensor_tensor(sel[:, 1, :], sel[:, 0, :], K[:, K_IOTA8:K_IOTA8 + NE], ALU.mult))
                rsteps(V.tensor_reduce(item_f[:, it_], sel[:, 1, :], axis=AX.X, op=ALU.add))
                kinds = [(t, kd) for t in two for kd in range(2)]
                rsteps(*[V.tensor_tensor(oh[:, t, kd, :], sel[:, 0, :], tab[:, t, kd, 0:NE], ALU.mult) for t, kd in kinds])
                rsteps(*[V.tensor_reduce(tab[:, t, kd, it_], oh[:, t, kd, :], axis=AX.X, op=ALU.add) for t, kd in kinds])
                rsteps(V.tensor_scalar(tab[:, :, 0, it_], tab[:, :, 0, it_], -float(CAP), None, ALU.add))
            rsteps(V.tensor_scalar(num_f[:, :], over[:, 1, NE - 1:NE], float(NE), None, ALU.add))
            inc(V.tensor_copy(item_e[:, :], item_f[:, :]), "items_done")
            inc(V.tensor_copy(n_items_t[:, :], num_f[:, :]), "items_done")
            assert rs["n"] == ROUTE_ALL, rs["n"]
            def gather_out(g):
                for q in range(2):
                    dve.wait_ge(sem["xe_hi"], g * 2 + q + 1)
                    xs = slice(4 * q, 4 * q + 4)
                    inc(V.tensor_tensor(xeL[:, xs, :], bank[B_G + q][:, :].rearrange("p (k n) -> p k n", k=4),
                                        xeH[:, xs, :].bitcast(F32), ALU.subtract), "xe_lo")

            def e_lo(x, t, kind, j):
                s = slot(kind, j)
                dve.wait_ge(sem["e_hi"], x * EUNITS + t * 6 + order(kind, j) + 1)
                inc(V.tensor_tensor(wl[s][:, :], raw[s][:, :], wh[s][:, :].bitcast(F32), ALU.subtract), "e_lo")

            def e_prod(x, t, j):
                dve.wait_ge(sem["e_silu"], x * NCH + t * 2 + j + 1)
                inc(V.tensor_tensor(esg[:, :], esg[:, :], bank[B_H + j % 2][:, UC:2 * UC], ALU.mult), "e_prod")

            def e_gl(x, t, j):
                dve.wait_ge(sem["e_gH"], x * NCH + t * 2 + j + 1)
                inc(V.tensor_tensor(egL[:, :], bank[B_T][:, 0:UC], egH[:, :].bitcast(F32), ALU.subtract), "e_gL")

            def y_low(x):
                for h in range(2):
                    dve.wait_ge(sem["y_hi"], x * 2 + h + 1)
                    inc(V.scalar_tensor_tensor(yL[:, h, :], bank[B_Y + h][:, :], cs[:, 0:1],
                                               yH[:, h, :].bitcast(F32), ALU.mult, ALU.subtract), "y_lo")

            g2 = [mt[1][:, 5 * KD + k, 0:1] for k in range(KD)]
            C_BANKS = (B_C, B_G, B_G + 1, B_C)

            def accumulate(x, f):
                dve.wait_ge(sem["comb_mm"], x * 4 + f + 1)
                b_ = bank[C_BANKS[f]]
                for kk in range(2):
                    k = 2 * f + kk
                    inc(V.scalar_tensor_tensor(xT[:, 1, k, :], b_[:, kk * S:(kk + 1) * S], g2[k], xT[:, 1, k, :],
                                               ALU.mult, ALU.add), "acc_done")

            def e_step(x, t, j):
                if j < NCH - 1:
                    e_lo(x, t, "w1", j + 1)
                if j == 0:
                    y_low(x)
                else:
                    e_gl(x, t, j - 1)
                if j < NCH - 1:
                    e_lo(x, t, "w3", j + 1)
                e_prod(x, t, j)
                e_lo(x, t, "w2", j)

            e_lo(0, 0, "w1", 0)
            gather_out(0)
            e_lo(0, 0, "w3", 0)
            dve.wait_ge(sem["items_done"], 2)
            n_items = dve.value_load(n_items_t[0:1, 0:1], min_val=NE, max_val=ITEMS)
            with dve.Fori(0, n_items) as x:
                e_step(x, 0, 0)
                e_step(x, 0, 1)
                accumulate(x, 0)
                accumulate(x, 1)
                e_step(x, 0, 2)
                accumulate(x, 2)
                accumulate(x, 3)
                dve.wait_ge(sem["pick_mm"], x * 2 + 2)
                inc(V.tensor_copy(cs[:, :], bank[B_G + 1][:, 0:1]), "cs_done")
                picks(x + 1)
                with dve.Fori(0, 3) as t:
                    e_step(x, t, 3)
                    e_step(x, t, 4)
                e_step(x, 0, NCH - 2)
                e_step(x, 0, NCH - 1)
                e_lo(x + 1, 0, "w1", 0)
                e_gl(x, 0, NCH - 1)
                gather_out(x + 1)
                e_lo(x + 1, 0, "w3", 0)
            y_low(n_items)
            for f in range(4):
                accumulate(n_items, f)
            dve.wait_ge(sem["root_done"], ROOT["final"])
            step(V.reciprocal(rstd[:, 0:S], rstd[:, 0:S]))
            for k in range(KD):
                inc(V.scalar_tensor_tensor(xT[:, 1, k, :], xT[:, 1, k, :], fg[:, k:k + 1], rstd[:, 0:S], ALU.mult, ALU.mult), "norm_step")

        @block.tensor
        def _(pe):
            mm = nc.tensor.matmul
            ident = K[:, K_ID:K_ID + P]
            ones = K[:, K_ONE:K_ONE + P]

            pe.wait_ge(sem["consts_in"], 16)
            pe.wait_ge(sem["misc_in"], 16 * 3)
            inc(nc.tensor.transpose(bank[B_MISC][:, 0:R_MEND], prow[0:R_MEND, 4, :], ident[0:R_MEND, 0:R_MEND]), "misc_t")

            def tokens(ks):
                pe.wait_ge(sem["x_in"], 16 * 4)
                for k in ks:
                    if k >= 4:
                        pe.wait_ge(sem["x_ready"], 2 * (k - 3))
                    for t in range(4):
                        last = nc.tensor.transpose(bank[k % 4][:, t * P:(t + 1) * P], xrow[:, t, k * P:(k + 1) * P], ident)
                    inc(last, "x_tr")

            def params():
                pe.wait_ge(sem["params_in"], 16 * len(PARAM_ROWS))
                pe.wait_ge(sem["x_ready"], 2 * KD)
                for n, (tile, rows_) in enumerate(ROW_PARTS):
                    inc(nc.tensor.transpose(bank[n][:, 0:rows_], prow[0:rows_, tile, :], ident[0:rows_, 0:rows_]), "params_t")

            pe.wait_ge(sem["cols_ready"], 4)
            pe.wait_ge(sem["memset_done"], 3)

            pending = []

            def transpose_rows():
                while pending:
                    l, q = pending.pop()
                    n = l * 24 + q
                    pe.wait_ge(sem["row_out"], n + 1)
                    for h in range(2):
                        o_ = (2 * q + h) * 2
                        last = mm(bank[B_MT][:, o_:o_ + 2], mrow[0:4, n % 2, h * P:(h + 1) * P], K[0:4, K_COMB:K_COMB + 2],
                                  start=True, stop=True)
                    inc(last, "mt_mm")

            st = dict(sq=0, hl=0, norms=0)

            def sums(n, count, w, a=0, b=None, b_=B_ST):
                for k in range(a, count if b is None else b):
                    pe.wait_ge(sem["sq_done"], st["sq"] + 1)
                    inc(mm(bank[b_][:, 0:n], w, sq[:, st["sq"] % 2, 0:n], start=(k == 0), stop=(k == count - 1)), "sum_mm")
                    st["sq"] += 1

            def chunk(dst, u, k_n, h, rH, rL, sel, a=0, b=None):
                s = u % RING
                n = 3 * a
                for k in range(a, k_n if b is None else b):
                    w_ = slice(k * UC + h * P, k * UC + (h + 1) * P)
                    for l_, r_ in split3(wh[s], wl[s], rH, rL):
                        last = mm(dst, l_[:, w_], r_[:, k, sel], start=(n == 0), stop=(n == 3 * k_n - 1))
                        n += 1
                return last

            def gate_map(l, c_, kd):
                g_ = l * KL + c_
                pe.wait_ge(sem["rconv_done"], RTAPS * (KL * l + c_ // 2 * 2 + 2))
                pe.wait_ge(sem["bd_in"], 16 * 8 * (l + 1))
                for d in range(2):
                    m_ = 4 * g_ + 2 * kd + d
                    if m_ >= 2:
                        pe.wait_ge(sem["sig_done"], m_ - 1)
                    inc(mm(bank[B_GATE[d]][:, :], bdw[:, c_, d, kd, :], rc[:, c_, :], start=True, stop=True), "bd_mm")

            def conv(l, a, b):
                full = side(l, "x")
                for m_ in range(a, b):
                    t, c_ = PE_CONV[l][m_]
                    if t == 0:
                        pe.wait_ge(sem["glu_done"], KL * l + c_ + 1)
                    pe.wait_ge(sem["diag_done"], PE_BASE[l] + m_ + 1)
                    b_ = bank[pe_bank(c_)]
                    dst = b_[:, :].rearrange("p (s n) -> p s n", s=2) if full == 0 else b_[:, 0:C]
                    src = glu[:, c_, :, t:t + C] if full == 0 else glu[:, c_, 1, t:t + C]
                    inc(mm(dst, diag[:, m_ % DIAGS, :], src, start=(t == 0), stop=(t == TAPS - 1)), "pe_conv")

            def first_chunks(u, full, hl):
                w = T if full == 0 else C
                pe.wait_ge(sem["lo_done"], u + 1)
                for k in range(KD):
                    pe.wait_ge(sem["hL_done"], hl - KD + k + 1)
                    for h in range(2):
                        last = chunk(bank[h][:, 0:w], u, KD, h, hH, hL, cols(full), k, k + 1)
                        if k == KD - 1:
                            inc(last, "mm_done")

            def mix(l):
                full = side(l, "x")
                w = T if full == 0 else C
                conv(l, pe_taps(AT[("wout", l, 0)] - 1)[2], len(PE_CONV[l]))
                pe.wait_ge(sem["sig_done"], 4 * KL * (l + 1))
                for c_ in range(KL):
                    if c_ == POOL_CHUNK:
                        pe.wait_ge(sem["pool_conv"], (l + 1) * (2 * TAPS - 1))
                    if c_ in DVE_CHUNKS[l]:
                        pe.wait_ge(sem["conv_step"], DVE_BASE[l] + (c_ + 1) * TAPS)
                    else:
                        pe.wait_ge(sem["pe_conv_out"], sum(len(w) for w in PE_CHUNKS[:l + 1]))
                    last = mm(bank[B_ST][:, 0:w], ones, cv[:, c_, :, :] if full == 0 else cv[:, c_, 1, :],
                              start=(c_ == 0), stop=(c_ == KL - 1))
                inc(last, "ln_mm")
                u0 = AT[("wout", l, 0)]
                pe.wait_ge(sem["gelu_done"], KL * (l + 1))
                pe.wait_ge(sem["hL_done"], HL[("mix", l)] - KL)
                for i in range(2):
                    pe.wait_ge(sem["lo_done"], u0 + i + 1)
                    for h in range(2):
                        chunk(bank[2 * i + h][:, 0:w], u0 + i, KD, h, hH, hL, cols(full), 0, KL)
                    if i == 0:
                        pe.wait_ge(sem["ln_step"], LN_STEPS * l + KL)
                        sums(w, KL, ones)
                pe.wait_ge(sem["hL_done"], HL[("mix", l)])

            for u, (kind, a, i) in enumerate(UNITS):
                if kind == "win" and i == 0:
                    transpose_rows()
                    sums(T, KD, ones, SUMMED if a else KD)
                    first_chunks(u, side(a, "x"), HL[("norm", a, 1)])
                    continue
                if kind == "wout" and i == 0:
                    transpose_rows()
                    mix(a)
                if kind == "f1" and i == 0:
                    sums(T, KD, ones, SUMMED)
                    first_chunks(u, 0, HL[("norm", 0, 2)])
                    continue
                pe.wait_ge(sem["lo_done"], u + 1)
                s = u % RING
                if by_dve((kind, a, i)):
                    if i == 0:
                        pe.wait_ge(sem["mod_ready"], 4)
                    vectors = range(mod_vectors(a, i))
                    if len(vectors) > 1:
                        pe.wait_ge(sem["mod_sum0"], i + 1)
                    for v_ in vectors:
                        for h in range(2):
                            o_ = (2 * i + h) * 2 + v_
                            last = mm(bank[B_MT][:, o_:o_ + 1], macc[:, i % 2, v_, h * P:(h + 1) * P], ones[:, 0:1],
                                      start=True, stop=True)
                    inc(last, "mt_mm")
                elif kind == "ad":
                    n = i
                    if n >= 1:
                        pe.wait_ge(sem["row_out"], n)
                    b_ = bank[B_ROW][:, 0:UC]
                    for k in range(KD):
                        for w_ in (wh[s], wl[s]):
                            last = mm(b_, smat[:, k, :], w_[:, k * UC:(k + 1) * UC], start=(k == 0 and w_ is wh[s]),
                                      stop=(k == KD - 1 and w_ is wl[s]))
                    inc(last, "mm_done")
                elif kind == "win":
                    full = side(a, "rec" if win_kind(i) == "rec" else "x")
                    w = T if full == 0 else C
                    for h in range(2):
                        t = 2 * i + h
                        if t >= WIN_BANKS:
                            free = {"gates": "gates_done", "values": "glu_done", "rec": "rec_done", "gelu": "gelu_done"}
                            last_t = t - WIN_BANKS
                            pe.wait_ge(sem[free[win_kind(last_t // 2)]], KL * a + win_chunk(last_t) + 1)
                        last = chunk(bank[t % WIN_BANKS][:, 0:w], u, KD, h, hH, hL, cols(full))
                        inc(last, "mm_done")
                        if i in LRU_AT:
                            gate_map(a, LRU_AT[i], h)
                elif kind == "wout":
                    full = side(a, "x")
                    w = T if full == 0 else C
                    for h in range(2):
                        k_ = 2 * i + h
                        if k_ >= MM_BANKS:
                            pe.wait_ge(sem["res_done"], RES[("wout", a)] + k_ - MM_BANKS + 1)
                        last = chunk(bank[k_ % MM_BANKS][:, 0:w], u, KD, h, hH, hL, cols(full), 0 if k_ >= 4 else KL)
                        inc(last, "mm_done")
                elif kind in ("f1", "f3"):
                    for h in range(2):
                        j = 2 * i + h
                        if j >= 2:
                            pe.wait_ge(sem["silu_out" if kind == "f1" else "g_prod"], j - 1)
                        if kind == "f1" and j % KD < 2 and j >= KD:
                            pe.wait_ge(sem["res_done"], RES[("f2", j // KD - 1)] + 8)
                        last = chunk(bank[(0 if kind == "f1" else 2) + h][:, :], u, KD, h, hH, hL, slice(0, T))
                        inc(last, "mm_done")
                elif kind == "f2" and i == 0:
                    pe.wait_ge(sem["silu_out"], 2 * sum(FFN_GROUPS[:a + 1]))
                    for k in range(2 * FFN_GROUPS[a]):
                        pe.wait_ge(sem["gL_done"], 2 * sum(FFN_GROUPS[:a]) + k + 1)
                        for h in range(2):
                            last = chunk(bank[h][:, :], u, 2 * FFN_GROUPS[a], h, gH, gL, slice(0, T), k, k + 1)
                            if k == 2 * FFN_GROUPS[a] - 1:
                                inc(last, "mm_done")
                elif kind == "f2":
                    for h in range(2):
                        k_ = 2 * i + h
                        if k_ >= MM_BANKS:
                            pe.wait_ge(sem["res_done"], RES[("f2", a)] + k_ - MM_BANKS + 1)
                        last = chunk(bank[k_ % MM_BANKS][:, :], u, 2 * FFN_GROUPS[a], h, gH, gL, slice(0, T))
                        inc(last, "mm_done")
                transpose_rows()
                if kind == "ad" and a == 0:
                    pending.append((a, i))
                if kind == "ad" and a == 0 and i < KD // 2:
                    tokens((2 * i, 2 * i + 1))
                if kind == "ad" and a == 0 and i == KD - 1:
                    params()
                if kind == "ad" and a == 0 and KD // 2 <= i < KD:
                    sums(T, KD, ones, 2 * i - KD, 2 * i - KD + 2)
                if pe_taps(u):
                    conv(*pe_taps(u))
                if i and (kind == "wout" or (kind == "f2" and a == 2)):
                    sums(S if (kind, a) == ("wout", 1) else T, KD, ones, 2 * i - 2, 2 * i)

            sums(S, KD, ones, SUMMED)
            pe.wait_ge(sem["router_in"], 16)
            for k in range(KD):
                pe.wait_ge(sem["fT_done"], k + 1)
                for t in range(2):
                    last = mm(bank[t][:, 0:NE], fT[:, k, t * P:(t + 1) * P], rt[:, k, :], start=(k == 0), stop=(k == KD - 1))
            inc(last, "logits_mm")
            for h in range(2):
                for z in range(2):
                    last = mm(bank[B_Y + h][:, z * UC:(z + 1) * UC], zeros[:, 0:P], zeros[:, :], start=(z == 0), stop=(z == 1))
            inc(last, "e_used", CREDIT)
            for f in range(4):
                t = f // 2
                for k in range(4):
                    last = nc.tensor.transpose(bank[B_TOK[f]][:, k * P:(k + 1) * P],
                                               fT[:, (f % 2) * 4 + k, t * P:(t + 1) * P], ident)
                inc(last, "tok_tr")
            pe.wait_ge(sem["route_step"], ROUTE_MASKS)
            up = K[:, K_UP:K_UP + P]
            for o_, parts in ((0, ((up, 0),)), (NE, ((ones, 0), (up, 1))), (2 * NE, ((ones, 0), (ones, 1)))):
                for n, (w_, t) in enumerate(parts):
                    last = mm(bank[0][:, o_:o_ + NE], w_, mask[:, t, :], start=(n == 0), stop=(n == len(parts) - 1))
            inc(last, "pos_mm")


            def gather(g):
                pe.wait_ge(sem["pick_done"], g * 3 + 3)
                for q in range(2):
                    for kk in range(4):
                        k = 4 * q + kk
                        n = 0
                        for t in range(2):
                            for ft in (ftH, ftL):
                                last = mm(bank[B_G + q][:, kk * CAP:(kk + 1) * CAP], ft[:, t, k * P:(k + 1) * P],
                                          pick[:, t, :], start=(n == 0), stop=(n == 3))
                                n += 1
                    inc(last, "gather_mm")

            def slots(x):
                pe.wait_ge(sem["acc_done"], x * 8 + 4 + 4)
                for t in range(2):
                    last = nc.tensor.transpose(bank[B_G][:, t * P:(t + 1) * P], pick[:, t, :].bitcast(F32), ident)
                inc(last, "pick_mm")
                pe.wait_ge(sem["acc_done"], x * 8 + 6 + 4)
                for t in range(2):
                    last = mm(bank[B_G + 1][:, 0:1], pick[:, t, :].bitcast(F32), cur[:, t, 1, :], start=(t == 0), stop=(t == 1))
                inc(last, "pick_mm")

            def e_up(x, t, kind, j):
                s = slot(kind, j)
                pe.wait_ge(sem["e_lo"], x * EUNITS + t * 6 + order(kind, j) + 1 + CREDIT)
                m_ = 0
                h = ("w1", "w3").index(kind)
                dst = bank[B_H + j % 2][:, h * UC:(h + 1) * UC]
                for k in range(KD):
                    for l_, r_ in split3(xeH, xeL, wh[s], wl[s]):
                        last = mm(dst, l_[:, k, :], r_[:, k * UC:(k + 1) * UC], start=(m_ == 0), stop=(m_ == 3 * KD - 1))
                        m_ += 1
                inc(last, "e_used")

            def e_tr(x, t, j):
                pe.wait_ge(sem["e_prod"], x * NCH + t * 2 + j + 1)
                for f in range(2):
                    last = nc.tensor.transpose(bank[B_T][:, f * P:(f + 1) * P], esg[:, f * P:(f + 1) * P], ident)
                inc(last, "g_tr")

            def e_down(x, t, j):
                s = slot("w2", j)
                pe.wait_ge(sem["e_gL"], x * NCH + t * 2 + j + 1)
                pe.wait_ge(sem["e_lo"], x * EUNITS + t * 6 + order("w2", j) + 1 + CREDIT)
                for f in range(2):
                    for h in range(2):
                        for n, (l_, r_) in enumerate(split3(egH, egL, wh[s], wl[s])):
                            last = mm(bank[B_Y + h][:, :], l_[:, f * P:(f + 1) * P],
                                      r_[:, f * D + h * 512:f * D + (h + 1) * 512],
                                      start=(j == 0 and f == 0 and n == 0), stop=(j == NCH - 1 and f == 1 and n == 2))
                inc(last, "e_used")

            def e_step(x, t, j):
                e_up(x, t, "w1", j)
                if j:
                    e_tr(x, t, j - 1)
                e_up(x, t, "w3", j)
                if j == 1:
                    pe.wait_ge(sem["y_lo"], x * 2 + 2)
                if j:
                    e_down(x, t, j - 1)

            def combine(x, h):
                pe.wait_ge(sem["y_lo"], x * 2 + h + 1)
                for q in range(2):
                    f = 2 * h + q
                    if f == 3:
                        pe.wait_ge(sem["acc_done"], x * 8 + 2 + 4)
                    for kk in range(2):
                        k = 2 * q + kk
                        for n, y_ in enumerate((yH, yL)):
                            last = mm(bank[C_BANKS[f]][:, kk * S:(kk + 1) * S], y_[:, h, k * P:(k + 1) * P], pickT[:, :],
                                      start=(n == 0), stop=(n == 1))
                    inc(last, "comb_mm")

            C_BANKS = (B_C, B_G, B_G + 1, B_C)
            pe.wait_ge(sem["tokL"], 4)
            gather(0)
            pe.wait_ge(sem["items_done"], 2)
            n_items = pe.value_load(n_items_t[0:1, 0:1], min_val=NE, max_val=ITEMS)
            with pe.Fori(0, n_items) as x:
                pe.wait_ge(sem["xe_lo"], x * 2 + 2)
                e_step(x, 0, 0)
                e_step(x, 0, 1)
                pe.wait_ge(sem["acc_done"], x * 8 + 4)
                combine(x, 0)
                e_step(x, 0, 2)
                combine(x, 1)
                slots(x)
                with pe.Fori(0, 4) as t:
                    e_step(x, t, 3)
                    e_step(x, t, 4)
                e_tr(x, 0, NCH - 1)
                pe.wait_ge(sem["pickT_done"], x + 1)
                pe.wait_ge(sem["cs_done"], x + 1)
                gather(x + 1)
                e_down(x, 0, NCH - 1)
            pe.wait_ge(sem["xe_lo"], n_items * 2 + 2)
            pe.wait_ge(sem["acc_done"], n_items * 8 + 4)
            combine(n_items, 0)
            combine(n_items, 1)
            sums(S, KD, ones, b_=B_H)
            for f in (0, 2, 1, 3):
                pe.wait_ge(sem["norm_step"], KD // 2 * (f % 2 + 1))
                for k in range(4):
                    last = nc.tensor.transpose(bank[f][:, k * P:(k + 1) * P],
                                               xT[:, 1, (f % 2) * 4 + k, (f // 2) * P:(f // 2 + 1) * P], ident)
                inc(last, "fin_tr")


_INS = ["x", "c", "ctx", "c_ctx", "w_mod", "b_mod", "norm1_g", "norm2_g", "w_in", "w_out",
        "lru_conv_w", "lru_conv_b", "lru_wa", "lru_ba", "lru_wx", "lru_bx", "lru_lambda",
        "conf_dw_w", "conf_dw_b", "conf_ln_g", "conf_ln_b",
        "ffn_w1", "ffn_w3", "ffn_w2", "moe_router", "moe_w1", "moe_w3", "moe_w2", "final_g"]
GRID_W = 64


def position_table():
    quarter = D // 4
    omega = (1.0 / (10000.0 ** (np.arange(quarter, dtype=np.float32) / np.float32(quarter)))).astype(np.float32)

    def emb1d(n):
        ang = np.arange(n, dtype=np.float32)[:, None] * omega[None, :]
        return np.concatenate([np.sin(ang), np.cos(ang)], axis=-1)

    n_rows = S // GRID_W
    er = np.broadcast_to(emb1d(n_rows)[:, None, :], (n_rows, GRID_W, D // 2))
    ec = np.broadcast_to(emb1d(GRID_W)[None, :, :], (n_rows, GRID_W, D // 2))
    return np.ascontiguousarray(np.concatenate([er, ec], axis=-1).reshape(S, D).T.astype(np.float32))


def shape_constants():
    k = np.zeros((P, K_W), np.float32)
    k[:, K_ID:K_ID + P] = np.eye(P)
    k[:, K_UP:K_UP + P] = np.triu(np.ones((P, P)), 1)
    k[:, K_ONE:K_ONE + P] = 1.0
    k[:, K_IOTA:K_IOTA + CAP] = np.arange(CAP)
    k[:, K_IOTA8:K_IOTA8 + NE] = np.arange(NE)
    for r in range(4):
        k[r, K_COMB + r % 2] = 1.0
    return k


def kernel(**inputs):
    import concourse.bacc as _bacc
    from concourse.bass_utils import run_bass_kernel_spmd as _run

    nc = _bacc.Bacc("TRN2", target_bir_lowering=False, num_devices=1)
    host = {name: np.ascontiguousarray(inputs[name]) for name in _INS}
    host["pos_t"] = position_table()
    host["consts"] = shape_constants()
    arrays, args = {}, []
    for name, a in host.items():
        arrays[f"in_{name}"] = a
        args.append(nc.dram_tensor(f"in_{name}", a.shape, mybir.dt.from_np(a.dtype), kind="ExternalInput").ap())
    args.append(nc.dram_tensor("out_0", (1, S, D), F32, kind="ExternalOutput").ap())
    dit_kernel(nc, *args)
    r = _run(nc, [arrays], core_ids=[0])
    return r.results[0]["out_0"]
```
